# Optimizing a Trainium2 kernel written in Bass

```python
import jax, jax.numpy as jnp
from jax import lax
import numpy as np

D_MODEL = 1024
BATCH = 1
SEQ = 256
DEPTH = 2

N_DENSE = (DEPTH + 1) // 2
N_MOE = DEPTH // 2

MLA_HEADS = 8
MLA_NOPE = 64
MLA_ROPE = 32
MLA_QK = MLA_NOPE + MLA_ROPE
MLA_V = 64
MLA_Q_RANK = D_MODEL // 4
MLA_KV_RANK = D_MODEL // 4
ROPE_BASE = 10000.0
Q_BLOCK = 128
GLA_HEADS = 4
GLA_DK = 64
GLA_DV = 128
GLA_GATE_RANK = 16
GLA_TAU = 16.0
GLA_CHUNK = 16
POOL_WINDOWS = (2, 4, 8, 16)
POOL_GROUP = 128
POOL_WIDTH = 4 * POOL_GROUP
N_BRANCH = 3
BRANCH_WIDTH = 512
D_FF = 2816
N_EXPERTS = 8
TOP_K = 2
D_EXPERT = 1408
EPS = 1e-6

IN_SPLITS = (MLA_Q_RANK, MLA_KV_RANK, MLA_ROPE,
             GLA_HEADS * GLA_DK, GLA_HEADS * GLA_DK, GLA_HEADS * GLA_DV, GLA_GATE_RANK, GLA_HEADS * GLA_DV,
             POOL_WIDTH, N_BRANCH * D_MODEL)
D_IN = sum(IN_SPLITS)

kernel_name = 'hybrid_mla_gla_pool_gated_moe'

def rms_norm(x, g):
    xf = x.astype(jnp.float32)
    y = xf * lax.rsqrt(jnp.mean(xf * xf, axis=-1, keepdims=True) + EPS)
    return (y * g.astype(jnp.float32)).astype(x.dtype)

def rope(x, positions):
    half = x.shape[-1] // 2
    inv_freq = ROPE_BASE ** (-jnp.arange(half, dtype=jnp.float32) / half)
    ang = positions.astype(jnp.float32)[..., None] * inv_freq
    cos = jnp.cos(ang)[:, :, None, :]
    sin = jnp.sin(ang)[:, :, None, :]
    xf = x.astype(jnp.float32)
    x1, x2 = xf[..., :half], xf[..., half:]
    return jnp.concatenate([x1 * cos - x2 * sin, x2 * cos + x1 * sin], axis=-1).astype(x.dtype)

def causal_block_attention(q, k, v):
    B, S, H, Dq = q.shape
    nb = S // Q_BLOCK
    scale = Dq ** -0.5
    key_pos = jnp.arange(S)
    q_blocks = q.reshape(B, nb, Q_BLOCK, H, Dq).transpose(1, 0, 2, 3, 4)

    def one_block(args):
        i, qb = args
        s = jnp.einsum('bqhd,bkhd->bhqk', qb, k, preferred_element_type=jnp.float32) * scale
        q_pos = i * Q_BLOCK + jnp.arange(Q_BLOCK)
        s = jnp.where(key_pos[None, :] <= q_pos[:, None], s, -jnp.inf)
        p = jax.nn.softmax(s, axis=-1).astype(v.dtype)
        return jnp.einsum('bhqk,bkhv->bqhv', p, v)

    o = lax.map(one_block, (jnp.arange(nb), q_blocks))
    return o.transpose(1, 0, 2, 3, 4).reshape(B, S, H, v.shape[-1])

def mla_branch(c_q, c_kv, k_rope, positions, g_cq, w_uq, g_ckv, w_ukv, g_qk_q, g_qk_k):
    B, S, _ = c_q.shape
    q = (rms_norm(c_q, g_cq) @ w_uq).reshape(B, S, MLA_HEADS, MLA_QK)
    kv = (rms_norm(c_kv, g_ckv) @ w_ukv).reshape(B, S, MLA_HEADS, MLA_NOPE + MLA_V)
    k_nope, v = kv[..., :MLA_NOPE], kv[..., MLA_NOPE:]
    k_r = jnp.broadcast_to(k_rope[:, :, None, :], (B, S, MLA_HEADS, MLA_ROPE))
    k = jnp.concatenate([k_nope, k_r], axis=-1)
    q = rms_norm(q, g_qk_q)
    k = rms_norm(k, g_qk_k)
    q = jnp.concatenate([q[..., :MLA_NOPE], rope(q[..., MLA_NOPE:], positions)], axis=-1)
    k = jnp.concatenate([k[..., :MLA_NOPE], rope(k[..., MLA_NOPE:], positions)], axis=-1)
    o = causal_block_attention(q, k, v)
    return o.reshape(B, S, MLA_HEADS * MLA_V)

def gla_branch(q, k, v, gate_lr, out_gate, w_gate_up, b_gate, g_out):
    B, S, _ = q.shape
    N, C, H = S // GLA_CHUNK, GLA_CHUNK, GLA_HEADS
    f32 = jnp.float32
    log_a = jax.nn.log_sigmoid((gate_lr @ w_gate_up + b_gate).astype(f32)) / GLA_TAU
    qc = q.astype(f32).reshape(B, N, C, H, GLA_DK) * (GLA_DK ** -0.5)
    kc = k.astype(f32).reshape(B, N, C, H, GLA_DK)
    vc = v.astype(f32).reshape(B, N, C, H, GLA_DV)
    bc = jnp.cumsum(log_a.reshape(B, N, C, H, GLA_DK), axis=2)
    causal = jnp.tril(jnp.ones((C, C), dtype=bool))[None, None, :, :, None, None]
    diff = bc[:, :, :, None] - bc[:, :, None, :]
    decay = jnp.exp(jnp.where(causal, diff, -jnp.inf))
    attn = jnp.einsum('bnijhd,bnjhd->bnhij', qc[:, :, :, None] * decay, kc)
    o_intra = jnp.einsum('bnhij,bnjhv->bnihv', attn, vc)
    b_last = bc[:, :, -1]
    q_dec = qc * jnp.exp(bc)
    k_dec = kc * jnp.exp(b_last[:, :, None] - bc)
    a_last = jnp.exp(b_last)

    def step(state, xs):
        qd, kd, vv, al = xs
        o = jnp.einsum('bihd,bhdv->bihv', qd, state)
        state = al[..., None] * state + jnp.einsum('bjhd,bjhv->bhdv', kd, vv)
        return state, o

    xs = (jnp.moveaxis(q_dec, 1, 0), jnp.moveaxis(k_dec, 1, 0), jnp.moveaxis(vc, 1, 0), jnp.moveaxis(a_last, 1, 0))
    state0 = jnp.zeros((B, H, GLA_DK, GLA_DV), f32)
    _, o_inter = lax.scan(step, state0, xs)
    o = o_intra + jnp.moveaxis(o_inter, 0, 1)
    o = rms_norm(o.reshape(B, S, H, GLA_DV), g_out).astype(q.dtype)
    o = o * jax.nn.silu(out_gate.reshape(B, S, H, GLA_DV))
    return o.reshape(B, S, H * GLA_DV)

def pool_branch(u, w_pool, pool_scale):
    B, S, _ = u.shape
    uf = u.astype(jnp.float32).reshape(B, S, len(POOL_WINDOWS), POOL_GROUP)
    cs = jnp.cumsum(uf, axis=1)
    t1 = jnp.arange(1, S + 1, dtype=jnp.float32)
    outs = []
    for gi, w in enumerate(POOL_WINDOWS):
        c = cs[:, :, gi]
        c_shift = jnp.pad(c, ((0, 0), (w, 0), (0, 0)))[:, :S]
        mean = (c - c_shift) / jnp.minimum(t1, w)[None, :, None]
        outs.append(mean - uf[:, :, gi])
    pooled = jnp.stack(outs, axis=2).astype(u.dtype)
    y = jnp.einsum('bsgc,gcd->bsgd', pooled, w_pool).reshape(B, S, POOL_WIDTH)
    return y * pool_scale

def swiglu(h, w_gate, w_up, w_down):
    return (jax.nn.silu(h @ w_gate) * (h @ w_up)) @ w_down

def moe_ffn(h, w_router, w_e_gate, w_e_up, w_e_down):
    logits = jnp.einsum('bsd,de->bse', h, w_router, preferred_element_type=jnp.float32)
    top_vals, top_idx = lax.top_k(logits, TOP_K)
    top_w = jax.nn.softmax(top_vals, axis=-1)
    combine = jnp.sum(jax.nn.one_hot(top_idx, N_EXPERTS, dtype=jnp.float32) * top_w[..., None], axis=-2)
    combine = combine.astype(h.dtype)
    y = jnp.zeros_like(h)
    for e in range(N_EXPERTS):
        y = y + combine[..., e:e + 1] * swiglu(h, w_e_gate[e], w_e_up[e], w_e_down[e])
    return y

def setup_inputs(seed: int = 0) -> dict:
    key = jax.random.key(seed)
    ks = jax.random.split(key, 32)
    f32 = jnp.float32

    def w(k, shape, fan_in):
        return jax.random.normal(k, shape, f32) * fan_in ** -0.5

    def gain(k, shape):
        return 1.0 + 0.05 * jax.random.normal(k, shape, f32)

    x = jax.random.normal(ks[0], (BATCH, SEQ, D_MODEL), f32)
    offset = jax.random.randint(ks[1], (BATCH, 1), 0, 1024, dtype=jnp.int32)
    positions = jnp.arange(SEQ, dtype=jnp.int32)[None, :] + offset
    return {
        'x': x,
        'positions': positions,
        'g_mix': gain(ks[2], (DEPTH, D_MODEL)),
        'w_in': w(ks[3], (DEPTH, D_MODEL, D_IN), D_MODEL),
        'g_cq': gain(ks[4], (DEPTH, MLA_Q_RANK)),
        'w_uq': w(ks[5], (DEPTH, MLA_Q_RANK, MLA_HEADS * MLA_QK), MLA_Q_RANK),
        'g_ckv': gain(ks[6], (DEPTH, MLA_KV_RANK)),
        'w_ukv': w(ks[7], (DEPTH, MLA_KV_RANK, MLA_HEADS * (MLA_NOPE + MLA_V)), MLA_KV_RANK),
        'g_qk_q': gain(ks[8], (DEPTH, MLA_QK)),
        'g_qk_k': gain(ks[9], (DEPTH, MLA_QK)),
        'w_gla_gate_up': w(ks[10], (DEPTH, GLA_GATE_RANK, GLA_HEADS * GLA_DK), GLA_GATE_RANK),
        'b_gla_gate': 0.1 * jax.random.normal(ks[11], (DEPTH, GLA_HEADS * GLA_DK), f32),
        'g_gla_out': gain(ks[12], (DEPTH, GLA_DV)),
        'w_pool': w(ks[13], (DEPTH, len(POOL_WINDOWS), POOL_GROUP, POOL_GROUP), POOL_GROUP),
        'pool_scale': gain(ks[14], (DEPTH, POOL_WIDTH)),
        'w_branch': w(ks[15], (DEPTH, N_BRANCH, BRANCH_WIDTH, D_MODEL), BRANCH_WIDTH),
        'w_out': w(ks[16], (DEPTH, D_MODEL, D_MODEL), D_MODEL),
        'g_ffn': gain(ks[17], (DEPTH, D_MODEL)),
        'w_ffn_gate': w(ks[18], (N_DENSE, D_MODEL, D_FF), D_MODEL),
        'w_ffn_up': w(ks[19], (N_DENSE, D_MODEL, D_FF), D_MODEL),
        'w_ffn_down': w(ks[20], (N_DENSE, D_FF, D_MODEL), D_FF),
        'w_router': w(ks[21], (N_MOE, D_MODEL, N_EXPERTS), D_MODEL),
        'w_exp_gate': w(ks[22], (N_MOE, N_EXPERTS, D_MODEL, D_EXPERT), D_MODEL),
        'w_exp_up': w(ks[23], (N_MOE, N_EXPERTS, D_MODEL, D_EXPERT), D_MODEL),
        'w_exp_down': w(ks[24], (N_MOE, N_EXPERTS, D_EXPERT, D_MODEL), D_EXPERT),
    }

def reference(x, positions, g_mix, w_in, g_cq, w_uq, g_ckv, w_ukv, g_qk_q, g_qk_k, w_gla_gate_up, b_gla_gate,
              g_gla_out, w_pool, pool_scale, w_branch, w_out, g_ffn, w_ffn_gate, w_ffn_up, w_ffn_down,
              w_router, w_exp_gate, w_exp_up, w_exp_down):
    B, S, _ = x.shape
    split_points = np.cumsum(IN_SPLITS)[:-1].tolist()
    for layer in range(DEPTH):
        h = rms_norm(x, g_mix[layer])
        proj = h @ w_in[layer]
        (c_q, c_kv, k_rope, gla_q, gla_k, gla_v, gla_lr, gla_og, u_pool, gate_logits) = jnp.split(proj, split_points, axis=-1)
        y_a = mla_branch(c_q, c_kv, k_rope, positions, g_cq[layer], w_uq[layer], g_ckv[layer], w_ukv[layer],
                         g_qk_q[layer], g_qk_k[layer])
        y_b = gla_branch(gla_q, gla_k, gla_v, gla_lr, gla_og, w_gla_gate_up[layer], b_gla_gate[layer], g_gla_out[layer])
        y_c = pool_branch(u_pool, w_pool[layer], pool_scale[layer])
        ys = jnp.stack([y_a, y_b, y_c], axis=2)
        y_d = jnp.einsum('bsnc,ncd->bsnd', ys, w_branch[layer])
        gates = jax.nn.sigmoid(gate_logits.astype(jnp.float32).reshape(B, S, N_BRANCH, D_MODEL)).astype(x.dtype)
        merged = jnp.sum(gates * y_d, axis=2)
        x = x + merged @ w_out[layer]
        h = rms_norm(x, g_ffn[layer])
        i = layer // 2
        if layer % 2 == 0:
            x = x + swiglu(h, w_ffn_gate[i], w_ffn_up[i], w_ffn_down[i])
        else:
            x = x + moe_ffn(h, w_router[i], w_exp_gate[i], w_exp_up[i], w_exp_down[i])
    return x


_drawn_inputs = setup_inputs


def setup_inputs(seed=0):
    import zlib

    import numpy as np

    out = dict(_drawn_inputs(seed))
    spreads = {}
    factors = {'g_cq': 3.548, 'g_ckv': 2.795, 'g_qk_q': 4.46, 'g_qk_k': 4.525}
    for name, (base, spread) in spreads.items():
        noise = np.random.default_rng([zlib.crc32(name.encode()), seed]).standard_normal(out[name].shape)
        drawn = base * np.exp(spread * noise) if base else spread * noise
        out[name] = __import__('jax').numpy.asarray(drawn.astype(out[name].dtype))
    for name, factor in factors.items():
        out[name] = (out[name] * factor).astype(out[name].dtype)
    return out
```

```python
import concourse.bass as bass
from concourse import mybir
from contextlib import ExitStack
import numpy as np

D, T, DEPTH, P = 1024, 256, 2, 128
KD = D // P
TT = T // P
H, NOPE, ROPE, DV = 8, 64, 32, 64
QK = NOPE + ROPE
HALF = ROPE // 2
RANK = D // 4
KR = RANK // P
GH, GDK, GDV, GRANK, GC = 4, 64, 128, 16, 16
TAU = 16.0
NCH = T // GC
NCT = P // GC
WINDOWS = (2, 4, 8, 16)
NG = len(WINDOWS)
NBR, BW = 3, 512
KB = BW // P
DFF, NE, DE = 2816, 8, 1408
EPS = 1e-6
ROPE_BASE = 10000.0
BIG = 1024.0
NEG = -1e30

C_Q, C_KV, C_KR = 0, RANK, 2 * RANK
C_GQ = C_KR + ROPE
C_GK = C_GQ + GH * GDK
C_GV = C_GK + GH * GDK
C_LR = C_GV + GH * GDV
C_OG = C_LR + GRANK
C_U = C_OG + GH * GDV
C_G = C_U + NG * P
D_IN = C_G + NBR * D

UF = DE
FT = UF // P
GROUPS = [(0, 3), (3, 3), (6, 3), (9, 2)]
UNIT_LOADS = ["G0", "U0", "G1", "U1", "D0", "G2", "U2", "D1", "G3", "U3", "D2", "D3"]
NDENSE = DFF // UF
CAP = 96
PASSES = -(-T // CAP)

GU = {"d": 4, "e": 2}


def tiles_in_bank(n):
    return [len(range(b, FT, n)) for b in range(n)]


def tile_before(t, n):
    return t - n if t >= n else max(x for x in range(FT) if x % n == t % n) - FT


SLOT, NSLOT = 3072, 6
GB = 384

PARAMS = [("g_mix", DEPTH * KD), ("g_ffn", DEPTH * KD), ("g_cq", DEPTH * KR), ("g_ckv", DEPTH * KR),
          ("b_gla_gate", DEPTH * 2), ("g_gla_out", DEPTH), ("pool_scale", DEPTH * NG),
          ("g_qk_q", DEPTH), ("g_qk_k", DEPTH)]
PCOL, NPAR = {}, 0
for _n, _k in PARAMS:
    PCOL[_n] = NPAR
    NPAR += _k

LOADS = (["cq", "ckv", "gq", "gk", "uq", "va", "ukv", "vb", "oga", "ogb", "ua", "ub"]
         + [f"g{i}" for i in range(4)] + ["pool"] + [f"g{i}" for i in range(4, 8)]
         + ["br00", "br01", "br20", "br21", "br10", "br11"] + ["out0", "out1", "out2"])
NL = len(LOADS)
LAST_USE = {"cq": "cq", "ckv": "kr", "gq": "gq", "gk": "gk", "uq": "q3", "va": "va", "ukv": "vm1", "vb": "lr",
            "oga": "oga", "ogb": "ogb", "ua": "ua", "ub": "ub", "pool": "pl1",
            **{f"g{b}": f"g{(3 * b + 2) // 2}" for b in range(8)},
            **{f"br{n}{hf}": f"b{n}{2 * hf + 1}" for n in range(3) for hf in range(2)},
            "out0": "w1", "out1": "w2", "out2": "w3"}
assert NL % NSLOT == 0 and len(UNIT_LOADS) % NSLOT == 0

NB = 6
PRE_USES = ["par", "inv", "x0", "x1", "x2", "x3"]
MIX_USES = (["ssm", "cq", "ckv", "kr", "gq", "sslat", "gk"] + [f"q{i}" for i in range(4)] + ["va"]
            + [f"k{i}" for i in range(4)] + ["vm0", "vm1", "vb", "lr", "oga", "ssq"]
            + [f"ssk{i}" for i in range(4)] + ["z", "ogb"]
            + [f"rq{i}" for i in range(4)] + [f"rk{i}" for i in range(4)] + ["ua", "ub"]
            + ["g0", "s0", "s1", "g1", "pt0", "pt1", "s2", "s3", "g2", "o0", "pt2", "pt3", "s4", "s5",
               "g3", "o1", "pt4", "pt5", "s6", "s7", "g4", "o2", "pt6", "pt7", "pl0", "pl1", "g5", "o3",
               "A0", "g6", "A1", "kd0", "g7", "kd1"]
            + [f"U{i}" for i in range(4)] + ["g8"] + [f"U{i}" for i in range(4, 8)] + ["g9", "g10", "ssg0", "ssg1", "g11"]
            + [f"b{n}{m}" for n in (0, 2, 1) for m in range(4)] + [f"w{m}" for m in range(4)] + ["ssf"])
USES = [(-1, u) for u in PRE_USES]
USES += [(0, u) for u in MIX_USES] + [(1, u) for u in MIX_USES]
USE = {u: i for i, u in enumerate(USES)}
MIX_END = [len(PRE_USES) + len(MIX_USES), len(PRE_USES) + 2 * len(MIX_USES)]


def hybrid_trunk(nc, A, out):
    F32, I32, U32, BF16 = mybir.dt.float32, mybir.dt.int32, mybir.dt.uint32, mybir.dt.bfloat16
    ALU, ACT, AX = mybir.AluOpType, mybir.ActivationFunctionType, mybir.AxisListType
    ADD, SUB, MUL, MAX, MIN = ALU.add, ALU.subtract, ALU.mult, ALU.max, ALU.min

    ctx = ExitStack()
    with ctx:
        def sb(name, shape, dt=F32):
            return ctx.enter_context(nc.sbuf_tensor(name, shape, dt))

        sems = {}

        def sem(name):
            if name not in sems:
                sems[name] = ctx.enter_context(nc.semaphore(name))
            return sems[name]

        ring = sb("ring", [P, NSLOT, SLOT])
        xT = sb("xT", [P, KD, T])
        hT = sb("hT", [P, KD, T])
        rt = sb("rt", [P, 2, T])
        rr = sb("rr", [P, 2, T])
        big = sb("big", [P, 24 * T])
        gates = big[:, :].rearrange("p (n t) -> p n t", t=T)
        lat, latn, sq, sk = gates[:, 0:4], gates[:, 4:8], gates[:, 8:16], gates[:, 16:24]
        xin = big[:, 0:TT * D].rearrange("p (a d) -> p a d", a=TT)
        rows3 = sb("rows3", [P, 3, T])
        krope = rows3[:, 2, :]
        gq = sb("gq", [P, 2, T])
        gk = sb("gk", [P, 2, T])
        gvt = sb("gvt", [P, TT, GH * GDV])
        glr = rows3[0:GRANK, 2, :]
        th = sb("th", [P, 2, T])
        PADW = max(WINDOWS)
        u = sb("u", [P, NG, PADW + T])
        scr = sb("scr", [P, 4096])
        E = scr[:, :].rearrange("p (d c n j) -> p d c n j", d=2, n=NCT, c=GC)
        pwa = scr[:, 0:NG * (PADW + T)].rearrange("p (g t) -> p g t", g=NG)
        pwb = scr[:, 2048:2048 + NG * (PADW + T)].rearrange("p (g t) -> p g t", g=NG)
        merged = scr[:, 0:KD * T].rearrange("p (k t) -> p k t", k=KD)
        ztmp = scr[:, 2048:4096].rearrange("p (k t) -> p k t", k=8)
        qk = sb("qk", [P, 4096])
        q = qk[0:QK, 0:2048].rearrange("p (h t) -> p h t", h=H)
        k = qk[0:QK, 2048:4096].rearrange("p (h t) -> p h t", h=H)
        gsq = qk[:, 0:4 * T].rearrange("p (a b t) -> p a b t", a=2, b=2)
        kdm = qk[:, 0:2048].rearrange("p (n f) -> p n f", n=NCT)
        S = qk[:, 2048:4096].rearrange("p (n d v) -> p n d v", n=NCT, d=2)
        vt = sb("vt", [P, TT, H * DV])
        ys = sb("ys", [P, NBR * KB, T])
        Pr = sb("Pr", [P, 3, 3 * P])
        PT = sb("PT", [P, 2, 3 * P])
        rqs = sb("rqs", [P, TT * H])
        small = sb("small", [P, 64])
        kdec = sb("kdec", [P, 2, T])
        bc = sb("bc", [P, 2, T])
        qdm = sb("qdm", [P, 2, 2, T])
        al = sb("al", [P, 2, NCH])
        attn = sb("attn", [P, GH, P])
        ident = sb("ident", [P, P])
        ones = sb("ones", [P, P])
        zb = sb("zb", [P, 512], BF16)
        maskc = sb("maskc", [P, 3 * P])
        maskg = sb("maskg", [P, P])
        chm = sb("chm", [P, NCT])
        keep = sb("keep", [P, T])
        winf = sb("winf", [P, NG, PADW])
        selh = sb("selh", [P, 2])
        R = sb("R", [QK, QK])
        cs = rows3[:, 0:2, :]
        par = sb("par", [P, NPAR])
        eps = sb("eps", [P, 1])
        one1 = sb("one1", [1, 1])
        invr = sb("invr", [1, QK])
        invc = sb("invc", [QK, 1])
        ang = qk[0:QK, 0:4 * T].rearrange("p (a t) -> p a t", a=4)
        cnt = sb("cnt", [P, PADW], I32)
        sloti = sb("sloti", [P, CAP], I32)
        eb = attn[:, :, :].rearrange("p h i -> p (h i)").rearrange("p (d t) -> p d t", d=2)
        ek = PT[:, :, :].rearrange("p a j -> p (a j)")[:, 0:2 * T].rearrange("p (d t) -> p d t", d=2)
        rq16 = small[:, 0:16]
        mx = small[:, 16:20].rearrange("p (a b) -> p a b", a=2)
        nbs = small[:, 20:24].rearrange("p (a b) -> p a b", a=2)
        sums = small[:, 24:28].rearrange("p (a b) -> p a b", a=2)
        angk = ang[:, 3, :]
        rtmp = th[0:QK, :, :]
        gtmp = th
        lg = sb("lg", [P, TT, NE])
        hid = scr[:, 0:FT * T].rearrange("p (f t) -> p f t", f=FT)
        sil = scr[:, FT * T:FT * T + 4 * T].rearrange("p (f t) -> p f t", f=4)
        htok = qk[:, 0:TT * D].rearrange("p (a d) -> p a d", a=TT)
        selT = qk[0:CAP, 2048:2048 + NE * T].rearrange("p (e t) -> p e t", e=NE)
        o0 = 0
        hTe = big[:, 0:KD * CAP].rearrange("p (k c) -> p k c", k=KD)
        yT = big[:, 768:768 + KD * CAP].rearrange("p (k c) -> p k c", k=KD)
        ye = big[0:CAP, 1536:1536 + D]
        psel = big[:, 2560:2560 + TT * NE * CAP].rearrange("p (a e c) -> p a e c", a=TT, e=NE)
        wsel = big[:, 4096:4096 + TT * NE * CAP].rearrange("p (a e c) -> p a e c", a=TT, e=NE)
        slots = sb("slots", [P, CAP])
        iot8 = sb("iot8", [P, NE])
        tri = sb("tri", [P, P])
        wgu = rows3[0:GRANK, 0:DEPTH, :]
        posi = qk[0:QK, 4 * T:5 * T].bitcast(I32)
        
        wr = sb("wr", [P, KD, NE])
        rt8 = sb("rt8", [P, TT, 8])
        ri8 = sb("ri8", [P, TT, 8], U32)
        rf8 = sb("rf8", [P, TT, 8])
        m12 = sb("m12", [P, TT, 2, NE])
        msel = sb("msel", [P, TT, NE])
        wt = sb("wt", [P, TT, NE])
        pos = sb("pos", [P, TT, NE])
        rsm = sb("rsm", [P, 16])
        npi = sb("npi", [P, 1], I32)
        yout = big[:, 0:TT * D].rearrange("p (a d) -> p a d", a=TT)

        PS = ctx.enter_context(nc.psum_tensor("PS", [P, 8, 512], F32))

        def use(L, name):
            i = USE[(L, name)]
            return PS[:, i % NB, :], sem(f"bank_full{i % NB}"), sem(f"bank_free{i % NB}"), i // NB

        def load_no(L, name):
            return L * (NL + NDENSE * len(UNIT_LOADS)) + LOADS.index(name)

        def slot_of(n):
            return n % NSLOT, n // NSLOT

        UNIT0 = [NL, 2 * NL + NDENSE * len(UNIT_LOADS)]
        PER = len(UNIT_LOADS) // NSLOT

        block = ctx.enter_context(nc.Block())

        @block.sync
        def _(sp):
            rows = ring[:, NSLOT - 1, 0:P]
            sp.dma_start(xin, A["x"].rearrange("b (a p) d -> p (b a) d", p=P)).then_inc(sem("x_in"), 16)

            sp.wait_ge(sem("rows_clear"), 1)
            for name, n in PARAMS:
                r0 = PCOL[name]
                wide = QK if name in ("g_qk_q", "g_qk_k") else P
                src = A[name] if wide == QK else A[name].rearrange("l (k p) -> (l k) p", p=P)
                sp.dma_start(rows[r0:r0 + n, 0:wide], src).then_inc(sem("params_in"), 16)
            sp.dma_start(posi[NOPE:QK, :], A["positions"].broadcast_to([ROPE, T])).then_inc(sem("pos_in"), 16)
            sp.dma_start(wgu[:, :, :], A["w_gla_gate_up"].rearrange("l r c -> r l c")).then_inc(sem("gu_in"), 16)
            sp.dma_start(wr[:, :, :], A["w_router"][0].rearrange("(k p) e -> p k e", p=P)).then_inc(sem("router_in"), 16)

            w_in, w_uq, w_ukv = A["w_in"], A["w_uq"], A["w_ukv"]

            def kp(ap):
                return ap.rearrange("(k p) c -> p k c", p=P)

            def mixer_read(L, name):
                _, full, _, n = use(L, LAST_USE[name])
                sp.wait_ge(full, n + 1)

            def unit_read(tag, uo, i):
                g = int(UNIT_LOADS[i][1])
                if UNIT_LOADS[i][0] == "D":
                    sp.wait_ge(sem(f"down_done_{tag}"), len(GROUPS) * uo + g + 1)
                else:
                    t = sum(GROUPS[g]) - 1
                    b, per = t % GU[tag], tiles_in_bank(GU[tag])
                    sp.wait_ge(sem(f"gu_full_{tag}{b}"), per[b] * uo + t // GU[tag] + 1)

            def mixer_load(L, name):
                s, r = slot_of(load_no(L, name))
                i = LOADS.index(name)
                if i == NSLOT - 1 and L == 0:
                    sp.wait_ge(use(-1, "par")[1], 1)
                if i >= NSLOT:
                    mixer_read(L, LOADS[i - NSLOT])
                elif L > 0:
                    unit_read("d", NDENSE - 1, len(UNIT_LOADS) - NSLOT + i)

                def put(src, cols, first=0):
                    kk = src.shape[0] // P
                    dst = ring[:, s, first:first + kk * cols].rearrange("p (k c) -> p k c", k=kk)
                    sp.dma_start(dst, kp(src)).then_inc(sem(f"slot_full{s}"), 16)

                cols = {"cq": (C_Q, 256), "ckv": (C_KV, 288), "gq": (C_GQ, 256), "gk": (C_GK, 256),
                        "va": (C_GV, 256), "vb": (C_GV + 256, 272), "oga": (C_OG, 256), "ogb": (C_OG + 256, 256),
                        "ua": (C_U, 256), "ub": (C_U + 256, 256)}
                if name in cols:
                    c0, cn = cols[name]
                    put(w_in[L, :, c0:c0 + cn], cn)
                elif name == "uq":
                    put(w_uq[L], H * QK)
                elif name == "ukv":
                    put(w_ukv[L], H * (NOPE + DV))
                elif name == "pool":
                    dst = ring[:, s, 0:NG * P].rearrange("p (g c) -> p g c", g=NG)
                    sp.dma_start(dst, A["w_pool"][L].rearrange("g p c -> p g c")).then_inc(sem(f"slot_full{s}"), 16)
                elif name[0] == "g":
                    b = int(name[1:])
                    put(w_in[L, :, C_G + b * GB:C_G + (b + 1) * GB], GB)
                elif name[:2] == "br":
                    n, hf = int(name[2]), int(name[3])
                    put(A["w_branch"][L, n, :, hf * 512:(hf + 1) * 512], 512)
                else:
                    m = int(name[3])
                    put(A["w_out"][L, :, m * GB:min((m + 1) * GB, D)], min(GB, D - m * GB))

            def unit_loads(tag, L, wg, wu, wd, x, uo):
                wg, wu, wd = wg[x], wu[x], wd[x]
                for i, name in enumerate(UNIT_LOADS):
                    s = i % NSLOT
                    g0, gn = GROUPS[int(name[1])]
                    if i >= NSLOT:
                        unit_read(tag, uo, i - NSLOT)
                    elif isinstance(uo, int) and uo == 0:
                        mixer_read(L, LOADS[NL - NSLOT + i])
                    else:
                        unit_read(tag, uo - 1, len(UNIT_LOADS) - NSLOT + i)
                    if name[0] == "D":
                        src = wd[g0 * P:(g0 + gn) * P, :].rearrange("(k p) c -> p k c", p=P)
                        dst = ring[:, s, 0:gn * D].rearrange("p (k c) -> p k c", k=gn)
                    else:
                        w = wg if name[0] == "G" else wu
                        src = w[:, g0 * P:(g0 + gn) * P].rearrange("(k p) c -> p k c", p=P)
                        dst = ring[:, s, 0:KD * gn * P].rearrange("p (k c) -> p k c", k=KD)
                    sp.dma_start(dst, src).then_inc(sem(f"slot_full{s}"), 16)

            for name in LOADS:
                mixer_load(0, name)
            fg = A["w_ffn_gate"][0].rearrange("k (u c) -> u k c", c=UF)
            fu = A["w_ffn_up"][0].rearrange("k (u c) -> u k c", c=UF)
            fd = A["w_ffn_down"][0].rearrange("(u k) c -> u k c", k=UF)
            unit_loads("d", 0, fg, fu, fd, 0, 0)
            with sp.Fori(1, NDENSE) as i:
                unit_loads("d", 0, fg, fu, fd, i, i)
            for name in LOADS:
                mixer_load(1, name)
            eg, eu, ed = A["w_exp_gate"][0], A["w_exp_up"][0], A["w_exp_down"][0]
            unit_loads("e", 1, eg, eu, ed, 0, 0)
            with sp.Fori(1, NE) as e:
                unit_loads("e", 1, eg, eu, ed, e, e)
            sp.wait_ge(sem("passes_known"), 1)
            npass = sp.value_load(npi[0:1, 0:1], min_val=1, max_val=PASSES)
            with sp.If(npass > 1):
                with sp.Fori(1, npass) as r:
                    with sp.Fori(0, NE) as e:
                        unit_loads("e", 1, eg, eu, ed, e, r * NE + e)
            sp.wait_ge(sem("y_out"), 4)
            sp.dma_start(out.rearrange("b (a p) d -> p (b a) d", p=P), yout).then_inc(sem("stored"), 16)
            sp.wait_ge(sem("stored"), 16)

        @block.tensor
        def _(pe):
            def begin(L, name):
                bank, full, free, n = use(L, name)
                if n >= 1:
                    pe.wait_ge(free, n)
                return bank, full

            def weights(L, name):
                s, r = slot_of(load_no(L, name))
                pe.wait_ge(sem(f"slot_full{s}"), 16 * (r + 1))
                return s

            def wslot(s, kk, cols):
                return ring[:, s, 0:kk * cols].rearrange("p (k c) -> p k c", k=kk)

            def evacuated(L, name):
                _, _, free, n = use(L, name)
                pe.wait_ge(free, n + 1)

            def project(dst, w, c0, m, rhs, kk=KD):
                for i in range(kk):
                    mm = pe.matmul(dst, w[:, i, c0:c0 + m], rhs(i), start=(i == 0), stop=(i == kk - 1))
                return mm

            def h_(i):
                return hT[:, i, :]

            def sumsq(L, name, layer):
                bank, full = begin(L, name)
                for i in range(4):
                    pe.wait_ge(sem("sq_act" if i % 2 == 0 else "sq_dve"), 2 * (2 * layer + (name == "ssf")) + i // 2 + 1)
                    for j in range(2):
                        kt = 2 * i + j
                        mm = pe.matmul(bank[:, 0:T], ones[:, :], sq[:, kt, :], start=(kt == 0), stop=(kt == KD - 1))
                mm.then_inc(full, 1)

            def pair(L, name, load, c0, cols):
                s = weights(L, load)
                w = wslot(s, KD, cols)
                bank, full = begin(L, name)
                project(bank[:, 0:T], w, c0, P, h_)
                mm = project(bank[:, T:2 * T], w, c0 + P, P, h_)
                mm.then_inc(full, 1)
                return s

            pe.wait_ge(sem("consts"), 1)
            pe.wait_ge(sem("params_in"), 16 * len(PARAMS))
            bank, full = begin(-1, "par")
            pe.transpose(bank[:, 0:NPAR], ring[0:NPAR, NSLOT - 1, 0:P], ident[0:NPAR, 0:NPAR]).then_inc(full, 1)
            bank, full = begin(-1, "inv")
            pe.matmul(bank[0:QK, 0:1], invr[:, :], one1[:, :], start=True, stop=True).then_inc(full, 1)
            pe.wait_ge(sem("x_in"), 16)
            for i in range(4):
                bank, full = begin(-1, f"x{i}")
                for j in range(2):
                    for a in range(TT):
                        mm = pe.transpose(bank[:, j * T + a * P:j * T + (a + 1) * P],
                                          xin[:, a, (2 * i + j) * P:(2 * i + j + 1) * P], ident[:, :])
                mm.then_inc(full, 1)

            def mixer(L):
                sumsq(L, "ssm", L)
                s = weights(L, "cq")
                w = wslot(s, KD, 256)
                bank, full = begin(L, "cq")
                for j in range(2):
                    for i in range(KD):
                        if j == 0:
                            pe.wait_ge(sem("h_ready"), 2 * KD * L + i + 1)
                        mm = pe.matmul(bank[:, j * T:(j + 1) * T], w[:, i, j * P:(j + 1) * P], h_(i),
                                       start=(i == 0), stop=(i == KD - 1))
                mm.then_inc(full, 1)
                s = pair(L, "ckv", "ckv", 0, 288)
                bank, full = begin(L, "kr")
                project(bank[NOPE:QK, 0:T], wslot(s, KD, 288), 256, ROPE, h_).then_inc(full, 1)
                s = pair(L, "gq", "gq", 0, 256)
                bank, full = begin(L, "sslat")
                evacuated(L, "ckv")
                for g in range(2):
                    for i in range(KR):
                        mm = pe.matmul(bank[:, g * T:(g + 1) * T], ones[:, :], sq[:, g * KR + i, :],
                                       start=(i == 0), stop=(i == KR - 1))
                mm.then_inc(full, 1)
                s = pair(L, "gk", "gk", 0, 256)
                s = weights(L, "uq")
                w = wslot(s, KR, H * QK)
                pe.wait_ge(sem("latn_ready"), 4 * L + KR)
                for i in range(4):
                    bank, full = begin(L, f"q{i}")
                    for j in range(2):
                        mm = project(bank[0:QK, j * T:(j + 1) * T], w, (2 * i + j) * QK, QK,
                                     lambda x: latn[:, x, :], KR)
                    mm.then_inc(full, 1)
                s = weights(L, "va")
                w = wslot(s, KD, 256)
                bank, full = begin(L, "va")
                for a in range(TT):
                    for i in range(KD):
                        mm = pe.matmul(bank[:, a * 256:(a + 1) * 256], hT[:, i, a * P:(a + 1) * P], w[:, i, 0:256],
                                       start=(i == 0), stop=(i == KD - 1))
                mm.then_inc(full, 1)
                s = weights(L, "ukv")
                w = wslot(s, KR, H * (NOPE + DV))
                pe.wait_ge(sem("latn_ready"), 4 * L + 2 * KR)
                for i in range(4):
                    bank, full = begin(L, f"k{i}")
                    for j in range(2):
                        mm = project(bank[0:NOPE, j * T:(j + 1) * T], w, (2 * i + j) * (NOPE + DV), NOPE,
                                     lambda x: latn[:, KR + x, :], KR)
                    mm.then_inc(full, 1)
                wv = w.rearrange("p k (h c) -> p k h c", h=H)
                for a in range(TT):
                    bank, full = begin(L, f"vm{a}")
                    for i in range(KR):
                        mm = pe.matmul(bank[:, :], latn[:, KR + i, a * P:(a + 1) * P], wv[:, i, :, NOPE:NOPE + DV],
                                       start=(i == 0), stop=(i == KR - 1))
                    mm.then_inc(full, 1)
                s = weights(L, "vb")
                w = wslot(s, KD, 272)
                bank, full = begin(L, "vb")
                for a in range(TT):
                    for i in range(KD):
                        mm = pe.matmul(bank[:, a * 256:(a + 1) * 256], hT[:, i, a * P:(a + 1) * P], w[:, i, 0:256],
                                       start=(i == 0), stop=(i == KD - 1))
                mm.then_inc(full, 1)
                bank, full = begin(L, "lr")
                project(bank[0:GRANK, 0:T], w, 256, GRANK, h_).then_inc(full, 1)
                s = pair(L, "oga", "oga", 0, 256)
                bank, full = begin(L, "ssq")
                evacuated(L, "q3")
                for a in range(TT):
                    for h in range(H):
                        mm = pe.matmul(bank[:, a * H + h:a * H + h + 1], sq[0:QK, h, a * P:(a + 1) * P],
                                       ones[0:QK, 0:1], start=True, stop=True)
                mm.then_inc(full, 1)
                evacuated(L, "k3")
                for i in range(4):
                    bank, full = begin(L, f"ssk{i}")
                    pe.matmul(bank[0:QK, :], ones[0:QK, 0:QK], sk[0:QK, 2 * i:2 * i + 2, :],
                              start=True, stop=True).then_inc(full, 1)
                bank, full = begin(L, "z")
                evacuated(L, "lr")
                pe.wait_ge(sem("gu_in"), 16)
                for d in range(2):
                    mm = pe.matmul(bank[:, d * T:(d + 1) * T], wgu[:, L, d * P:(d + 1) * P], glr[:, :],
                                   start=True, stop=True)
                mm.then_inc(full, 1)
                s = pair(L, "ogb", "ogb", 0, 256)
                for c, src in (("q", q), ("k", k)):
                    for i in range(4):
                        bank, full = begin(L, f"r{c}{i}")
                        evacuated(L, f"{c}{i}")
                        pe.matmul(bank[0:QK, :], R[:, :], src[:, 2 * i:2 * i + 2, :], start=True, stop=True).then_inc(full, 1)
                s = pair(L, "ua", "ua", 0, 256)
                s = pair(L, "ub", "ub", 0, 256)

                def gate(i):
                    bank, full = begin(L, f"g{i}")
                    for j in range(2):
                        t = 2 * i + j
                        b, c = t // 3, t % 3
                        s = weights(L, f"g{b}")
                        mm = project(bank[:, j * T:(j + 1) * T], wslot(s, KD, GB), c * P, P, h_)
                        if j == 1:
                            mm.then_inc(full, 1)

                def scores(h):
                    bank, full = begin(L, f"s{h}")
                    pe.wait_ge(sem("q_ready"), 4 * L + h // 2 + 1)
                    pe.wait_ge(sem("k_ready"), 4 * L + h // 2 + 1)
                    pe.matmul(bank[:, 0:P], q[:, h, 0:P], k[:, h, 0:P], start=True, stop=True)
                    pe.matmul(bank[:, P:3 * P], q[:, h, P:T], k[:, h, :], start=True, stop=True).then_inc(full, 1)

                def turn(h):
                    bank, full = begin(L, f"pt{h}")
                    pe.wait_ge(sem("p_ready"), H * L + h + 1)
                    for j in range(3):
                        mm = pe.transpose(bank[:, j * P:(j + 1) * P], Pr[:, h % 3, j * P:(j + 1) * P], ident[:, :])
                    mm.then_inc(full, 1)

                def values(i):
                    bank, full = begin(L, f"o{i}")
                    for j in range(2):
                        h = 2 * i + j
                        evacuated(L, f"pt{h}")
                        o = bank[j * DV:(j + 1) * DV, 0:T]
                        pe.matmul(o, vt[:, 0, h * DV:(h + 1) * DV], PT[:, j, 0:T], start=True, stop=False)
                        mm = pe.matmul(o[:, P:T], vt[:, 1, h * DV:(h + 1) * DV], PT[:, j, T:3 * P], start=False, stop=True)
                    mm.then_inc(full, 1)

                gate(0)
                scores(0), scores(1)
                gate(1)
                turn(0), turn(1)
                scores(2), scores(3)
                gate(2)
                values(0)
                turn(2), turn(3)
                scores(4), scores(5)
                gate(3)
                values(1)
                turn(4), turn(5)
                scores(6), scores(7)
                gate(4)
                values(2)
                turn(6), turn(7)
                s = weights(L, "pool")
                pe.wait_ge(sem("pooled"), L + 1)
                for i in range(2):
                    bank, full = begin(L, f"pl{i}")
                    for j in range(2):
                        g = 2 * i + j
                        mm = pe.matmul(bank[:, j * T:(j + 1) * T], ring[:, s, g * P:(g + 1) * P], u[:, g, PADW:PADW + T],
                                       start=True, stop=True)
                    mm.then_inc(full, 1)
                gate(5)
                values(3)

                def intra(a):
                    bank, full = begin(L, f"A{a}")
                    for d in range(2):
                        pe.wait_ge(sem("e_ready"), 4 * L + 2 * a + d + 1)
                        for c in range(GC):
                            mm = pe.matmul(bank[:, c * GH + 2 * d:c * GH + 2 * d + 2], E[:, d, c, :, :], selh[:, :],
                                           start=True, stop=True)
                    mm.then_inc(full, 1)

                def turn_k(a):
                    bank, full = begin(L, f"kd{a}")
                    pe.wait_ge(sem("dec_ready"), L + 1)
                    for d in range(2):
                        mm = pe.transpose(bank[:, d * P:(d + 1) * P], kdec[:, d, a * P:(a + 1) * P], ident[:, :])
                    mm.then_inc(full, 1)

                def go(h, lo, hi):
                    return PS[:, 6 + h // 2, (h % 2) * T + lo:(h % 2) * T + hi]

                def within(a):
                    pe.wait_ge(sem("attn_ready"), 2 * L + a + 1)
                    for h in range(GH):
                        mm = pe.matmul(go(h, a * P, (a + 1) * P), gvt[:, a, h * GDV:(h + 1) * GDV], attn[:, h, :],
                                       start=(a == 0 and h % 2 == 0), stop=False, skip_group_check=True)
                    mm.then_inc(sem("attn_used"), 1)

                def updates(a):
                    pe.wait_ge(sem("kdm_ready"), 2 * L + a + 1)
                    for i in range(4):
                        bank, full = begin(L, f"U{4 * a + i}")
                        for j in range(1 if 4 * a + i == 7 else 2):
                            n = 2 * i + j
                            for h in range(GH):
                                mm = pe.matmul(bank[(h % 2) * GDK:(h % 2 + 1) * GDK,
                                                    j * T + (h // 2) * P:j * T + (h // 2 + 1) * P],
                                               kdm[:, n, h * GDK:(h + 1) * GDK], gvt[:, a, h * GDV:(h + 1) * GDV],
                                               start=True, stop=True)
                        mm.then_inc(full, 1)

                def across(a):
                    for n in range(max(1, a * NCT), (a + 1) * NCT):
                        m = n - 1
                        if m % 2 == 1 or m == NCH - 2:
                            evacuated(L, f"U{m // 2}")
                        else:
                            pe.wait_ge(sem("state_ready"), (NCH // 2 - 1) * L + m // 2 + 1)
                        for h in range(GH):
                            mm = pe.matmul(go(h, n * GC, (n + 1) * GC), S[:, (n - 1) % NCT, h // 2, :],
                                           qdm[:, h % 2, h // 2, n * GC:(n + 1) * GC],
                                           start=False, stop=(n == NCH - 1), skip_group_check=True)
                        if n < NCH - 1:
                            mm.then_inc(sem("state_used"), 1)
                    if a == 1:
                        mm.then_inc(sem("go_full"), 1)

                intra(0)
                gate(6)
                intra(1)
                turn_k(0)
                within(0)
                gate(7)
                turn_k(1)
                within(1)
                updates(0)
                gate(8)
                across(0)
                updates(1)
                gate(9)
                across(1)
                gate(10)
                for i in range(2):
                    bank, full = begin(L, f"ssg{i}")
                    pe.wait_ge(sem("gsq_ready"), 2 * L + i + 1)
                    pe.matmul(bank[:, :], ones[:, :], gsq[:, i, :, :], start=True, stop=True).then_inc(full, 1)
                gate(11)
                for n in (0, 2, 1):
                    if n == 0:
                        evacuated(L, "o3")
                    elif n == 2:
                        evacuated(L, "pl1")
                    else:
                        pe.wait_ge(sem("yb_ready"), 2 * (L + 1))
                    for m in range(4):
                        s = weights(L, f"br{n}{m // 2}")
                        w = wslot(s, KB, 512)
                        bank, full = begin(L, f"b{n}{m}")
                        for j in range(2):
                            mm = project(bank[:, j * T:(j + 1) * T], w, (m % 2) * 256 + j * P, P,
                                         lambda x: ys[:, n * KB + x, :], KB)
                        mm.then_inc(full, 1)
                pe.wait_ge(sem("merged"), 4 * (L + 1))
                for m in range(4):
                    bank, full = begin(L, f"w{m}")
                    for j in range(2):
                        t = 2 * m + j
                        b, c = t // 3, t % 3
                        s = weights(L, f"out{b}")
                        w = wslot(s, KD, min(GB, D - b * GB))
                        mm = project(bank[:, j * T:(j + 1) * T], w, c * P, P, lambda x: merged[:, x, :])
                        if j == 1:
                            mm.then_inc(full, 1)
                sumsq(L, "ssf", L)
                for b in range(NB):
                    n = len([i for i in range(MIX_END[L]) if i % NB == b])
                    pe.wait_ge(sem(f"bank_free{b}"), n)

            def gate_up(tag, uo, base, g, N, rhs, first=False):
                g0, gn = GROUPS[g]
                n, per = GU[tag], tiles_in_bank(GU[tag])
                sg, su = loaded(uo, base, f"G{g}"), loaded(uo, base, f"U{g}")
                for t in range(g0, g0 + gn):
                    if t >= n or not first:
                        pe.wait_ge(sem(f"hid_ready_{tag}"), FT * uo + tile_before(t, n) + 1)
                    for j, s in enumerate((sg, su)):
                        mm = project(PS[:, t % n, j * N:(j + 1) * N], wslot(s, KD, gn * P), (t - g0) * P, P, rhs)
                    mm.then_inc(sem(f"gu_full_{tag}{t % n}"), 1)

            def down(tag, uo, base, g, acc):
                g0, gn = GROUPS[g]
                w = wslot(loaded(uo, base, f"D{g}"), gn, D)
                for t in range(g0, g0 + gn):
                    pe.wait_ge(sem(f"hid_ready_{tag}"), FT * uo + t + 1)
                    for m in range(KD):
                        mm = acc(m, w[:, t - g0, m * P:(m + 1) * P], t)
                mm.then_inc(sem(f"down_done_{tag}"), 1)

            def loaded(uo, base, name):
                i = UNIT_LOADS.index(name)
                pe.wait_ge(sem(f"slot_full{i % NSLOT}"), 16 * (PER * uo + base // NSLOT + i // NSLOT + 1))
                return i % NSLOT

            def dense(uo, first=False):
                def acc(m, w, t):
                    return pe.matmul(PS[:, 4 + m // 2, (m % 2) * T:(m % 2 + 1) * T], w, hid[:, t, :], start=False,
                                     stop=(t == FT - 1), skip_group_check=True)

                def gu(g):
                    gate_up("d", uo, UNIT0[0], g, T, h_, first)

                def dn(g):
                    down("d", uo, UNIT0[0], g, acc)
                gu(0), gu(1), dn(0), gu(2), dn(1), gu(3), dn(2), dn(3)

            mixer(0)
            pe.wait_ge(sem("h_ready"), KD * 2)
            for b in range(4, 8):
                pe.matmul(PS[:, b, :], zb[:, 0:P], zb[:, :], start=True, stop=True, skip_group_check=True)
            dense(0, first=True)
            with pe.Fori(1, NDENSE) as i:
                dense(i)
            mixer(1)

            pe.wait_ge(sem("h_ready"), KD * 2 * DEPTH)
            pe.wait_ge(sem("router_in"), 16)
            for a in range(TT):
                for i in range(KD):
                    mm = pe.matmul(PS[:, 0, a * NE:(a + 1) * NE], hT[:, i, a * P:(a + 1) * P], wr[:, i, :],
                                   start=(i == 0), stop=(i == KD - 1))
            mm.then_inc(sem("logits_full"), 1)
            for a in range(TT):
                for c in range(2):
                    for i in range(4):
                        kt = 4 * c + i
                        mm = pe.transpose(PS[:, 4 + 2 * a + c, i * P:(i + 1) * P], hT[:, kt, a * P:(a + 1) * P], ident[:, :])
                    mm.then_inc(sem("htok_full"), 1)
            pe.wait_ge(sem("msel_ready"), 1)
            pe.matmul(PS[:, 1, 0:NE], tri[:, :], msel[:, 0, :], start=True, stop=True)
            pe.matmul(PS[:, 1, NE:2 * NE], ones[:, :], msel[:, 0, :], start=True, stop=False)
            pe.matmul(PS[:, 1, NE:2 * NE], tri[:, :], msel[:, 1, :], start=False, stop=True)
            pe.matmul(PS[:, 1, 2 * NE:3 * NE], ones[:, :], msel[:, 0, :], start=True, stop=False)
            pe.matmul(PS[:, 1, 2 * NE:3 * NE], ones[:, :], msel[:, 1, :], start=False, stop=True)\
              .then_inc(sem("rank_full"), 1)
            pe.wait_ge(sem("htok_ready"), 4)

            def gather(e, n, first=False):
                if not first:
                    pe.wait_ge(sem("hTe_act"), n)
                    pe.wait_ge(sem("hTe_dve"), n)
                for c in range(2):
                    for i in range(4):
                        for a in range(TT):
                            mm = pe.matmul(PS[:, 4 + c, i * CAP:(i + 1) * CAP], htok[:, a, (4 * c + i) * P:(4 * c + i + 1) * P],
                                           psel[:, a, e, :], start=(a == 0), stop=(a == TT - 1))
                    mm.then_inc(sem(f"gath_full{c}"), 1)

            def turn_y(n):
                pe.wait_ge(sem("yT_ready"), 2 * n + 2)
                if not (isinstance(n, int) and n == 0):
                    pe.wait_ge(sem("x_added"), 4 * n)
                for c in range(2):
                    for i in range(4):
                        mm = pe.transpose(PS[0:CAP, 6 + c, i * P:(i + 1) * P], yT[:, 4 * c + i, :], ident[:, :])
                    mm.then_inc(sem(f"yt_full{c}"), 1)

            def scatter(e, n):
                pe.wait_ge(sem("ye_act"), n + 1)
                pe.wait_ge(sem("ye_dve"), n + 1)
                for c in range(4):
                    if c >= 2:
                        pe.wait_ge(sem("x_added"), 4 * n + c - 1)
                    for j in range(2):
                        kt = 2 * c + j
                        mm = pe.matmul(PS[:, 6 + c % 2, j * T:(j + 1) * T], ye[:, kt * P:(kt + 1) * P], selT[:, e, :],
                                       start=True, stop=True)
                    mm.then_inc(sem("scat_full"), 1)

            def acc(m, w, t):
                return pe.matmul(PS[:, 2 + m // 4, (m % 4) * CAP:(m % 4 + 1) * CAP], w, hid[:, t, 0:CAP],
                                 start=(t == 0 and m % 4 == 0), stop=(t == FT - 1), skip_group_check=True)

            def expert(e, n, after=False, first=False, ahead=True):
                def gu(g):
                    gate_up("e", n, UNIT0[1], g, CAP, lambda i: hTe[:, i, :], first)

                def dn(g):
                    down("e", n, UNIT0[1], g, acc)
                pe.wait_ge(sem("hTe_act"), n + 1)
                pe.wait_ge(sem("hTe_dve"), n + 1)
                gu(0)
                if after:
                    turn_y(n - 1)
                gu(1)
                if after:
                    scatter(e - 1, n - 1)
                if not first:
                    pe.wait_ge(sem("yT_ready"), 2 * n)
                dn(0), gu(2), dn(1), gu(3)
                if ahead:
                    gather(e + 1, n + 1)
                dn(2), dn(3)

            def prepare(r):
                pe.wait_ge(sem("sel_ready"), 2 * (r + 1))
                for c in range(4):
                    if c >= 2:
                        pe.wait_ge(sem("selT_ready"), 4 * r + c - 1)
                    for i in range(2):
                        for a in range(TT):
                            mm = pe.transpose(PS[0:CAP, 6 + c % 2, i * T + a * P:i * T + (a + 1) * P],
                                              wsel[:, a, 2 * c + i, :], ident[:, :])
                    mm.then_inc(sem("selT_full"), 1)
                pe.wait_ge(sem("selT_ready"), 4 * r + 4)

            def one_pass(r):
                prepare(r)
                n = r * NE
                start = isinstance(r, int)
                gather(0, n, first=start)
                expert(0, n, first=start)
                with pe.Fori(1, NE - 1) as e:
                    expert(e, n + e, after=True)
                expert(NE - 1, n + NE - 1, after=True, ahead=False)
                turn_y(n + NE - 1)
                scatter(NE - 1, n + NE - 1)
                pe.wait_ge(sem("x_added"), 4 * (n + NE))

            one_pass(0)
            pe.wait_ge(sem("passes_known"), 1)
            npass = pe.value_load(npi[0:1, 0:1], min_val=1, max_val=PASSES)
            with pe.If(npass > 1):
                with pe.Fori(1, npass) as r:
                    one_pass(r)
            for i in range(4):
                bank = PS[:, 2 + i, :]
                for j in range(4):
                    a, kt = i // 2, 4 * (i % 2) + j
                    mm = pe.transpose(bank[:, j * P:(j + 1) * P], xT[:, kt, a * P:(a + 1) * P], ident[:, :])
                mm.then_inc(sem("yo_full"), 1)

        @block.gpsimd
        def _(pool):
            step = Chain(pool, sem("pool_step"))
            pool.memset(ring[:, NSLOT - 1, 0:P], 0.0).then_inc(sem("rows_clear"), 1)
            for t, v in ((ident, 0.0), (ones, 1.0), (zb, 0.0), (maskc, 0.0), (maskg, 1.0), (chm, 1.0), (keep, 1.0),
                         (eps, EPS), (one1, 1.0), (invr, 0.0), (R, 0.0), (tri, 1.0), (u, 0.0), (qdm, 0.0), (selh, 0.0)):
                pool.memset(t[:], v).then_inc(sem("pool_step"), 1)
                step.n += 1
            step.wait()
            for i in range(ROPE):
                step(pool.memset(invr[0:1, NOPE + i:NOPE + i + 1], float(np.float32(ROPE_BASE ** (-(i % HALF) / HALF)))))
            step(pool.memset(selh[0:GDK, 0:1], GDK ** -0.5))
            step(pool.memset(selh[GDK:P, 1:2], GDK ** -0.5))

            def select(t, pattern, base, cm, fill, op=ALU.is_ge):
                step(pool.affine_select(out=t, in_=t, compare_op=op, fill=fill, base=base, pattern=pattern,
                                        channel_multiplier=cm))
            select(ident[:, :], [[-1, P]], 0, 1, 1.0, ALU.not_equal)
            select(maskc[:, 0:P], [[-1, P]], 0, 1, NEG)
            select(maskc[:, 2 * P:3 * P], [[-1, P]], 0, 1, NEG)
            g3 = maskg[:, :].rearrange("p (n c) -> p n c", n=NCT)
            select(g3, [[-GC, NCT], [0, GC]], 0, 1, 0.0)
            select(g3, [[GC, NCT], [0, GC]], GC - 1, -1, 0.0)
            select(g3, [[GC, NCT], [1, GC]], 0, -1, 0.0)
            select(chm[:, :], [[-GC, NCT]], 0, 1, 0.0)
            select(chm[:, :], [[GC, NCT]], GC - 1, -1, 0.0)
            k3 = keep[:, :].rearrange("p (n c) -> p n c", c=GC)
            select(k3, [[0, NCH], [1, GC]], 0, 0, 0.0, ALU.not_equal)
            rr_ = R[NOPE:QK, NOPE:QK]
            select(rr_, [[-1, ROPE]], -HALF, 1, -1.0, ALU.not_equal)
            select(rr_, [[-1, ROPE]], HALF, 1, 1.0, ALU.not_equal)
            select(tri[:, :], [[1, P]], -1, -1, 0.0)
            pool.iota(cnt[:, :], pattern=[[1, PADW]], base=1, channel_multiplier=0).then_inc(sem("iotas"), 1)
            pool.iota(sloti[:, :], pattern=[[1, CAP]], base=0, channel_multiplier=0).then_inc(sem("iotas"), 1)
            pool.memset(one1[:, :], 1.0).then_inc(sem("consts"), 1)
            for L in range(DEPTH):
                for a in range(TT):
                    for d in range(2):
                        pool.wait_ge(sem("e_exp"), 4 * L + 2 * a + d + 1)
                        e = scr[:, d * 2048:(d + 1) * 2048].rearrange("p (c t) -> p c t", c=GC)
                        ins = pool.tensor_tensor(e, e, gk[:, d, a * P:(a + 1) * P].unsqueeze(1).broadcast_to([P, GC, P]), MUL)
                        ins.then_inc(sem("e_k"), 1)

        @block.scalar
        def _(act):
            def full(L, name):
                bank, f, free, n = use(L, name)
                act.wait_ge(f, n + 1)
                return bank, free

            def freed(L, name):
                _, _, free, n = use(L, name)
                act.wait_ge(free, n + 1)

            def pcol(name, i=0, rows=P):
                return par[0:rows, PCOL[name] + i:PCOL[name] + i + 1]

            def two(ap):
                return ap.rearrange("p (a t) -> p a t", a=2)

            bank, free = full(-1, "par")
            act.activation(par[:, :], bank[:, 0:NPAR], ACT.Copy).then_inc(free, 1)
            bank, free = full(-1, "inv")
            act.activation(invc[NOPE:QK, :], bank[NOPE:QK, 0:1], ACT.Copy).then_inc(free, 1)

            def squares(L, first):
                for i in (0, 2):
                    if L < 0:
                        freed(-1, f"x{i}")
                    act.activation(sq[:, 2 * i:2 * i + 2, :], xT[:, 2 * i:2 * i + 2, :], ACT.Square)\
                       .then_inc(sem("sq_act"), 1)

            nrt = [0]

            def root(bank, free, n, scale):
                if nrt[0]:
                    act.wait_ge(sem("rt_read"), nrt[0])
                nrt[0] += 1
                act.activation(rt[:, 0:n, :], bank[:, 0:n * T].rearrange("p (a t) -> p a t", a=n), ACT.Sqrt,
                               bias=eps[:, 0:1], scale=scale).then_inc(free, 1)

            def mixer(L):
                for i in (0, 2):
                    if L == 0:
                        freed(-1, f"x{i}")
                    else:
                        act.wait_ge(sem("x_dense"), i + 2)
                    act.activation(sq[:, 2 * i:2 * i + 2, :], xT[:, 2 * i:2 * i + 2, :], ACT.Square)\
                       .then_inc(sem("sq_act"), 1)
                if L == 0:
                    act.wait_ge(sem("consts"), 1)
                root(*full(L, "ssm"), 1, 1.0 / D)
                for i, name in enumerate(("cq", "ckv")):
                    bank, free = full(L, name)
                    act.activation(sq[:, 2 * i:2 * i + 2, :], two(bank), ACT.Square)
                    act.activation(lat[:, 2 * i:2 * i + 2, :], two(bank), ACT.Copy).then_inc(free, 1)
                bank, free = full(L, "kr")
                act.activation(krope[NOPE:QK, :], bank[NOPE:QK, 0:T], ACT.Copy).then_inc(free, 1)
                if L == 0:
                    act.wait_ge(sem("angles"), 1)
                    act.activation(cs[NOPE:QK, :, :], ang[NOPE:QK, 1:3, :], ACT.Sin).then_inc(sem("rope_tables"), 1)
                root(*full(L, "sslat"), 2, 1.0 / RANK)
                for i in range(4):
                    bank, free = full(L, f"q{i}")
                    act.activation(sq[0:QK, 2 * i:2 * i + 2, :], two(bank[0:QK, :]), ACT.Square)
                    act.activation(q[:, 2 * i:2 * i + 2, :], two(bank[0:QK, :]), ACT.Copy,
                                   scale=pcol("g_qk_q", L, QK)).then_inc(free, 1)
                freed(L, "kr")
                kr8 = krope[NOPE:QK, :].unsqueeze(1).broadcast_to([ROPE, H, T])
                act.activation(sk[NOPE:QK, :, :], kr8, ACT.Square)
                act.activation(k[NOPE:QK, :, :], kr8, ACT.Copy, scale=par[NOPE:QK, PCOL["g_qk_k"] + L:PCOL["g_qk_k"] + L + 1])
                for i in range(4):
                    bank, free = full(L, f"k{i}")
                    act.activation(sk[0:NOPE, 2 * i:2 * i + 2, :], two(bank[0:NOPE, :]), ACT.Square)
                    act.activation(k[0:NOPE, 2 * i:2 * i + 2, :], two(bank[0:NOPE, :]), ACT.Copy,
                                   scale=pcol("g_qk_k", L, NOPE)).then_inc(free, 1)
                bank, free = full(L, "lr")
                act.activation(glr[:, :], bank[0:GRANK, 0:T], ACT.Copy).then_inc(free, 1)

                def out_gate(i):
                    bank, _ = full(L, f"og{'ab'[i]}")
                    if 2 * L + i:
                        act.wait_ge(sem("og_done"), 2 * L + i)
                    act.activation(th[:, :, :], two(bank), ACT.Tanh, scale=0.5).then_inc(sem("og_tanh"), 1)
                out_gate(0)
                bank, free = full(L, "ssq")
                act.activation(rq16[:, :], bank[:, 0:TT * H], ACT.Sqrt, bias=eps[:, 0:1], scale=1.0 / QK).then_inc(free, 1)
                for i in range(4):
                    bank, free = full(L, f"ssk{i}")
                    act.activation(sk[0:QK, 2 * i:2 * i + 2, :], two(bank[0:QK, :]), ACT.Sqrt, bias=eps[0:QK, 0:1],
                                   scale=1.0 / QK).then_inc(free, 1)
                freed(L, "z")
                act.activation(ztmp[:, 2:4, :], ztmp[:, 0:2, :], ACT.Abs).then_inc(sem("z_step"), 1)
                act.wait_ge(sem("z_step"), 3 * L + 1)
                act.activation(ztmp[:, 2:4, :], ztmp[:, 2:4, :], ACT.Exp, scale=-1.0).then_inc(sem("z_step"), 1)
                act.wait_ge(sem("z_step"), 3 * L + 2)
                act.activation(ztmp[:, 2:4, :], ztmp[:, 2:4, :], ACT.Ln, bias=1.0).then_inc(sem("z_step"), 1)
                out_gate(1)
                for i, name in enumerate(("ua", "ub")):
                    bank, free = full(L, name)
                    act.activation(u[:, 2 * i:2 * i + 2, PADW:PADW + T], two(bank), ACT.Copy).then_inc(free, 1)
                act.wait_ge(sem("bc_ready"), L + 1)
                act.activation(eb[:, :, :], bc[:, :, :], ACT.Exp).then_inc(sem("eb_ready"), 1)
                act.activation(al[:, :, :], bc[:, :, :].rearrange("p d (n c) -> p d n c", c=GC)[:, :, :, GC - 1],
                               ACT.Exp).then_inc(sem("al_ready"), 1)
                act.wait_ge(sem("db_ready"), L + 1)
                act.activation(ek[:, :, :], ek[:, :, :], ACT.Exp).then_inc(sem("ek_ready"), 1)

                def gate(i):
                    bank, free = full(L, f"g{i}")
                    if i == 0:
                        act.wait_ge(sem("latn_ready"), 4 * (L + 1))
                        _, f, _, n = use(L, "vm1")
                        act.wait_ge(f, n + 1)
                    if i == 8:
                        act.wait_ge(sem("k_ready"), 4 * (L + 1))
                    act.activation(gates[:, 2 * i:2 * i + 2, :], two(bank), ACT.Tanh, scale=0.5).then_inc(free, 1)

                def exps(h):
                    act.wait_ge(sem("nb_ready"), H * L + h + 1)
                    for a in range(TT):
                        w = slice(0, P) if a == 0 else slice(P, 3 * P)
                        ins = act.activation(Pr[:, h % 3, w], Pr[:, h % 3, w], ACT.Exp, bias=nbs[:, h % 2, a:a + 1],
                                             scale=rqs[:, a * H + h:a * H + h + 1], accum_out=sums[:, h % 2, a:a + 1])
                    ins.then_inc(sem("exp_done"), 1)

                def turned(h):
                    bank, free = full(L, f"pt{h}")
                    if h >= 2:
                        _, f, _, n = use(L, f"o{(h - 2) // 2}")
                        act.wait_ge(f, n + 1)
                    act.activation(PT[:, h % 2, :], bank[:, 0:3 * P], ACT.Copy).then_inc(free, 1)

                def values(i):
                    bank, free = full(L, f"o{i}")
                    act.activation(ys[:, i, :], bank[:, 0:T], ACT.Copy).then_inc(free, 1)

                def decay(a, d):
                    act.wait_ge(sem("e_diff"), 4 * L + 2 * a + d + 1)
                    e = scr[:, d * 2048:(d + 1) * 2048]
                    act.activation(e, e, ACT.Exp).then_inc(sem("e_exp"), 1)

                def pool_out(i):
                    bank, free = full(L, f"pl{i}")
                    for j in range(2):
                        ins = act.activation(ys[:, 2 * KB + 2 * i + j, :], bank[:, j * T:(j + 1) * T], ACT.Copy,
                                             scale=pcol("pool_scale", L * NG + 2 * i + j))
                    ins.then_inc(free, 1)

                gate(0), exps(0), exps(1), gate(1), turned(0), turned(1), exps(2), exps(3)
                gate(2), values(0), turned(2), turned(3), exps(4), exps(5)
                gate(3), values(1), turned(4), turned(5), exps(6), exps(7)
                gate(4), values(2), turned(6), turned(7), pool_out(0), pool_out(1)
                decay(0, 0), decay(0, 1)
                gate(5), values(3), gate(6)
                decay(1, 0), decay(1, 1)
                gate(7), gate(8), gate(9)
                act.wait_ge(sem("go_full"), L + 1)
                for i in range(2):
                    act.activation(gsq[:, i, :, :], two(PS[:, 6 + i, :]), ACT.Square).then_inc(sem("gsq_ready"), 1)
                gate(10)
                for i in range(2):
                    bank, free = full(L, f"ssg{i}")
                    if i == 0:
                        root(bank, free, 2, 1.0 / GDV)
                    else:
                        root(bank, free, 2, 1.0 / GDV)
                gate(11)
                for i in (0, 2):
                    freed(L, f"w{i + 1}")
                    freed(L, f"w{i}")
                    act.activation(sq[:, 2 * i:2 * i + 2, :], xT[:, 2 * i:2 * i + 2, :], ACT.Square)\
                       .then_inc(sem("sq_act"), 1)
                root(*full(L, "ssf"), 1, 1.0 / D)

            def silu(tag, uo, t, N, first=False):
                n = 4
                b, per = t % GU[tag], tiles_in_bank(GU[tag])
                act.wait_ge(sem(f"gu_full_{tag}{b}"), per[b] * uo + t // GU[tag] + 1)
                if t >= n or not first:
                    act.wait_ge(sem(f"hid_ready_{tag}"), FT * uo + tile_before(t, n) + 1)
                act.activation(sil[:, t % n, 0:N], PS[:, b, 0:N], ACT.Silu).then_inc(sem(f"sil_ready_{tag}"), 1)

            mixer(0)
            for t in range(FT):
                silu("d", 0, t, T, first=True)
            with act.Fori(1, NDENSE) as i:
                for t in range(FT):
                    silu("d", i, t, T)
            mixer(1)

            act.wait_ge(sem("logit_gap"), 1)
            act.activation(rsm[:, 2:4], rsm[:, 0:2], ACT.Exp).then_inc(sem("top_exp"), 1)

            def tokens(n, first=False):
                act.wait_ge(sem("gath_full0"), n + 1)
                if not first:
                    act.wait_ge(sem("gu_full_e0"), tiles_in_bank(2)[0] * n)
                act.activation(hTe[:, 0:4, :], PS[:, 4, 0:4 * CAP].rearrange("p (k c) -> p k c", k=4), ACT.Copy)\
                   .then_inc(sem("hTe_act"), 1)

            def rows_out(n):
                act.wait_ge(sem("yt_full0"), n + 1)
                if not (isinstance(n, int) and n == 0):
                    act.wait_ge(sem("scat_full"), 4 * n)
                act.activation(ye[:, 0:512], PS[0:CAP, 6, :], ACT.Copy).then_inc(sem("ye_act"), 1)

            def expert(n, after=False, first=False, ahead=True):
                for t in range(FT):
                    silu("e", n, t, CAP, first)
                    if t == 2 and after:
                        rows_out(n - 1)
                if ahead:
                    tokens(n + 1)
                act.wait_ge(sem("down_done_e"), len(GROUPS) * (n + 1))
                if not first:
                    act.wait_ge(sem("yt_full1"), n)
                for c in range(2):
                    act.activation(yT[:, 4 * c:4 * c + 4, :], PS[:, 2 + c, 0:4 * CAP].rearrange("p (k c) -> p k c", k=4),
                                   ACT.Copy).then_inc(sem("yT_ready"), 1)

            def one_pass(r):
                n, start = r * NE, isinstance(r, int)
                for c in range(4):
                    act.wait_ge(sem("selT_full"), 4 * r + c + 1)
                    act.activation(selT[:, 2 * c:2 * c + 2, :], two(PS[0:CAP, 6 + c % 2, :]), ACT.Copy)\
                       .then_inc(sem("selT_ready"), 1)
                tokens(n, first=start)
                expert(n, first=start)
                with act.Fori(1, NE - 1) as e:
                    expert(n + e, after=True)
                expert(n + NE - 1, after=True, ahead=False)
                rows_out(n + NE - 1)

            one_pass(0)
            act.wait_ge(sem("passes_known"), 1)
            npass = act.value_load(npi[0:1, 0:1], min_val=1, max_val=PASSES)
            with act.If(npass > 1):
                with act.Fori(1, npass) as r:
                    one_pass(r)
            for i in range(4):
                act.wait_ge(sem("yo_full"), i + 1)
                act.activation(yout[:, i // 2, (i % 2) * 512:(i % 2 + 1) * 512], PS[:, 2 + i, :], ACT.Copy)\
                   .then_inc(sem("y_out"), 1)

        @block.vector
        def _(dve):
            step = Chain(dve, sem("dve_step"))

            def full(L, name):
                bank, f, free, n = use(L, name)
                dve.wait_ge(f, n + 1)
                return bank, free

            def freed(L, name):
                _, _, free, n = use(L, name)
                dve.wait_ge(free, n + 1)

            def pcol(name, i=0, rows=P):
                return par[0:rows, PCOL[name] + i:PCOL[name] + i + 1]

            def two(ap):
                return ap.rearrange("p (a t) -> p a t", a=2)

            for i in range(4):
                bank, free = full(-1, f"x{i}")
                dve.tensor_copy(xT[:, 2 * i:2 * i + 2, :], two(bank)).then_inc(free, 1)

            def tables():
                TWO_PI = 2 * np.pi
                c1 = 6.28125
                c2 = float(np.float32(np.floor((TWO_PI - c1) * 2 ** 21) / 2 ** 21))
                c3 = float(np.float32(TWO_PI - c1 - c2))
                magic = 1.5 * 2 ** 23
                pi = float(np.nextafter(np.float32(np.pi), np.float32(0)))
                r = slice(NOPE, QK)
                dve.wait_ge(sem("pos_in"), 16)
                step(dve.tensor_copy(ang[r, 0, :], posi[r, :]))
                freed(-1, "inv")
                step(dve.tensor_scalar(ang[r, 0, :], ang[r, 0, :], invc[r, 0:1], None, MUL))
                for j, shift in ((1, 0.25), (2, 0.0)):
                    step(dve.tensor_scalar(angk[r, :], ang[r, 0, :], 1 / TWO_PI, shift, MUL, ADD))
                    step(dve.tensor_scalar(angk[r, :], angk[r, :], magic, magic, ADD, SUB))
                    step(dve.scalar_tensor_tensor(ang[r, j, :], angk[r, :], -c1, ang[r, 0, :], MUL, ADD))
                    step(dve.scalar_tensor_tensor(ang[r, j, :], angk[r, :], -c2, ang[r, j, :], MUL, ADD))
                    step(dve.scalar_tensor_tensor(ang[r, j, :], angk[r, :], -c3, ang[r, j, :], MUL, ADD))
                    if shift:
                        step(dve.tensor_scalar(ang[r, j, :], ang[r, j, :], np.pi / 2, None, ADD))
                    ins = dve.tensor_scalar(ang[r, j, :], ang[r, j, :], pi, -pi, MIN, MAX)
                    if j == 1:
                        step(ins)
                ins.then_inc(sem("angles"), 1)
                dve.wait_ge(sem("iotas"), 2)
                for g, w in enumerate(WINDOWS):
                    step(dve.tensor_scalar(winf[:, g, :], cnt[:, :], float(w), 1.0 / w, MIN, MUL))
                step(dve.reciprocal(winf[:, :, :], winf[:, :, :]))
                step(dve.tensor_copy(slots[:, :], sloti[:, :]))
                step(dve.tensor_copy(iot8[:, :], sloti[:, 0:NE]))

            def inverse(n, bank_free_of):
                freed(*bank_free_of)
                dve.reciprocal(rr[:, 0:n, :], rt[:, 0:n, :]).then_inc(sem("rt_read"), 1)
                inv_n[0] += 1
                dve.wait_ge(sem("rt_read"), inv_n[0])

            inv_n = [0]

            def norm_x(L, which, gain):
                for i in (1, 3):
                    if which == "ssm" and L == 1:
                        dve.wait_ge(sem("x_dense"), i + 1)
                    elif which == "ssf":
                        freed(L, f"w{i}")
                    else:
                        freed(-1, f"x{i}")
                    dve.tensor_tensor(sq[:, 2 * i:2 * i + 2, :], xT[:, 2 * i:2 * i + 2, :], xT[:, 2 * i:2 * i + 2, :], MUL)\
                       .then_inc(sem("sq_dve"), 1)
                inverse(1, (L, which))
                for i in range(KD):
                    dve.scalar_tensor_tensor(hT[:, i, :], xT[:, i, :], pcol(gain, L * KD + i), rr[:, 0, :], MUL, MUL)\
                       .then_inc(sem("h_ready"), 1)

            def mixer(L):
                norm_x(L, "ssm", "g_mix")
                if L == 0:
                    tables()
                bank, free = full(L, "gq")
                dve.tensor_copy(gq[:, :, :], two(bank)).then_inc(free, 1)
                inverse(2, (L, "sslat"))
                for i in range(4):
                    g = pcol("g_cq" if i < 2 else "g_ckv", L * KR + i % 2)
                    dve.scalar_tensor_tensor(latn[:, i, :], lat[:, i, :], g, rr[:, i // 2, :], MUL, MUL)\
                       .then_inc(sem("latn_ready"), 1)
                bank, free = full(L, "gk")
                dve.tensor_copy(gk[:, :, :], two(bank)).then_inc(free, 1)

                def v_half(name, c):
                    bank, free = full(L, name)
                    dve.tensor_copy(gvt[:, :, c * 256:(c + 1) * 256], two(bank)).then_inc(free, 1)
                v_half("va", 0)
                for a in range(TT):
                    bank, free = full(L, f"vm{a}")
                    dve.tensor_copy(vt[:, a, :], bank).then_inc(free, 1)
                v_half("vb", 1)

                def out_gate(i):
                    bank, free = full(L, f"og{'ab'[i]}")
                    dve.wait_ge(sem("og_tanh"), 2 * L + i + 1)
                    y = ys[:, KB + 2 * i:KB + 2 * i + 2, :]
                    dve.scalar_tensor_tensor(y, th[:, :, :], 1.0, two(bank), ADD, MUL).then_inc(free, 1)
                    freed(L, f"og{'ab'[i]}")
                    dve.engine_nop().then_inc(sem("og_done"), 1)
                out_gate(0)
                freed(L, "ssq")
                step(dve.reciprocal(rqs[:, :], rq16[:, :]))
                step(dve.tensor_scalar(rqs[:, :], rqs[:, :], QK ** -0.5, None, MUL))
                bank, free = full(L, "z")
                for d in range(2):
                    ins = dve.tensor_scalar(ztmp[:, d, :], bank[:, d * T:(d + 1) * T], pcol("b_gla_gate", 2 * L + d), None, ADD)
                ins.then_inc(free, 1)
                for i in range(4):
                    freed(L, f"ssk{i}")
                    step(dve.reciprocal(sk[0:QK, 2 * i:2 * i + 2, :], sk[0:QK, 2 * i:2 * i + 2, :]))
                freed(L, "z")
                dve.wait_ge(sem("z_step"), 3 * L + 3)
                step(dve.scalar_tensor_tensor(ztmp[:, 0:2, :], ztmp[:, 0:2, :], 0.0, ztmp[:, 2:4, :], MIN, SUB))
                step(dve.tensor_scalar(ztmp[:, 0:2, :], ztmp[:, 0:2, :], 1.0 / TAU, None, MUL))
                for d in range(2):
                    ins = dve.tensor_tensor_scan(bc[:, d, :], keep[:, :], ztmp[:, d, :], 0.0, MUL, ADD)
                    if d == 0:
                        step(ins)
                ins.then_inc(sem("bc_ready"), 1)
                dve.wait_ge(sem("bc_ready"), L + 1)
                out_gate(1)

                r = slice(NOPE, QK)
                for c, t in (("q", q), ("k", k)):
                    for i in range(4):
                        bank, free = full(L, f"r{c}{i}")
                        if L == 0 and c == "q" and i == 0:
                            dve.wait_ge(sem("rope_tables"), 1)
                        x = t[r, 2 * i:2 * i + 2, :]
                        cos, sin = (cs[r, j, :].unsqueeze(1).broadcast_to([ROPE, 2, T]) for j in (0, 1))
                        dve.tensor_tensor(rtmp[r, :, :], two(bank[r, :]), sin, MUL).then_inc(free, 1)
                        step(dve.tensor_tensor(x, x, cos, MUL))
                        freed(L, f"r{c}{i}")
                        if c == "q":
                            dve.tensor_tensor(x, x, rtmp[r, :, :], ADD).then_inc(sem("q_ready"), 1)
                            dve.wait_ge(sem("q_ready"), 4 * L + i + 1)
                        else:
                            step(dve.tensor_tensor(x, x, rtmp[r, :, :], ADD))
                            dve.tensor_tensor(k[:, 2 * i:2 * i + 2, :], k[:, 2 * i:2 * i + 2, :],
                                              sk[0:QK, 2 * i:2 * i + 2, :], MUL).then_inc(sem("k_ready"), 1)
                            dve.wait_ge(sem("k_ready"), 4 * L + i + 1)

                b4 = bc[:, :, :].rearrange("p d (n c) -> p d n c", c=GC)
                for d in range(2):
                    ins = dve.tensor_tensor(ek[:, d, :].rearrange("p (n c) -> p n c", c=GC),
                                            b4[:, d, :, GC - 1:GC].broadcast_to([P, NCH, GC]), b4[:, d], SUB)
                    if d == 0:
                        step(ins)
                ins.then_inc(sem("db_ready"), 1)

                def masked(h):
                    bank, free = full(L, f"s{h}")
                    if h >= 3:
                        _, f, _, n = use(L, f"pt{h - 3}")
                        dve.wait_ge(f, n + 1)
                    dve.tensor_tensor(Pr[:, h % 3, :], bank[:, 0:3 * P], maskc[:, :], ADD).then_inc(free, 1)
                    freed(L, f"s{h}")
                    for a, w in ((0, slice(0, P)), (1, slice(P, 3 * P))):
                        step(dve.tensor_reduce(mx[:, h % 2, a:a + 1], Pr[:, h % 3, w], AX.X, MAX))
                    for a in range(TT):
                        ins = dve.tensor_scalar(nbs[:, h % 2, a:a + 1], mx[:, h % 2, a:a + 1],
                                                rqs[:, a * H + h:a * H + h + 1], -1.0, MUL, MUL)
                        if a == 0:
                            step(ins)
                    ins.then_inc(sem("nb_ready"), 1)

                def scaled(h):
                    dve.wait_ge(sem("exp_done"), H * L + h + 1)
                    step(dve.reciprocal(mx[:, h % 2, :], sums[:, h % 2, :]))
                    for a, w in ((0, slice(0, P)), (1, slice(P, 3 * P))):
                        ins = dve.tensor_scalar(Pr[:, h % 3, w], Pr[:, h % 3, w], mx[:, h % 2, a:a + 1], None, MUL)
                        if a == 0:
                            step(ins)
                    ins.then_inc(sem("p_ready"), 1)
                    dve.wait_ge(sem("p_ready"), H * L + h + 1)

                masked(0), masked(1)
                dve.wait_ge(sem("eb_ready"), L + 1)
                for c in range(2):
                    rows = slice(c * GDK, (c + 1) * GDK)
                    step(dve.tensor_tensor(qdm[rows, c, :, :], gq[rows, :, :], eb[rows, :, :], MUL))
                step(dve.tensor_scalar(qdm[:, :, :, :], qdm[:, :, :, :], GDK ** -0.5, None, MUL))
                dve.wait_ge(sem("ek_ready"), L + 1)
                dve.tensor_tensor(kdec[:, :, :], gk[:, :, :], ek[:, :, :], MUL).then_inc(sem("dec_ready"), 1)
                scaled(0), scaled(1), masked(2), masked(3)
                scaled(2), scaled(3), masked(4), masked(5)
                freed(L, "ub")
                W = PADW + T
                step(dve.tensor_tensor(pwa[:, :, 1:W], u[:, :, 1:W], u[:, :, 0:W - 1], ADD))
                step(dve.tensor_tensor(pwb[:, 1:, 3:W], pwa[:, 1:, 3:W], pwa[:, 1:, 1:W - 2], ADD))
                step(dve.tensor_tensor(pwa[:, 2:, 7:W], pwb[:, 2:, 7:W], pwb[:, 2:, 3:W - 4], ADD))
                step(dve.tensor_tensor(pwb[:, 3, 15:W], pwa[:, 3, 15:W], pwa[:, 3, 7:W - 8], ADD))
                for g, w in enumerate(WINDOWS):
                    win = (pwa if g % 2 == 0 else pwb)[:, g, :]
                    step(dve.tensor_tensor(win[:, PADW:2 * PADW], win[:, PADW:2 * PADW], winf[:, g, :], MUL))
                    ins = dve.scalar_tensor_tensor(u[:, g, PADW:W], win[:, PADW:W], 1.0 / w, u[:, g, PADW:W], MUL, SUB)
                    if g < NG - 1:
                        step(ins)
                ins.then_inc(sem("pooled"), 1)
                scaled(4), scaled(5), masked(6), masked(7)
                dve.wait_ge(sem("pooled"), L + 1)

                def bcn(d, a):
                    return bc[:, d, a * P:(a + 1) * P].rearrange("p (n c) -> p n c", c=GC)

                def diff(a, d):
                    b = bcn(d, a)
                    if a > 0:
                        _, f, _, n = use(L, "A0")
                        dve.wait_ge(f, n + 1)
                    step(dve.tensor_tensor(E[:, d], b.rearrange("p n c -> p c n").unsqueeze(3).broadcast_to([P, GC, NCT, GC]),
                                           b.unsqueeze(1).broadcast_to([P, GC, NCT, GC]), SUB))
                    e = scr[:, d * 2048:(d + 1) * 2048]
                    dve.tensor_scalar(e, e, 0.0, None, MIN).then_inc(sem("e_diff"), 1)

                def times_q(a, d):
                    dve.wait_ge(sem("e_k"), 4 * L + 2 * a + d + 1)
                    g = gq[:, d, a * P:(a + 1) * P].rearrange("p (n c) -> p n c", c=GC)
                    dve.tensor_tensor(E[:, d], E[:, d],
                                      g.rearrange("p n c -> p c n").unsqueeze(3).broadcast_to([P, GC, NCT, GC]), MUL)\
                       .then_inc(sem("e_ready"), 1)

                diff(0, 0), diff(0, 1)
                scaled(6), scaled(7)
                times_q(0, 0), times_q(0, 1)

                def scores_in_chunk(a):
                    bank, free = full(L, f"A{a}")
                    if 2 * L + a:
                        dve.wait_ge(sem("attn_used"), 2 * L + a)
                    A4 = bank[:, 0:GC * GH].rearrange("p (c h) -> p h c", h=GH)
                    for h in range(GH):
                        ins = dve.tensor_tensor(attn[:, h, :].rearrange("p (n c) -> p n c", c=GC),
                                                A4[:, h].unsqueeze(1).broadcast_to([P, NCT, GC]),
                                                maskg[:, :].rearrange("p (n c) -> p n c", c=GC), MUL)
                    ins.then_inc(free, 1)
                    freed(L, f"A{a}")
                    dve.engine_nop().then_inc(sem("attn_ready"), 1)

                def keys_by_chunk(a):
                    bank, free = full(L, f"kd{a}")
                    if a > 0:
                        _, f, _, n = use(L, "U3")
                        dve.wait_ge(f, n + 1)
                    dve.tensor_tensor(kdm[:, :, :], bank[:, 0:T].unsqueeze(1).broadcast_to([P, NCT, T]),
                                      chm[:, :].unsqueeze(2).broadcast_to([P, NCT, T]), MUL).then_inc(free, 1)
                    freed(L, f"kd{a}")
                    dve.engine_nop().then_inc(sem("kdm_ready"), 1)

                def states(a):
                    for i in range(4):
                        bank, free = full(L, f"U{4 * a + i}")
                        for j in range(2):
                            n = NCT * a + 2 * i + j
                            if n == NCH - 1:
                                continue
                            if n >= NCT:
                                dve.wait_ge(sem("state_used"), (NCH - 2) * L + n - NCT + 1)
                            for d in range(2):
                                up = bank[:, j * T + d * P:j * T + (d + 1) * P]
                                dst = S[:, n % NCT, d, :]
                                if n == 0:
                                    ins = dve.tensor_copy(dst, up)
                                else:
                                    ins = dve.scalar_tensor_tensor(dst, S[:, (n - 1) % NCT, d, :], al[:, d, n:n + 1], up, MUL, ADD)
                                if d == 0:
                                    step(ins)
                            if n % 2 == 1 or n == NCH - 2:
                                ins.then_inc(free, 1)
                                freed(L, f"U{n // 2}")
                            else:
                                ins.then_inc(sem("state_ready"), 1)
                                dve.wait_ge(sem("state_ready"), (NCH // 2 - 1) * L + n // 2 + 1)

                dve.wait_ge(sem("al_ready"), L + 1)
                scores_in_chunk(0)
                diff(1, 0), diff(1, 1)
                times_q(1, 0), times_q(1, 1)
                keys_by_chunk(0)
                scores_in_chunk(1)
                states(0)
                keys_by_chunk(1)
                states(1)
                for i in range(2):
                    inverse(2, (L, f"ssg{i}"))
                    go = PS[:, 6 + i, :]
                    step(dve.scalar_tensor_tensor(gtmp[:, :, :], two(go), pcol("g_gla_out", L), rr[:, :, :], MUL, MUL))
                    y = ys[:, KB + 2 * i:KB + 2 * i + 2, :]
                    dve.scalar_tensor_tensor(y, gtmp[:, :, :], 0.5, y, MUL, MUL).then_inc(sem("yb_ready"), 1)
                    dve.wait_ge(sem("yb_ready"), 2 * L + i + 1)
                for n in (0, 2, 1):
                    for m in range(4):
                        bank, free = full(L, f"b{n}{m}")
                        g = gates[:, n * KD + 2 * m:n * KD + 2 * m + 2, :]
                        dst = merged[:, 2 * m:2 * m + 2, :]
                        if n == 0:
                            dve.scalar_tensor_tensor(dst, g, 1.0, two(bank), ADD, MUL).then_inc(free, 1)
                        else:
                            dve.scalar_tensor_tensor(g, g, 1.0, two(bank), ADD, MUL).then_inc(free, 1)
                            freed(L, f"b{n}{m}")
                            ins = dve.tensor_tensor(dst, dst, g, ADD)
                            if n == 2:
                                step(ins)
                            else:
                                ins.then_inc(sem("merged"), 1)
                for m in range(4):
                    bank, free = full(L, f"w{m}")
                    x = xT[:, 2 * m:2 * m + 2, :]
                    dve.scalar_tensor_tensor(x, two(bank), 0.5, x, MUL, ADD).then_inc(free, 1)
                norm_x(L, "ssf", "g_ffn")

            def hidden(tag, uo, t, N, first=False):
                dve.wait_ge(sem(f"sil_ready_{tag}"), FT * uo + t + 1)
                if not first:
                    g = [i for i, (a, n) in enumerate(GROUPS) if a <= t < a + n][0]
                    dve.wait_ge(sem(f"down_done_{tag}"), len(GROUPS) * uo + g + 1 - len(GROUPS))
                dve.tensor_tensor(hid[:, t, 0:N], sil[:, t % 4, 0:N], PS[:, t % GU[tag], N:2 * N], MUL)\
                   .then_inc(sem(f"hid_ready_{tag}"), 1)

            mixer(0)
            for t in range(FT):
                hidden("d", 0, t, T, first=True)
            with dve.Fori(1, NDENSE) as i:
                for t in range(FT):
                    hidden("d", i, t, T)
            dve.wait_ge(sem("down_done_d"), len(GROUPS) * NDENSE)
            for c in range(4):
                x = xT[:, 2 * c:2 * c + 2, :]
                dve.tensor_tensor(x, x, two(PS[:, 4 + c, :]), ADD).then_inc(sem("x_dense"), 1)
            mixer(1)

            dve.wait_ge(sem("logits_full"), 1)
            step(dve.tensor_copy(lg[:, :, :], PS[:, 0, 0:TT * NE].rearrange("p (a e) -> p a e", a=TT)))
            for a in range(TT):
                step(dve.max(rt8[:, a, :], lg[:, a, :]))
                step(dve.max_index(ri8[:, a, :], rt8[:, a, :], lg[:, a, :]))
            step(dve.tensor_copy(rf8[:, :, :], ri8[:, :, :]))
            dve.tensor_tensor(rsm[:, 0:2], rt8[:, :, 1], rt8[:, :, 0], SUB).then_inc(sem("logit_gap"), 1)
            for a in range(TT):
                for j in range(2):
                    step(dve.tensor_scalar(m12[:, a, j, :], iot8[:, :], rf8[:, a, j:j + 1], None, ALU.is_equal))
            dve.tensor_tensor(msel[:, :, :], m12[:, :, 0, :], m12[:, :, 1, :], ADD).then_inc(sem("msel_ready"), 1)
            dve.wait_ge(sem("msel_ready"), 1)
            dve.wait_ge(sem("top_exp"), 1)
            step(dve.tensor_scalar(rsm[:, 4:6], rsm[:, 2:4], 1.0, None, ADD))
            step(dve.reciprocal(rsm[:, 4:6], rsm[:, 4:6]))
            step(dve.tensor_tensor(rsm[:, 6:8], rsm[:, 2:4], rsm[:, 4:6], MUL))
            for a in range(TT):
                step(dve.tensor_scalar(wt[:, a, :], m12[:, a, 1, :], rsm[:, 6 + a:7 + a], None, MUL))
                step(dve.scalar_tensor_tensor(wt[:, a, :], m12[:, a, 0, :], rsm[:, 4 + a:5 + a], wt[:, a, :], MUL, ADD))
            for c in range(4):
                dve.wait_ge(sem("htok_full"), c + 1)
                dve.tensor_copy(htok[:, c // 2, (c % 2) * 512:(c % 2 + 1) * 512], PS[:, 4 + c, :]).then_inc(sem("htok_ready"), 1)
            dve.wait_ge(sem("rank_full"), 1)
            rank = PS[:, 1, 0:TT * NE].rearrange("p (a e) -> p a e", a=TT)
            step(dve.scalar_tensor_tensor(pos[:, :, :], rank, BIG, msel[:, :, :], ADD, MUL))
            step(dve.tensor_scalar(pos[:, :, :], pos[:, :, :], BIG, None, SUB))
            step(dve.tensor_reduce(rsm[:, 8:9], PS[:, 1, TT * NE:(TT + 1) * NE], AX.X, MAX))
            step(dve.tensor_scalar(rsm[:, 9:10], rsm[:, 8:9], float(CAP), 1.0, ALU.is_gt, ADD))
            for r in range(2, PASSES):
                step(dve.scalar_tensor_tensor(rsm[:, 9:10], rsm[:, 8:9], float(r * CAP), rsm[:, 9:10], ALU.is_gt, ADD))
            dve.tensor_copy(npi[:, :], rsm[:, 9:10]).then_inc(sem("passes_known"), 1)

            def tokens(n, first=False):
                dve.wait_ge(sem("gath_full1"), n + 1)
                if not first:
                    dve.wait_ge(sem("gu_full_e0"), tiles_in_bank(2)[0] * n)
                dve.tensor_copy(hTe[:, 4:8, :], PS[:, 5, 0:4 * CAP].rearrange("p (k c) -> p k c", k=4))\
                   .then_inc(sem("hTe_dve"), 1)

            def rows_out(n):
                dve.wait_ge(sem("yt_full1"), n + 1)
                if not (isinstance(n, int) and n == 0):
                    dve.wait_ge(sem("scat_full"), 4 * n)
                dve.tensor_copy(ye[:, 512:1024], PS[0:CAP, 7, :]).then_inc(sem("ye_dve"), 1)

            def added(n):
                for c in range(4):
                    dve.wait_ge(sem("scat_full"), 4 * n + c + 1)
                    x = xT[:, 2 * c:2 * c + 2, :]
                    dve.tensor_tensor(x, x, two(PS[:, 6 + c % 2, :]), ADD).then_inc(sem("x_added"), 1)
                dve.wait_ge(sem("x_added"), 4 * n + 4)

            def expert(n, after=False, first=False, ahead=True):
                for t in range(FT):
                    hidden("e", n, t, CAP, first)
                    if t == 2 and after:
                        rows_out(n - 1)
                    if t == 5 and after:
                        added(n - 1)
                if ahead:
                    tokens(n + 1)

            def one_pass(r):
                n, start = r * NE, isinstance(r, int)
                for a in range(TT):
                    step.plain(dve.tensor_tensor(psel[:, a], slots[:, :].unsqueeze(1).broadcast_to([P, NE, CAP]),
                                                 pos[:, a, :].unsqueeze(2).broadcast_to([P, NE, CAP]), ALU.is_equal),
                               sem("psel_step"), 2 * r + a + 1)
                    dve.tensor_tensor(wsel[:, a], psel[:, a], wt[:, a, :].unsqueeze(2).broadcast_to([P, NE, CAP]), MUL)\
                       .then_inc(sem("sel_ready"), 1)
                dve.tensor_scalar(pos[:, :, :], pos[:, :, :], float(CAP), None, SUB).then_inc(sem("pos_step"), 1)
                dve.wait_ge(sem("pos_step"), r + 1)
                tokens(n, first=start)
                expert(n, first=start)
                with dve.Fori(1, NE - 1) as e:
                    expert(n + e, after=True)
                expert(n + NE - 1, after=True, ahead=False)
                rows_out(n + NE - 1)
                added(n + NE - 1)

            one_pass(0)
            dve.wait_ge(sem("passes_known"), 1)
            npass = dve.value_load(npi[0:1, 0:1], min_val=1, max_val=PASSES)
            with dve.If(npass > 1):
                with dve.Fori(1, npass) as r:
                    one_pass(r)


class Chain:

    def __init__(self, eng, sem):
        self.eng, self.sem, self.n = eng, sem, 0

    def __call__(self, ins):
        ins.then_inc(self.sem, 1)
        self.n += 1
        self.wait()

    def wait(self):
        self.eng.wait_ge(self.sem, self.n)

    def plain(self, ins, sem, value):
        ins.then_inc(sem, 1)
        self.eng.wait_ge(sem, value)


_INS = ["x", "positions", "g_mix", "w_in", "g_cq", "w_uq", "g_ckv", "w_ukv", "g_qk_q", "g_qk_k", "w_gla_gate_up",
        "b_gla_gate", "g_gla_out", "w_pool", "pool_scale", "w_branch", "w_out", "g_ffn", "w_ffn_gate", "w_ffn_up",
        "w_ffn_down", "w_router", "w_exp_gate", "w_exp_up", "w_exp_down"]


def kernel(**inputs):
    import numpy as _np
    import concourse.bacc as _bacc
    from concourse import mybir as _mybir
    from concourse.bass_utils import run_bass_kernel_spmd as _run

    nc = _bacc.Bacc("TRN2", target_bir_lowering=False, num_devices=1)
    arrays, aps = {}, {}
    for name in _INS:
        a = _np.ascontiguousarray(inputs[name])
        arrays[f"in_{name}_dram"] = a
        aps[name] = nc.dram_tensor(f"in_{name}_dram", a.shape, _mybir.dt.from_np(a.dtype), kind="ExternalInput").ap()
    out = nc.dram_tensor("out_dram", (1, T, D), _mybir.dt.float32, kind="ExternalOutput").ap()
    hybrid_trunk(nc, aps, out)
    r = _run(nc, [arrays], core_ids=[0])
    return r.results[0]["out_dram"]
```

```python
import concourse.bass as bass
from concourse import mybir
from contextlib import ExitStack
import numpy as np

D, T, DEPTH, P = 1024, 256, 2, 128
KD = D // P
TT = T // P
H, NOPE, ROPE, DV = 8, 64, 32, 64
QK = NOPE + ROPE
HALF = ROPE // 2
RANK = D // 4
KR = RANK // P
GH, GDK, GDV, GRANK, GC = 4, 64, 128, 16, 16
TAU = 16.0
NCH = T // GC
NCT = P // GC
WINDOWS = (2, 4, 8, 16)
NG = len(WINDOWS)
NBR, BW = 3, 512
KB = BW // P
DFF, NE, DE = 2816, 8, 1408
EPS = 1e-6
ROPE_BASE = 10000.0
BIG = 1024.0
NEG = -1e30

C_Q, C_KV, C_KR = 0, RANK, 2 * RANK
C_GQ = C_KR + ROPE
C_GK = C_GQ + GH * GDK
C_GV = C_GK + GH * GDK
C_LR = C_GV + GH * GDV
C_OG = C_LR + GRANK
C_U = C_OG + GH * GDV
C_G = C_U + NG * P
D_IN = C_G + NBR * D

UF = DE
FT = UF // P
GROUPS = [(0, 3), (3, 3), (6, 3), (9, 2)]
UNIT_LOADS = ["G0", "U0", "G1", "U1", "D0", "G2", "U2", "D1", "G3", "U3", "D2", "D3"]
NDENSE = DFF // UF
CAP = 96
PASSES = -(-T // CAP)

HALVES = 2 * len(UNIT_LOADS)
NSPLIT = 3
PERH = HALVES // NSPLIT
HALF_OF = {f"{c}{g}": 2 * UNIT_LOADS.index(f"{c}{g}") for c in "GUD" for g in range(len(GROUPS))}
DENSE_AFTER = {HALF_OF[f"U{g}"] + 1: [("gu", g)] for g in range(4)}
EXPERT_AFTER = {3: [("gu", 0), ("scatter", 0)], 5: [("tr", 0)], 7: [("gu", 1)], 11: [("tr", 1)], 13: [("gu", 2)],
                17: [("tr", 2)], 19: [("gu", 3), ("gather", 0)], 20: [("tr", 3)]}
DB = 4
PASS_USES = 42


def scatter_use(r, e):
    return PASS_USES * r + (5 * e + 1 if not (isinstance(e, int) and e == NE) else PASS_USES - 2)


def turn_use(r, e, g, last=False):
    base = PASS_USES * r + 5 * e + 3
    return (g % 2, base + (g // 2 if g < 3 else (1 if last else 2)))


def gather_use(r, e, c):
    if isinstance(e, int) and e < 0:
        return (1 - c, PASS_USES * r + 2)
    return (1 - c, PASS_USES * r + 5 * e + 3 + 1 + c)


SLOT, NSLOT = 3072, 4
GB = 384
MB = 256
PIECES = 4

PARAMS = [("g_mix", DEPTH * KD), ("g_ffn", DEPTH * KD), ("g_cq", DEPTH * KR), ("g_ckv", DEPTH * KR),
          ("b_gla_gate", DEPTH * 2), ("g_gla_out", DEPTH), ("pool_scale", DEPTH * NG),
          ("g_qk_q", DEPTH), ("g_qk_k", DEPTH)]
PCOL, NPAR = {}, 0
for _n, _k in PARAMS:
    PCOL[_n] = NPAR
    NPAR += _k

LOADS = (["cq", "ckv", "gq", "gk", "uq", "va", "ukv", "vb", "oga", "ogb", "ua", "ub"]
         + [f"g{i}" for i in range(6)] + ["pool"] + [f"g{i}" for i in range(6, 12)]
         + ["br00", "br01", "br20", "br21", "br10", "br11"] + ["out0", "out1", "out2", "out3"])
NL = len(LOADS)
LAST_USE = {"uq": "q3", "ukv": "vm1", "pool": "pl1",
            **{f"br{n}{hf}": f"b{n}{2 * hf + 1}" for n in range(3) for hf in range(2)},
            **{f"out{m}": f"w{m}" for m in range(4)}}
W_IN = {"cq": (C_Q, 256), "ckv": (C_KV, 288), "gq": (C_GQ, 256), "gk": (C_GK, 256),
        "va": (C_GV, 256), "vb": (C_GV + 256, 272), "oga": (C_OG, 256), "ogb": (C_OG + 256, 256),
        "ua": (C_U, 256), "ub": (C_U + 256, 256), **{f"g{b}": (C_G + b * MB, MB) for b in range(12)}}
W_IN_NO = {name: i for i, name in enumerate(W_IN)}
LAST_OF = {"ckv": "kr", "vb": "lr"}
assert len(UNIT_LOADS) % NSLOT == 0


def filled(segment, s):
    mixer, per = len(range(s, NL, NSLOT)), len(UNIT_LOADS) // NSLOT
    return [0, mixer, mixer + NDENSE * per, 2 * mixer + NDENSE * per][segment]


NB = 6
PRE_USES = ["x0", "x1", "x2", "x3", "par", "inv"]
MIX_USES = (["ssm", "cq", "ckv", "kr", "gq", "sslat", "gk"] + [f"q{i}" for i in range(4)] + ["va"]
            + [f"k{i}" for i in range(4)] + ["vm0", "vm1", "vb", "lr", "oga", "ssq"]
            + ["z", "ogb"] + [f"ssk{i}" for i in range(4)]
            + ["ua"] + [f"rq{i}" for i in range(4)] + ["ub"] + [f"rk{i}" for i in range(4)] + ["g0", "s0", "s1", "g1", "pt0", "pt1", "s2", "s3", "g2", "o0", "pt2", "pt3", "s4", "s5",
               "g3", "o1", "pt4", "pt5", "s6", "s7", "g4", "o2", "pt6", "pt7", "A0", "g5", "kd0", "pl0", "pl1", "g6"]
            + [f"U{i}" for i in range(4)] + ["o3", "A1", "g7", "kd1", "g8"]
            + [f"U{i}" for i in range(4, 8)] + ["g9", "g10", "ssg0", "ssg1", "g11"]
            + [f"b{n}{m}" for n in (0, 2, 1) for m in range(4)] + [f"w{m}" for m in range(4)] + ["ssf"])
USES = [(-1, u) for u in PRE_USES]
USES += [(0, u) for u in MIX_USES] + [(1, u) for u in MIX_USES]
USE = {u: i for i, u in enumerate(USES)}
MIX_END = [len(PRE_USES) + len(MIX_USES), len(PRE_USES) + 2 * len(MIX_USES)]


def hybrid_trunk(nc, A, out):
    F32, F32R, I32, U32, BF16 = (mybir.dt.float32, mybir.dt.float32r, mybir.dt.int32, mybir.dt.uint32,
                                 mybir.dt.bfloat16)
    ALU, ACT, AX = mybir.AluOpType, mybir.ActivationFunctionType, mybir.AxisListType
    ADD, SUB, MUL, MAX, MIN = ALU.add, ALU.subtract, ALU.mult, ALU.max, ALU.min

    ctx = ExitStack()
    with ctx:
        def sb(name, shape, dt=F32):
            return ctx.enter_context(nc.sbuf_tensor(name, shape, dt))

        def over(*wanted):
            with ExitStack() as tmp:
                return [tmp.enter_context(nc.sbuf_tensor(name, shape, dt)) for name, shape, dt in wanted]

        sems = {}

        def sem(name):
            if name not in sems:
                sems[name] = ctx.enter_context(nc.semaphore(name))
            return sems[name]

        ring = sb("ring", [P, NSLOT, SLOT])
        xT = sb("xT", [P, KD, T])
        h_hi = sb("h_hi", [P, KD, T], F32R)
        h_lo = sb("h_lo", [P, KD, T], F32R)
        m_hi = sb("m_hi", [P, PIECES, 576], F32R)
        m_lo = sb("m_lo", [P, PIECES, 576], F32R)
        rt = sb("rt", [P, 2, T])
        rr = sb("rr", [P, 2, T])
        big = sb("big", [P, 24 * T])
        gates = big[:, :].rearrange("p (n t) -> p n t", t=T)
        lat, latn, sq, sk = gates[:, 0:4], gates[:, 4:8], gates[:, 8:16], gates[:, 16:24]
        hT = gates[:, 0:KD]
        xin = big[:, 0:TT * D].rearrange("p (a d) -> p a d", a=TT)
        w_hi, w_lo = over(("w_hi", [P, NSPLIT, SLOT // 2], F32R), ("w_lo", [P, NSPLIT, SLOT // 2], F32R))
        gq = sb("gq", [P, 2, T])
        gk = sb("gk", [P, 2, T])
        gvt = sb("gvt", [P, TT, GH * GDV])
        th = sb("th", [P, 2, T])
        vt = sb("vt", [P, TT, H * DV])
        ys = sb("ys", [P, NBR * KB, T])
        Pr = sb("Pr", [P, 3, 3 * P])
        PT = sb("PT", [P, 2, 3 * P])
        kdec = sb("kdec", [P, 2, T])
        bc = sb("bc", [P, 2, T])
        attn = sb("attn", [P, GH, P])
        rows3 = sb("rows3", [P, 3, T])
        krope = rows3[:, 2, :]
        glr = rows3[0:GRANK, 2, :]
        PADW = max(WINDOWS)
        u = sb("u", [P, NG, PADW + T])
        hid_hi, = over(("hid_hi", [P, FT, T], F32R))
        hTe_hi, hTe_lo, hdT_hi, hdT_lo = over(*((n, [P, k, CAP], F32R) for n, k in (
            ("hTe_hi", KD), ("hTe_lo", KD), ("hdT_hi", FT), ("hdT_lo", FT))))
        scr = sb("scr", [P, 4096])
        E = scr[:, :].rearrange("p (d c n j) -> p d c n j", d=2, n=NCT, c=GC)
        pwa = scr[:, 0:NG * (PADW + T)].rearrange("p (g t) -> p g t", g=NG)
        pwb = scr[:, 2048:2048 + NG * (PADW + T)].rearrange("p (g t) -> p g t", g=NG)
        merged = scr[:, 0:KD * T].rearrange("p (k t) -> p k t", k=KD)
        ztmp = scr[:, 2048:4096].rearrange("p (k t) -> p k t", k=8)
        hid_lo, = over(("hid_lo", [P, FT, T], F32R))
        qk = sb("qk", [P, 4096])
        q = qk[0:QK, 0:2048].rearrange("p (h t) -> p h t", h=H)
        k = qk[0:QK, 2048:4096].rearrange("p (h t) -> p h t", h=H)
        gsq = qk[:, 0:4 * T].rearrange("p (a b t) -> p a b t", a=2, b=2)
        kdm = qk[:, 0:2048].rearrange("p (n f) -> p n f", n=NCT)
        S = qk[:, 2048:4096].rearrange("p (n d v) -> p n d v", n=NCT, d=2)
        rqs = sb("rqs", [P, TT * H])
        small = sb("small", [P, 64])
        qdm = sb("qdm", [P, 2, 2, T])
        al = sb("al", [P, 2, NCH])
        ident = sb("ident", [P, P])
        ones = sb("ones", [P, P])
        zb = sb("zb", [P, P], BF16)
        maskc = sb("maskc", [P, 3 * P])
        maskg = sb("maskg", [P, P])
        chm = sb("chm", [P, NCT])
        keep = sb("keep", [P, T])
        winf = sb("winf", [P, NG, PADW])
        selh = sb("selh", [P, 2])
        R = sb("R", [QK, QK])
        cs = rows3[:, 0:2, :]
        par = sb("par", [P, NPAR])
        eps = sb("eps", [P, 2])
        one1 = sb("one1", [1, 1])
        invr = sb("invr", [1, QK])
        invc = sb("invc", [QK, 1])
        ang = scr[0:QK, T:5 * T].rearrange("p (a t) -> p a t", a=4)
        cnt = scr[:, 0:PADW].bitcast(I32)
        sloti = scr[:, PADW:PADW + CAP].bitcast(I32)
        eb = attn[:, :, :].rearrange("p h i -> p (h i)").rearrange("p (d t) -> p d t", d=2)
        ek = PT[:, :, :].rearrange("p a j -> p (a j)")[:, 0:2 * T].rearrange("p (d t) -> p d t", d=2)
        rq16 = small[:, 0:16]
        rk16 = small[:, 32:48]
        mx = small[:, 16:20].rearrange("p (a b) -> p a b", a=2)
        nbs = small[:, 20:24].rearrange("p (a b) -> p a b", a=2)
        sums = small[:, 24:28].rearrange("p (a b) -> p a b", a=2)
        angk = ang[:, 3, :]
        rtmp = th[0:QK, :, :]
        gtmp = th
        sil = big[:, 4096:4096 + 3 * T].rearrange("p (f t) -> p f t", f=3)
        hidf = big[:, 5120:5120 + 3 * T].rearrange("p (f t) -> p f t", f=3)
        htok = qk[:, 0:TT * D].rearrange("p (a d) -> p a d", a=TT)
        selT = qk[0:CAP, 2048:2048 + NE * T].rearrange("p (e t) -> p e t", e=NE)
        psel = big[:, 0:TT * NE * CAP].rearrange("p (a e c) -> p a e c", a=TT, e=NE)
        wsel = big[:, 1536:1536 + TT * NE * CAP].rearrange("p (a e c) -> p a e c", a=TT, e=NE)
        ye = big[0:CAP, 3072:3072 + D]
        sile = big[0:CAP, 4096:4096 + 2 * GB].rearrange("p (f t) -> p f t", f=2)
        hide = big[0:CAP, 5120:5120 + 2 * GB].rearrange("p (f t) -> p f t", f=2)
        slots = sb("slots", [P, CAP])
        us = u[:, :, :].rearrange("p g t -> p (g t)")
        tri = us[:, 0:P]
        lg, rt8, rf8, msel, wt, pos = (us[:, P + i * TT * NE:P + (i + 1) * TT * NE].rearrange("p (a e) -> p a e", a=TT)
                                       for i in range(6))
        ri8 = us[:, 2 * P:2 * P + TT * NE].bitcast(U32).rearrange("p (a e) -> p a e", a=TT)
        m12 = us[:, 2 * P + 32:2 * P + 64].rearrange("p (a j e) -> p a j e", a=TT, j=2)
        iot8 = sb("iot8", [P, NE])
        wgu = rows3[0:GRANK, 0:DEPTH, :]
        posi = scr[0:QK, 5 * T:6 * T].bitcast(I32)
        
        wr = sb("wr", [P, KD, NE])
        rsm = sb("rsm", [P, 16])
        npi = sb("npi", [P, 1], I32)
        yout = big[:, 0:TT * D].rearrange("p (a d) -> p a d", a=TT)

        PS = ctx.enter_context(nc.psum_tensor("PS", [P, 8, 512], F32))

        def use(L, name):
            i = USE[(L, name)]
            return PS[:, i % NB, :], sem(f"bank_full{i % NB}"), sem(f"bank_free{i % NB}"), i // NB

        def slot_of(L, name):
            i = LOADS.index(name)
            return i % NSLOT, filled(2 * L, i % NSLOT) + i // NSLOT + 1


        def half_buffer(u, j):
            return j % NSPLIT, PERH * u + j // NSPLIT + 1

        def wait_hi(eng, u, j):
            b, n = half_buffer(u, j)
            eng.wait_ge(sem(f"hi_ready{b}"), n)

        def wait_lo(eng, u, j):
            b, n = half_buffer(u, j)
            eng.wait_ge(sem(f"lo_ready{b}"), n)

        def wait_used(eng, u, j):
            b, n = half_buffer(u, j)
            eng.wait_ge(sem(f"split_used{b}"), n)

        def half_words(j):
            gn = GROUPS[int(UNIT_LOADS[j // 2][1])][1]
            n = gn * D // 2
            return n, (j % 2) * n

        def round_hi(act, u, j, kind, n):
            b, uses = half_buffer(u, j)
            i = j // 2
            act.wait_ge(sem(f"slot_full{i % NSLOT}"), 16 * (PER * n + filled(2 * kind + 1, i % NSLOT) + i // NSLOT + 1))
            if not isinstance(uses, int) or uses > 1:
                act.wait_ge(sem(f"split_used{b}"), uses - 1)
            words, w0 = half_words(j)
            act.activation(w_hi[:, b, 0:words], ring[:, i % NSLOT, w0:w0 + words], ACT.Copy)\
               .then_inc(sem(f"hi_ready{b}"), 1)

        def rest_lo(dve, u, j):
            b, _ = half_buffer(u, j)
            wait_hi(dve, u, j)
            words, w0 = half_words(j)
            dve.tensor_tensor(w_lo[:, b, 0:words], ring[:, (j // 2) % NSLOT, w0:w0 + words],
                              w_hi[:, b, 0:words].bitcast(F32), SUB).then_inc(sem(f"lo_ready{b}"), 1)

        def wait_aux_full(eng, b, n):
            eng.wait_ge(sem(f"aux_full{b}"), n + 1)

        def wait_aux_free(eng, b, n):
            if not isinstance(n, int) or n > 0:
                eng.wait_ge(sem(f"aux_free{b}"), n)
        PER = len(UNIT_LOADS) // NSLOT

        def piece_done(eng, L, name, p):
            x = len(W_IN) * L + W_IN_NO[name] - 1
            if x < 0:
                return
            if p < PIECES - 1:
                eng.wait_ge(sem("piece_used"), (PIECES - 1) * x + p + 1)
            else:
                prev = list(W_IN)[x % len(W_IN)]
                _, full, _, n = use(x // len(W_IN), LAST_OF.get(prev, prev))
                eng.wait_ge(full, n + 1)

        def piece_no(L, name, p):
            return PIECES * (len(W_IN) * L + W_IN_NO[name]) + p

        def piece_of(L, name, p):
            n = W_IN[name][1] * KD // PIECES
            s, _ = slot_of(L, name)
            return ring[:, s, p * n:(p + 1) * n], m_hi[:, p, 0:n], m_lo[:, p, 0:n]

        block = ctx.enter_context(nc.Block())

        @block.sync
        def _(sp):
            rows = ring[:, NSLOT - 1, 0:P]
            sp.dma_start(xin, A["x"].rearrange("b (a p) d -> p (b a) d", p=P)).then_inc(sem("x_in"), 16)

            sp.wait_ge(sem("rows_clear"), 1)
            for name, n in PARAMS:
                r0 = PCOL[name]
                wide = QK if name in ("g_qk_q", "g_qk_k") else P
                src = A[name] if wide == QK else A[name].rearrange("l (k p) -> (l k) p", p=P)
                sp.dma_start(rows[r0:r0 + n, 0:wide], src).then_inc(sem("params_in"), 16)
            sp.dma_start(posi[NOPE:QK, :], A["positions"].broadcast_to([ROPE, T])).then_inc(sem("pos_in"), 16)
            sp.dma_start(wgu[:, :, :], A["w_gla_gate_up"].rearrange("l r c -> r l c")).then_inc(sem("gu_in"), 16)
            sp.dma_start(wr[:, :, :], A["w_router"][0].rearrange("(k p) e -> p k e", p=P)).then_inc(sem("router_in"), 16)

            w_in, w_uq, w_ukv = A["w_in"], A["w_uq"], A["w_ukv"]

            def kp(ap):
                return ap.rearrange("(k p) c -> p k c", p=P)

            def mixer_read(L, name):
                if name in W_IN:
                    sp.wait_ge(sem("m_lo_ready"), piece_no(L, name, PIECES - 1) + 1)
                    return
                _, full, _, n = use(L, LAST_USE[name])
                sp.wait_ge(full, n + 1)

            def unit_read(u, i):
                wait_lo(sp, u, 2 * i + 1)

            def mixer_load(L, name):
                s, _ = slot_of(L, name)
                i = LOADS.index(name)
                if i == NSLOT - 1 and L == 0:
                    sp.wait_ge(use(-1, "par")[1], 1)
                if i >= NSLOT:
                    mixer_read(L, LOADS[i - NSLOT])
                elif L > 0:
                    unit_read(NDENSE - 1, len(UNIT_LOADS) - NSLOT + i)

                def put(src, cols, first=0):
                    kk = src.shape[0] // P
                    dst = ring[:, s, first:first + kk * cols].rearrange("p (k c) -> p k c", k=kk)
                    sp.dma_start(dst, kp(src)).then_inc(sem(f"slot_full{s}"), 16)

                if name in W_IN:
                    c0, cn = W_IN[name]
                    put(w_in[L, :, c0:c0 + cn], cn)
                elif name == "uq":
                    put(w_uq[L], H * QK)
                elif name == "ukv":
                    put(w_ukv[L], H * (NOPE + DV))
                elif name == "pool":
                    dst = ring[:, s, 0:NG * P].rearrange("p (g c) -> p g c", g=NG)
                    sp.dma_start(dst, A["w_pool"][L].rearrange("g p c -> p g c")).then_inc(sem(f"slot_full{s}"), 16)
                elif name[:2] == "br":
                    n, hf = int(name[2]), int(name[3])
                    put(A["w_branch"][L, n, :, hf * 512:(hf + 1) * 512], 512)
                else:
                    m = int(name[3])
                    put(A["w_out"][L, :, m * MB:(m + 1) * MB], MB)

            def unit_loads(kind, wg, wu, wd, x, uo):
                u = kind * NDENSE + uo
                wg, wu, wd = wg[x], wu[x], wd[x]
                for i, name in enumerate(UNIT_LOADS):
                    s = i % NSLOT
                    g0, gn = GROUPS[int(name[1])]
                    if i >= NSLOT:
                        unit_read(u, i - NSLOT)
                    elif isinstance(uo, int) and uo == 0:
                        mixer_read(kind, LOADS[max(x for x in range(NL) if x % NSLOT == i)])
                    else:
                        unit_read(u - 1, len(UNIT_LOADS) - NSLOT + i)
                    if name[0] == "D":
                        src = wd[g0 * P:(g0 + gn) * P, :].rearrange("(k p) c -> p k c", p=P)
                        dst = ring[:, s, 0:gn * D].rearrange("p (k c) -> p k c", k=gn)
                    else:
                        w = wg if name[0] == "G" else wu
                        src = w[:, g0 * P:(g0 + gn) * P].rearrange("(k p) c -> p k c", p=P)
                        dst = ring[:, s, 0:KD * gn * P].rearrange("p (k c) -> p k c", k=KD)
                    sp.dma_start(dst, src).then_inc(sem(f"slot_full{s}"), 16)

            for name in LOADS:
                mixer_load(0, name)
            fg = A["w_ffn_gate"][0].rearrange("k (u c) -> u k c", c=UF)
            fu = A["w_ffn_up"][0].rearrange("k (u c) -> u k c", c=UF)
            fd = A["w_ffn_down"][0].rearrange("(u k) c -> u k c", k=UF)
            unit_loads(0, fg, fu, fd, 0, 0)
            with sp.Fori(1, NDENSE) as i:
                unit_loads(0, fg, fu, fd, i, i)
            for name in LOADS:
                mixer_load(1, name)
            eg, eu, ed = A["w_exp_gate"][0], A["w_exp_up"][0], A["w_exp_down"][0]
            unit_loads(1, eg, eu, ed, 0, 0)
            with sp.Fori(1, NE) as e:
                unit_loads(1, eg, eu, ed, e, e)
            sp.wait_ge(sem("passes_known"), 1)
            npass = sp.value_load(npi[0:1, 0:1], min_val=1, max_val=PASSES)
            with sp.If(npass > 1):
                with sp.Fori(1, npass) as r:
                    with sp.Fori(0, NE) as e:
                        unit_loads(1, eg, eu, ed, e, r * NE + e)
            sp.wait_ge(sem("y_out"), 4)
            sp.dma_start(out.rearrange("b (a p) d -> p (b a) d", p=P), yout).then_inc(sem("stored"), 16)
            sp.wait_ge(sem("stored"), 16)

        @block.tensor
        def _(pe):
            def begin(L, name):
                bank, full, free, n = use(L, name)
                if n >= 1:
                    pe.wait_ge(free, n)
                return bank, full

            def weights(L, name):
                s, r = slot_of(L, name)
                pe.wait_ge(sem(f"slot_full{s}"), 16 * r)
                return s

            def wslot(s, kk, cols):
                return ring[:, s, 0:kk * cols].rearrange("p (k c) -> p k c", k=kk)

            def evacuated(L, name):
                _, _, free, n = use(L, name)
                pe.wait_ge(free, n + 1)

            def project(dst, w, c0, m, rhs, kk=KD):
                for i in range(kk):
                    mm = pe.matmul(dst, w[:, i, c0:c0 + m], rhs(i), start=(i == 0), stop=(i == kk - 1))
                return mm

            def sumsq(L, name, layer):
                bank, full = begin(L, name)
                for i in range(4):
                    pe.wait_ge(sem("sq_act" if i % 2 == 0 else "sq_dve"), 2 * (2 * layer + (name == "ssf")) + i // 2 + 1)
                    for j in range(2):
                        kt = 2 * i + j
                        mm = pe.matmul(bank[:, 0:T], ones[:, :], sq[:, kt, :], start=(kt == 0), stop=(kt == KD - 1))
                mm.then_inc(full, 1)

            def by_pieces(L, name, groups):
                cols = W_IN[name][1]
                for p in range(PIECES):
                    pe.wait_ge(sem("m_lo_ready"), piece_no(L, name, p) + 1)
                    pe.wait_ge(sem("m_hi_ready"), piece_no(L, name, p) + 1)
                    _, hi, lo = piece_of(L, name, p)
                    hi, lo = (x.rearrange("p (k c) -> p k c", c=cols) for x in (hi, lo))
                    for full, dsts in groups:
                        for x, (dst, c0, m, a) in enumerate(dsts):
                            for k in range(KD // PIECES):
                                kt = p * KD // PIECES + k
                                if name == "cq":
                                    pe.wait_ge(sem("h_lo_ready"), KD // 2 * 2 * L + kt // 2 + 1)
                                w = slice(c0, c0 + m)
                                t = slice(0, T) if a is None else slice(a * P, (a + 1) * P)
                                whi, wlo, xhi, xlo = hi[:, k, w], lo[:, k, w], h_hi[:, kt, t], h_lo[:, kt, t]
                                for y, (ww, xx) in enumerate(((whi, xhi), (whi, xlo), (wlo, xhi))):
                                    l, r = (ww, xx) if a is None else (xx, ww)
                                    mm = pe.matmul(dst, l, r, start=(kt == 0 and x == 0 and y == 0),
                                                   stop=(kt == KD - 1 and y == 2), skip_group_check=True)
                        if p == PIECES - 1:
                            mm.then_inc(full, 1)
                    if p < PIECES - 1:
                        mm.then_inc(sem("piece_used"), 1)

            def pair(L, name):
                bank, full = begin(L, name)
                by_pieces(L, name, [(full, [(bank[:, j * T:(j + 1) * T], j * P, P, None) for j in range(2)])])

            def by_tokens(L, name):
                bank, full = begin(L, name)
                return (full, [(bank[:, a * 256:(a + 1) * 256], 0, 256, a) for a in range(TT)])

            pe.wait_ge(sem("ident_ready"), 1)
            pe.wait_ge(sem("x_in"), 16)
            for i in range(4):
                bank, full = begin(-1, f"x{i}")
                for j in range(2):
                    for a in range(TT):
                        mm = pe.transpose(bank[:, j * T + a * P:j * T + (a + 1) * P],
                                          xin[:, a, (2 * i + j) * P:(2 * i + j + 1) * P], ident[:, :])
                mm.then_inc(full, 1)
            pe.wait_ge(sem("consts"), 1)
            pe.wait_ge(sem("params_in"), 16 * len(PARAMS))
            bank, full = begin(-1, "par")
            pe.transpose(bank[:, 0:NPAR], ring[0:NPAR, NSLOT - 1, 0:P], ident[0:NPAR, 0:NPAR]).then_inc(full, 1)
            bank, full = begin(-1, "inv")
            pe.matmul(bank[0:QK, 0:1], invr[:, :], one1[:, :], start=True, stop=True).then_inc(full, 1)

            def mixer(L):
                sumsq(L, "ssm", L)
                pair(L, "cq")
                ckv, full = begin(L, "ckv")
                kr, kr_full = begin(L, "kr")
                by_pieces(L, "ckv", [(full, [(ckv[:, j * T:(j + 1) * T], j * P, P, None) for j in range(2)]),
                                     (kr_full, [(kr[0:QK, 0:T], 256 - NOPE, QK, None)])])
                pair(L, "gq")
                bank, full = begin(L, "sslat")
                evacuated(L, "ckv")
                for g in range(2):
                    for i in range(KR):
                        mm = pe.matmul(bank[:, g * T:(g + 1) * T], ones[:, :], sq[:, g * KR + i, :],
                                       start=(i == 0), stop=(i == KR - 1))
                mm.then_inc(full, 1)
                pair(L, "gk")
                s = weights(L, "uq")
                w = wslot(s, KR, H * QK)
                pe.wait_ge(sem("latn_ready"), 4 * L + KR)
                for i in range(4):
                    bank, full = begin(L, f"q{i}")
                    for j in range(2):
                        mm = project(bank[0:QK, j * T:(j + 1) * T], w, (2 * i + j) * QK, QK,
                                     lambda x: latn[:, x, :], KR)
                    mm.then_inc(full, 1)
                by_pieces(L, "va", [by_tokens(L, "va")])
                s = weights(L, "ukv")
                w = wslot(s, KR, H * (NOPE + DV))
                pe.wait_ge(sem("latn_ready"), 4 * L + 2 * KR)
                for i in range(4):
                    bank, full = begin(L, f"k{i}")
                    for j in range(2):
                        mm = project(bank[0:NOPE, j * T:(j + 1) * T], w, (2 * i + j) * (NOPE + DV), NOPE,
                                     lambda x: latn[:, KR + x, :], KR)
                    mm.then_inc(full, 1)
                wv = w.rearrange("p k (h c) -> p k h c", h=H)
                for a in range(TT):
                    bank, full = begin(L, f"vm{a}")
                    for i in range(KR):
                        mm = pe.matmul(bank[:, :], latn[:, KR + i, a * P:(a + 1) * P], wv[:, i, :, NOPE:NOPE + DV],
                                       start=(i == 0), stop=(i == KR - 1))
                    mm.then_inc(full, 1)
                vb = by_tokens(L, "vb")
                bank, full = begin(L, "lr")
                by_pieces(L, "vb", [vb, (full, [(bank[0:GRANK, 0:T], 256, GRANK, None)])])
                pair(L, "oga")
                bank, full = begin(L, "ssq")
                evacuated(L, "q3")
                evacuated(L, "k3")
                for c, src in enumerate((sq, sk)):
                    for a in range(TT):
                        for h in range(H):
                            x = c * TT * H + a * H + h
                            mm = pe.matmul(bank[:, x:x + 1], src[0:QK, h, a * P:(a + 1) * P], ones[0:QK, 0:1],
                                           start=True, stop=True)
                mm.then_inc(full, 1)
                bank, full = begin(L, "z")
                evacuated(L, "lr")
                pe.wait_ge(sem("gu_in"), 16)
                for d in range(2):
                    mm = pe.matmul(bank[:, d * T:(d + 1) * T], wgu[:, L, d * P:(d + 1) * P], glr[:, :],
                                   start=True, stop=True)
                mm.then_inc(full, 1)
                pair(L, "ogb")
                pe.wait_ge(sem("rk_ready"), L + 1)
                for i in range(4):
                    bank, full = begin(L, f"ssk{i}")
                    for j in range(2):
                        for a in range(TT):
                            x = a * H + 2 * i + j
                            mm = pe.matmul(bank[0:QK, j * T + a * P:j * T + (a + 1) * P], rk16[:, x:x + 1].broadcast_to([P, QK]),
                                           ident[:, :], start=True, stop=True)
                    mm.then_inc(full, 1)
                pair(L, "ua")
                for c, src in (("q", q), ("k", k)):
                    if c == "k":
                        pair(L, "ub")
                    for i in range(4):
                        bank, full = begin(L, f"r{c}{i}")
                        evacuated(L, f"ssk{i}" if c == "k" else f"q{i}")
                        pe.matmul(bank[0:QK, :], R[:, :], src[:, 2 * i:2 * i + 2, :], start=True, stop=True).then_inc(full, 1)

                def gate(i):
                    pair(L, f"g{i}")

                def scores(h):
                    bank, full = begin(L, f"s{h}")
                    pe.wait_ge(sem("q_ready"), 4 * L + h // 2 + 1)
                    pe.wait_ge(sem("k_ready"), 4 * L + h // 2 + 1)
                    pe.matmul(bank[:, 0:P], q[:, h, 0:P], k[:, h, 0:P], start=True, stop=True)
                    pe.matmul(bank[:, P:3 * P], q[:, h, P:T], k[:, h, :], start=True, stop=True).then_inc(full, 1)

                def turn(h):
                    bank, full = begin(L, f"pt{h}")
                    pe.wait_ge(sem("p_ready"), H * L + h + 1)
                    for j in range(3):
                        mm = pe.transpose(bank[:, j * P:(j + 1) * P], Pr[:, h % 3, j * P:(j + 1) * P], ident[:, :])
                    mm.then_inc(full, 1)

                def values(i):
                    bank, full = begin(L, f"o{i}")
                    for j in range(2):
                        h = 2 * i + j
                        evacuated(L, f"pt{h}")
                        o = bank[j * DV:(j + 1) * DV, 0:T]
                        pe.matmul(o, vt[:, 0, h * DV:(h + 1) * DV], PT[:, j, 0:T], start=True, stop=False)
                        mm = pe.matmul(o[:, P:T], vt[:, 1, h * DV:(h + 1) * DV], PT[:, j, T:3 * P], start=False, stop=True)
                    mm.then_inc(full, 1)

                def intra(a):
                    bank, full = begin(L, f"A{a}")
                    for d in range(2):
                        pe.wait_ge(sem("e_ready"), 4 * L + 2 * a + d + 1)
                        for c in range(GC):
                            mm = pe.matmul(bank[:, c * GH + 2 * d:c * GH + 2 * d + 2], E[:, d, c, :, :], selh[:, :],
                                           start=True, stop=True)
                    mm.then_inc(full, 1)

                def turn_k(a):
                    bank, full = begin(L, f"kd{a}")
                    pe.wait_ge(sem("dec_ready"), L + 1)
                    for d in range(2):
                        mm = pe.transpose(bank[:, d * P:(d + 1) * P], kdec[:, d, a * P:(a + 1) * P], ident[:, :])
                    mm.then_inc(full, 1)

                def go(h, lo, hi):
                    return PS[:, 6 + h // 2, (h % 2) * T + lo:(h % 2) * T + hi]

                def within(a):
                    pe.wait_ge(sem("attn_ready"), 2 * L + a + 1)
                    for h in range(GH):
                        mm = pe.matmul(go(h, a * P, (a + 1) * P), gvt[:, a, h * GDV:(h + 1) * GDV], attn[:, h, :],
                                       start=(a == 0 and h % 2 == 0), stop=False, skip_group_check=True)
                    mm.then_inc(sem("attn_used"), 1)

                def updates(a):
                    pe.wait_ge(sem("kdm_ready"), 2 * L + a + 1)
                    for i in range(4):
                        bank, full = begin(L, f"U{4 * a + i}")
                        for j in range(1 if 4 * a + i == 7 else 2):
                            n = 2 * i + j
                            for h in range(GH):
                                mm = pe.matmul(bank[(h % 2) * GDK:(h % 2 + 1) * GDK,
                                                    j * T + (h // 2) * P:j * T + (h // 2 + 1) * P],
                                               kdm[:, n, h * GDK:(h + 1) * GDK], gvt[:, a, h * GDV:(h + 1) * GDV],
                                               start=True, stop=True)
                        mm.then_inc(full, 1)

                def across(a):
                    pe.wait_ge(sem("qdm_ready"), L + 1)
                    for n in range(max(1, a * NCT), (a + 1) * NCT):
                        m = n - 1
                        if m % 2 == 1 or m == NCH - 2:
                            evacuated(L, f"U{m // 2}")
                        else:
                            pe.wait_ge(sem("state_ready"), (NCH // 2 - 1) * L + m // 2 + 1)
                        for h in range(GH):
                            mm = pe.matmul(go(h, n * GC, (n + 1) * GC), S[:, (n - 1) % NCT, h // 2, :],
                                           qdm[:, h % 2, h // 2, n * GC:(n + 1) * GC],
                                           start=False, stop=(n == NCH - 1), skip_group_check=True)
                        if n < NCH - 1:
                            mm.then_inc(sem("state_used"), 1)
                    if a == 1:
                        mm.then_inc(sem("go_full"), 1)

                gate(0)
                scores(0), scores(1)
                gate(1)
                turn(0), turn(1)
                scores(2), scores(3)
                gate(2)
                values(0)
                turn(2), turn(3)
                scores(4), scores(5)
                gate(3)
                values(1)
                turn(4), turn(5)
                scores(6), scores(7)
                gate(4)
                values(2)
                turn(6), turn(7)
                intra(0)
                gate(5)
                within(0)
                turn_k(0)
                s = weights(L, "pool")
                pe.wait_ge(sem("pooled"), NG * (L + 1))
                for i in range(2):
                    bank, full = begin(L, f"pl{i}")
                    for j in range(2):
                        g = 2 * i + j
                        mm = pe.matmul(bank[:, j * T:(j + 1) * T], ring[:, s, g * P:(g + 1) * P], u[:, g, PADW:PADW + T],
                                       start=True, stop=True)
                    mm.then_inc(full, 1)
                gate(6)
                updates(0)
                values(3)
                intra(1)
                gate(7)
                within(1)
                turn_k(1)
                gate(8)
                across(0)
                updates(1)
                gate(9)
                across(1)
                gate(10)
                for i in range(2):
                    bank, full = begin(L, f"ssg{i}")
                    pe.wait_ge(sem("gsq_ready"), 2 * L + i + 1)
                    pe.matmul(bank[:, :], ones[:, :], gsq[:, i, :, :], start=True, stop=True).then_inc(full, 1)
                gate(11)
                for n in (0, 2, 1):
                    if n == 0:
                        evacuated(L, "o3")
                    elif n == 2:
                        evacuated(L, "pl1")
                    else:
                        pe.wait_ge(sem("yb_ready"), 2 * (L + 1))
                    for m in range(4):
                        s = weights(L, f"br{n}{m // 2}")
                        w = wslot(s, KB, 512)
                        bank, full = begin(L, f"b{n}{m}")
                        for j in range(2):
                            mm = project(bank[:, j * T:(j + 1) * T], w, (m % 2) * 256 + j * P, P,
                                         lambda x: ys[:, n * KB + x, :], KB)
                        mm.then_inc(full, 1)
                pe.wait_ge(sem("merged"), 4 * (L + 1))
                for m in range(4):
                    bank, full = begin(L, f"w{m}")
                    for j in range(2):
                        s = weights(L, f"out{m}")
                        mm = project(bank[:, j * T:(j + 1) * T], wslot(s, KD, MB), j * P, P, lambda x: merged[:, x, :])
                    mm.then_inc(full, 1)
                sumsq(L, "ssf", L)
                for b in range(NB):
                    n = len([i for i in range(MIX_END[L]) if i % NB == b])
                    pe.wait_ge(sem(f"bank_free{b}"), n)

            def used(mm, u, j):
                mm.then_inc(sem(f"split_used{j % NSPLIT}"), 1)

            def parts(u, j):
                n, _ = half_words(j)
                wait_hi(pe, u, j)
                wait_lo(pe, u, j)
                hi, lo = w_hi[:, j % NSPLIT, 0:n], w_lo[:, j % NSPLIT, 0:n]
                if UNIT_LOADS[j // 2][0] != "D":
                    hi, lo = (x.rearrange("p (k c) -> p k c", k=KD // 2) for x in (hi, lo))
                return hi, lo

            def dense(u, first=False):
                def three(dst, whi, wlo, xhi, xlo, start, stop):
                    pe.matmul(dst, whi, xhi, start=start, stop=False, skip_group_check=True)
                    pe.matmul(dst, whi, xlo, start=False, stop=False, skip_group_check=True)
                    return pe.matmul(dst, wlo, xhi, start=False, stop=stop, skip_group_check=True)

                for j in range(HALVES):
                    name = UNIT_LOADS[j // 2]
                    g0, gn = GROUPS[int(name[1])]
                    hi, lo = parts(u, j)
                    if name[0] == "D":
                        if j % 2 == 0:
                            pe.wait_ge(sem("hid_lo_ready"), len(GROUPS) * u + int(name[1]) + 1)
                        for x in range(gn * KD // 2):
                            t, m = divmod((j % 2) * gn * KD // 2 + x, KD)
                            c = slice(x * P, (x + 1) * P)
                            mm = three(PS[:, 4 + m // 2, (m % 2) * T:(m % 2 + 1) * T], hi[:, c], lo[:, c],
                                       hid_hi[:, g0 + t, :], hid_lo[:, g0 + t, :], False, False)
                    else:
                        up = name[0] == "U"
                        for t in range(g0, g0 + gn):
                            if j % 2 == 0 and not up and (t >= DB or not first):
                                before = t - DB if t >= DB else max(x for x in range(FT) if x % DB == t % DB) - FT
                                pe.wait_ge(sem("hidf_ready"), FT * u + before + 1)
                            for k in range(KD // 2):
                                kt = (j % 2) * KD // 2 + k
                                if first and j < 2 and t == g0:
                                    pe.wait_ge(sem("h_lo_ready"), KD // 2 + kt // 2 + 1)
                                c = slice((t - g0) * P, (t - g0 + 1) * P)
                                mm = three(PS[:, t % DB, up * T:(up + 1) * T], hi[:, k, c], lo[:, k, c],
                                           h_hi[:, kt, :], h_lo[:, kt, :], kt == 0, kt == KD - 1)
                            if up and j % 2 == 1 and t < g0 + gn - 1:
                                mm.then_inc(sem("tile_full"), 1)
                    used(mm, u, j)

            mixer(0)
            for b in range(4, 8):
                pe.matmul(PS[:, b, :], zb[:, :], zb[:, :].unsqueeze(1).broadcast_to([P, 4, P]), start=True, stop=True, skip_group_check=True)
            dense(0, first=True)
            with pe.Fori(1, NDENSE) as i:
                dense(i)
            mixer(1)

            pe.wait_ge(sem("h_ready"), KD * 2 * DEPTH)
            pe.wait_ge(sem("router_in"), 16)
            for a in range(TT):
                for i in range(KD):
                    mm = pe.matmul(PS[:, 0, a * NE:(a + 1) * NE], hT[:, i, a * P:(a + 1) * P], wr[:, i, :],
                                   start=(i == 0), stop=(i == KD - 1))
            mm.then_inc(sem("logits_full"), 1)
            for a in range(TT):
                for c in range(2):
                    for i in range(4):
                        kt = 4 * c + i
                        mm = pe.transpose(PS[:, 2 + 2 * a + c, i * P:(i + 1) * P], hT[:, kt, a * P:(a + 1) * P], ident[:, :])
                    mm.then_inc(sem("htok_full"), 1)
            pe.wait_ge(sem("msel_ready"), 1)
            pe.wait_ge(sem("tri_ready"), 1)
            pe.matmul(PS[:, 1, 0:NE], tri[:, :], msel[:, 0, :], start=True, stop=True)
            pe.matmul(PS[:, 1, NE:2 * NE], ones[:, :], msel[:, 0, :], start=True, stop=False)
            pe.matmul(PS[:, 1, NE:2 * NE], tri[:, :], msel[:, 1, :], start=False, stop=True)
            pe.matmul(PS[:, 1, 2 * NE:3 * NE], ones[:, :], msel[:, 0, :], start=True, stop=False)
            pe.matmul(PS[:, 1, 2 * NE:3 * NE], ones[:, :], msel[:, 1, :], start=False, stop=True)\
              .then_inc(sem("rank_full"), 1)
            pe.wait_ge(sem("htok_ready"), 4)

            def gather(e, r, at):
                for c in range(2):
                    b, n = at(c)
                    wait_aux_free(pe, b, n)
                    for i in range(4):
                        for a in range(TT):
                            mm = pe.matmul(PS[:, 4 + b, i * CAP:(i + 1) * CAP], htok[:, a, (4 * c + i) * P:(4 * c + i + 1) * P],
                                           psel[:, a, e, :], start=(a == 0), stop=(a == TT - 1))
                    mm.then_inc(sem(f"aux_full{b}"), 1)

            def scatter(e, n, uses):
                pe.wait_ge(sem("ye_act"), n + 1)
                pe.wait_ge(sem("ye_dve"), n + 1)
                for c in range(4):
                    wait_aux_free(pe, c % 2, uses + c // 2)
                    for j in range(2):
                        kt = 2 * c + j
                        mm = pe.matmul(PS[:, 4 + c % 2, j * T:(j + 1) * T], ye[:, kt * P:(kt + 1) * P], selT[:, e, :],
                                       start=True, stop=True)
                    mm.then_inc(sem(f"aux_full{c % 2}"), 1)

            def turn(r, e, n, g, last):
                b, uses = turn_use(r, e, g, last)
                g0, gn = GROUPS[g]
                pe.wait_ge(sem("hide_ready"), len(GROUPS) * n + g + 1)
                wait_aux_free(pe, b, uses)
                for i in range(gn):
                    mm = pe.transpose(PS[:, 4 + b, i * CAP:(i + 1) * CAP], hide[:, g % 2, i * P:(i + 1) * P],
                                      ident[0:CAP, 0:CAP])
                mm.then_inc(sem(f"aux_full{b}"), 1)

            def expert(r, e, n, first=False, last=False):
                def three(dst, xhi, xlo, whi, wlo, start, stop):
                    pe.matmul(dst, xhi, whi, start=start, stop=False)
                    pe.matmul(dst, xlo, whi, start=False, stop=False)
                    return pe.matmul(dst, xhi, wlo, start=False, stop=stop)

                for c in range(2):
                    b, uses = gather_use(r, e - 1, c)
                    wait_aux_free(pe, b, uses + 1)
                for j in range(HALVES):
                    name = UNIT_LOADS[j // 2]
                    g = int(name[1])
                    g0, gn = GROUPS[g]
                    hi, lo = parts(NDENSE + n, j)
                    if name[0] == "D":
                        if j % 2 == 0:
                            b, uses = turn_use(r, e, g, last)
                            wait_aux_free(pe, b, uses + 1)
                        if name == "D0" and j % 2 == 0 and not (isinstance(n, int) and n == 0):
                            pe.wait_ge(sem("ye_act"), n)
                            pe.wait_ge(sem("ye_dve"), n)
                        for x in range(gn):
                            t, c = divmod((j % 2) * gn + x, 2)
                            t += g0
                            w = slice(x * 512, (x + 1) * 512)
                            mm = three(PS[0:CAP, 6 + c, :], hdT_hi[:, t, :], hdT_lo[:, t, :], hi[:, w], lo[:, w],
                                       t == 0, t == FT - 1)
                    else:
                        up = name[0] == "U"
                        if j % 2 == 0 and not up and (g >= 2 or not (isinstance(n, int) and n == 0)):
                            pe.wait_ge(sem("hide_ready"), len(GROUPS) * n + g - 1)
                        for k in range(KD // 2):
                            kt = (j % 2) * KD // 2 + k
                            mm = three(PS[0:CAP, 2 * (g % 2) + up, 0:gn * P], hTe_hi[:, kt, :], hTe_lo[:, kt, :],
                                       hi[:, k, :], lo[:, k, :], kt == 0, kt == KD - 1)
                    used(mm, NDENSE + n, j)
                    for what, x in EXPERT_AFTER.get(j, ()):
                        if what == "tr":
                            turn(r, e, n, x, last)
                        elif what == "scatter" and not first:
                            scatter(e - 1, n - 1, scatter_use(r, e))
                        elif what == "gather" and not last:
                            gather(e + 1, r, lambda c: gather_use(r, e, c))

            def prepare(r):
                pe.wait_ge(sem("sel_ready"), 2 * (r + 1))
                for c in range(4):
                    wait_aux_free(pe, c % 2, PASS_USES * r + c // 2)
                    for i in range(2):
                        for a in range(TT):
                            mm = pe.transpose(PS[0:CAP, 4 + c % 2, i * T + a * P:i * T + (a + 1) * P],
                                              wsel[:, a, 2 * c + i, :], ident[:, :])
                    mm.then_inc(sem(f"aux_full{c % 2}"), 1)

            def one_pass(r):
                prepare(r)
                n = r * NE
                gather(0, r, lambda c: gather_use(r, -1, c))
                expert(r, 0, n, first=True)
                with pe.Fori(1, NE - 1) as e:
                    expert(r, e, n + e)
                expert(r, NE - 1, n + NE - 1, last=True)
                scatter(NE - 1, n + NE - 1, scatter_use(r, NE))
                for b in range(2):
                    wait_aux_free(pe, b, PASS_USES * (r + 1))

            one_pass(0)
            pe.wait_ge(sem("passes_known"), 1)
            npass = pe.value_load(npi[0:1, 0:1], min_val=1, max_val=PASSES)
            with pe.If(npass > 1):
                with pe.Fori(1, npass) as r:
                    one_pass(r)
            for i in range(4):
                bank = PS[:, 2 + i, :]
                for j in range(4):
                    a, kt = i // 2, 4 * (i % 2) + j
                    mm = pe.transpose(bank[:, j * P:(j + 1) * P], xT[:, kt, a * P:(a + 1) * P], ident[:, :])
                mm.then_inc(sem("yo_full"), 1)

        @block.gpsimd
        def _(pool):
            step = Chain(pool, sem("pool_step"))
            pool.memset(ring[:, NSLOT - 1, 0:P], 0.0).then_inc(sem("rows_clear"), 1)
            for t, v in ((ident, 0.0), (ones, 1.0), (eps, EPS)):
                pool.memset(t[:], v).then_inc(sem("pool_step"), 1)
                step.n += 1
            step.wait()
            step(pool.memset(eps[:, 1:2], QK * EPS))
            pool.affine_select(out=ident[:, :], in_=ident[:, :], compare_op=ALU.not_equal, fill=1.0, base=0,
                               pattern=[[-1, P]], channel_multiplier=1).then_inc(sem("ident_ready"), 1)
            for t, v in ((zb, 0.0), (maskc, 0.0), (maskg, 1.0), (chm, 1.0), (keep, 1.0),
                         (one1, 1.0), (invr, 0.0), (R, 0.0), (u, 0.0), (qdm, 0.0), (selh, 0.0)):
                pool.memset(t[:], v).then_inc(sem("pool_step"), 1)
                step.n += 1
            step.wait()
            for i in range(ROPE):
                step(pool.memset(invr[0:1, NOPE + i:NOPE + i + 1], float(np.float32(ROPE_BASE ** (-(i % HALF) / HALF)))))
            step(pool.memset(selh[0:GDK, 0:1], GDK ** -0.5))
            step(pool.memset(selh[GDK:P, 1:2], GDK ** -0.5))

            def select(t, pattern, base, cm, fill, op=ALU.is_ge):
                step(pool.affine_select(out=t, in_=t, compare_op=op, fill=fill, base=base, pattern=pattern,
                                        channel_multiplier=cm))
            select(maskc[:, 0:P], [[-1, P]], 0, 1, NEG)
            select(maskc[:, 2 * P:3 * P], [[-1, P]], 0, 1, NEG)
            g3 = maskg[:, :].rearrange("p (n c) -> p n c", n=NCT)
            select(g3, [[-GC, NCT], [0, GC]], 0, 1, 0.0)
            select(g3, [[GC, NCT], [0, GC]], GC - 1, -1, 0.0)
            select(g3, [[GC, NCT], [1, GC]], 0, -1, 0.0)
            select(chm[:, :], [[-GC, NCT]], 0, 1, 0.0)
            select(chm[:, :], [[GC, NCT]], GC - 1, -1, 0.0)
            k3 = keep[:, :].rearrange("p (n c) -> p n c", c=GC)
            select(k3, [[0, NCH], [1, GC]], 0, 0, 0.0, ALU.not_equal)
            rr_ = R[NOPE:QK, NOPE:QK]
            select(rr_, [[-1, ROPE]], -HALF, 1, -1.0, ALU.not_equal)
            select(rr_, [[-1, ROPE]], HALF, 1, 1.0, ALU.not_equal)
            pool.iota(cnt[:, :], pattern=[[1, PADW]], base=1, channel_multiplier=0).then_inc(sem("iotas"), 1)
            pool.iota(sloti[:, :], pattern=[[1, CAP]], base=0, channel_multiplier=0).then_inc(sem("iotas"), 1)
            pool.memset(one1[:, :], 1.0).then_inc(sem("consts"), 1)
            for L in range(DEPTH):
                r = slice(NOPE, QK)
                if L == 0:
                    pool.wait_ge(sem("rope_tables"), 1)
                cos = cs[r, 0, :].unsqueeze(1).broadcast_to([ROPE, 2, T])
                for c, t in (("q", q), ("k", k)):
                    for i in range(4):
                        _, f, _, n = use(L, f"r{c}{i}")
                        pool.wait_ge(f, n + 1)
                        x = t[r, 2 * i:2 * i + 2, :]
                        pool.tensor_tensor(x, x, cos, MUL).then_inc(sem("cos_done"), 1)
                pool.wait_ge(sem("eb_ready"), L + 1)
                for x in ("gq", "gk"):
                    _, _, free, n = use(L, x)
                    pool.wait_ge(free, n + 1)
                for c in range(2):
                    rows = slice(c * GDK, (c + 1) * GDK)
                    pool.tensor_tensor(qdm[rows, c, :, :], gq[rows, :, :], eb[rows, :, :], MUL).then_inc(sem("qdm_step"), 1)
                pool.wait_ge(sem("qdm_step"), 2 * (L + 1))
                pool.tensor_scalar(qdm[:, :, :, :], qdm[:, :, :, :], GDK ** -0.5, None, MUL).then_inc(sem("qdm_ready"), 1)
                pool.wait_ge(sem("ek_ready"), L + 1)
                pool.tensor_tensor(kdec[:, :, :], gk[:, :, :], ek[:, :, :], MUL).then_inc(sem("dec_ready"), 1)
                for x in ("ua", "ub"):
                    _, _, free, n = use(L, x)
                    pool.wait_ge(free, n + 1)
                if L == 0:
                    pool.wait_ge(sem("windows"), 1)
                W = PADW + T
                step(pool.tensor_tensor(pwa[:, :, 1:W], u[:, :, 1:W], u[:, :, 0:W - 1], ADD))
                step(pool.tensor_tensor(pwb[:, 1:, 3:W], pwa[:, 1:, 3:W], pwa[:, 1:, 1:W - 2], ADD))
                step(pool.tensor_tensor(pwa[:, 2:, 7:W], pwb[:, 2:, 7:W], pwb[:, 2:, 3:W - 4], ADD))
                step(pool.tensor_tensor(pwb[:, 3, 15:W], pwa[:, 3, 15:W], pwa[:, 3, 7:W - 8], ADD))
                for g, w in enumerate(WINDOWS):
                    win = (pwa if g % 2 == 0 else pwb)[:, g, :]
                    step(pool.tensor_tensor(win[:, PADW:2 * PADW], win[:, PADW:2 * PADW], winf[:, g, :], MUL))
                    step(pool.tensor_scalar(win[:, PADW:W], win[:, PADW:W], 1.0 / w, None, MUL))
                    pool.tensor_tensor(u[:, g, PADW:W], win[:, PADW:W], u[:, g, PADW:W], SUB).then_inc(sem("pooled"), 1)
                for a in range(TT):
                    for d in range(2):
                        pool.wait_ge(sem("e_exp"), 4 * L + 2 * a + d + 1)
                        e = scr[:, d * 2048:(d + 1) * 2048].rearrange("p (c t) -> p c t", c=GC)
                        ins = pool.tensor_tensor(e, e, gk[:, d, a * P:(a + 1) * P].unsqueeze(1).broadcast_to([P, GC, P]), MUL)
                        ins.then_inc(sem("e_k"), 1)
            _, f, _, n = use(DEPTH - 1, "pl1")
            pool.wait_ge(f, n + 1)
            step(pool.memset(tri, 1.0))
            pool.affine_select(out=tri, in_=tri, compare_op=ALU.is_ge, fill=0.0, base=-1, pattern=[[1, P]],
                               channel_multiplier=-1).then_inc(sem("tri_ready"), 1)

        @block.scalar
        def _(act):
            def full(L, name):
                bank, f, free, n = use(L, name)
                act.wait_ge(f, n + 1)
                return bank, free

            def freed(L, name):
                _, _, free, n = use(L, name)
                act.wait_ge(free, n + 1)

            def pcol(name, i=0, rows=P):
                return par[0:rows, PCOL[name] + i:PCOL[name] + i + 1]

            def two(ap):
                return ap.rearrange("p (a t) -> p a t", a=2)

            bank, free = full(-1, "par")
            act.activation(par[:, :], bank[:, 0:NPAR], ACT.Copy).then_inc(free, 1)
            bank, free = full(-1, "inv")
            act.activation(invc[NOPE:QK, :], bank[NOPE:QK, 0:1], ACT.Copy).then_inc(free, 1)

            def squares(L, first):
                for i in (0, 2):
                    if L < 0:
                        freed(-1, f"x{i}")
                    act.activation(sq[:, 2 * i:2 * i + 2, :], xT[:, 2 * i:2 * i + 2, :], ACT.Square)\
                       .then_inc(sem("sq_act"), 1)

            def inverse_rms(L, i, name, n, scale):
                bank, free = full(L, name)
                x = 5 * L + i
                r = (rt, rr)[x % 2][:, 0:n, :]
                last = {2: ("h_ready", KD * (2 * L + 1)), 3: ("latn_ready", 4 * (L + 1)), 4: ("yb_ready", 2 * L + 1),
                        0: ("yb_ready", 2 * L), 1: ("h_ready", 2 * KD * L)}[i]
                if last[1]:
                    act.wait_ge(sem(last[0]), last[1])
                act.activation(r, bank[:, 0:n * T].rearrange("p (a t) -> p a t", a=n), ACT.Ln, bias=eps[:, 0:1],
                               scale=scale).then_inc(free, 1)
                freed(L, name)
                act.activation(r, r, ACT.Exp, scale=-0.5).then_inc(sem("rms_ready"), 1)

            def split(L, name, pieces=range(PIECES)):
                s, r = slot_of(L, name)
                act.wait_ge(sem(f"slot_full{s}"), 16 * r)
                for p in pieces:
                    piece_done(act, L, name, p)
                    raw, hi, _ = piece_of(L, name, p)
                    act.activation(hi, raw, ACT.Copy).then_inc(sem("m_hi_ready"), 1)

            FIRST, LAST = range(PIECES - 1), [PIECES - 1]

            def split_h(which):
                for i in range(4):
                    act.wait_ge(sem("h_ready"), KD * which + 2 * i + 2)
                    act.activation(h_hi[:, 2 * i:2 * i + 2, :], hT[:, 2 * i:2 * i + 2, :], ACT.Copy).then_inc(sem("h_hi_ready"), 1)

            def mixer(L):
                for i in (0, 2):
                    if L == 0:
                        freed(-1, f"x{i}")
                    else:
                        act.wait_ge(sem("x_dense"), i + 2)
                    act.activation(sq[:, 2 * i:2 * i + 2, :], xT[:, 2 * i:2 * i + 2, :], ACT.Square)\
                       .then_inc(sem("sq_act"), 1)
                if L == 0:
                    act.wait_ge(sem("ident_ready"), 1)
                split(L, "cq")
                inverse_rms(L, 0, "ssm", 1, 1.0 / D)
                split_h(2 * L)
                for i, name in enumerate(("cq", "ckv")):
                    split(L, ("ckv", "gq")[i], FIRST)
                    bank, free = full(L, name)
                    act.activation(sq[:, 2 * i:2 * i + 2, :], two(bank), ACT.Square)
                    act.activation(lat[:, 2 * i:2 * i + 2, :], two(bank), ACT.Copy).then_inc(free, 1)
                    if i == 0:
                        split(L, "ckv", LAST)
                bank, free = full(L, "kr")
                act.activation(krope[NOPE:QK, :], bank[NOPE:QK, 0:T], ACT.Copy).then_inc(free, 1)
                split(L, "gq", LAST)
                split(L, "gk")
                inverse_rms(L, 1, "sslat", 2, 1.0 / RANK)
                split(L, "va")
                for i in range(4):
                    bank, free = full(L, f"q{i}")
                    act.activation(sq[0:QK, 2 * i:2 * i + 2, :], two(bank[0:QK, :]), ACT.Square)
                    act.activation(q[:, 2 * i:2 * i + 2, :], two(bank[0:QK, :]), ACT.Copy,
                                   scale=pcol("g_qk_q", L, QK)).then_inc(free, 1)
                split(L, "vb")
                freed(L, "kr")
                kr8 = krope[NOPE:QK, :].unsqueeze(1).broadcast_to([ROPE, H, T])
                act.activation(sk[NOPE:QK, :, :], kr8, ACT.Square)
                act.activation(k[NOPE:QK, :, :], kr8, ACT.Copy, scale=par[NOPE:QK, PCOL["g_qk_k"] + L:PCOL["g_qk_k"] + L + 1])
                for i in range(4):
                    bank, free = full(L, f"k{i}")
                    act.activation(sk[0:NOPE, 2 * i:2 * i + 2, :], two(bank[0:NOPE, :]), ACT.Square)
                    act.activation(k[0:NOPE, 2 * i:2 * i + 2, :], two(bank[0:NOPE, :]), ACT.Copy,
                                   scale=pcol("g_qk_k", L, NOPE)).then_inc(free, 1)
                split(L, "oga", FIRST)
                bank, free = full(L, "lr")
                act.activation(glr[:, :], bank[0:GRANK, 0:T], ACT.Copy).then_inc(free, 1)
                split(L, "oga", LAST)
                if L == 0:
                    act.wait_ge(sem("angles"), 1)
                    act.activation(cs[NOPE:QK, :, :], ang[NOPE:QK, 1:3, :], ACT.Sin).then_inc(sem("rope_tables"), 1)

                def out_gate(i):
                    bank, _ = full(L, f"og{'ab'[i]}")
                    if 2 * L + i:
                        act.wait_ge(sem("og_done"), 2 * L + i)
                    act.activation(th[:, :, :], two(bank), ACT.Tanh, scale=0.5).then_inc(sem("og_tanh"), 1)
                split(L, "ogb", FIRST)
                out_gate(0)
                split(L, "ogb", LAST)
                bank, free = full(L, "ssq")
                act.activation(rq16[:, :], bank[:, 0:TT * H], ACT.Sqrt, bias=eps[:, 1:2])
                act.activation(rk16[:, :], bank[:, TT * H:2 * TT * H], ACT.Sqrt, bias=eps[:, 0:1], scale=1.0 / QK).then_inc(free, 1)
                act.wait_ge(sem("z_abs"), L + 1)
                act.activation(ztmp[:, 2:4, :], ztmp[:, 2:4, :], ACT.Exp, scale=-1.0).then_inc(sem("z_step"), 1)
                act.wait_ge(sem("z_step"), 2 * L + 1)
                act.activation(ztmp[:, 2:4, :], ztmp[:, 2:4, :], ACT.Ln, bias=1.0).then_inc(sem("z_step"), 1)
                split(L, "ua", FIRST)
                out_gate(1)
                split(L, "ua", LAST)
                for i, name in enumerate(("ua", "ub")):
                    split(L, ("ub", "g0")[i], FIRST)
                    bank, free = full(L, name)
                    act.activation(u[:, 2 * i:2 * i + 2, PADW:PADW + T], two(bank), ACT.Copy).then_inc(free, 1)
                    split(L, ("ub", "g0")[i], LAST)
                act.wait_ge(sem("bc_ready"), L + 1)
                act.activation(eb[:, :, :], bc[:, :, :], ACT.Exp).then_inc(sem("eb_ready"), 1)
                act.activation(al[:, :, :], bc[:, :, :].rearrange("p d (n c) -> p d n c", c=GC)[:, :, :, GC - 1],
                               ACT.Exp).then_inc(sem("al_ready"), 1)
                act.wait_ge(sem("db_ready"), L + 1)
                act.activation(ek[:, :, :], ek[:, :, :], ACT.Exp).then_inc(sem("ek_ready"), 1)

                def gate(i):
                    if i < 11:
                        split(L, f"g{i + 1}", FIRST)
                    bank, free = full(L, f"g{i}")
                    if i == 0:
                        act.wait_ge(sem("latn_ready"), 4 * (L + 1))
                        _, f, _, n = use(L, "vm1")
                        act.wait_ge(f, n + 1)
                    if i == 8:
                        act.wait_ge(sem("k_ready"), 4 * (L + 1))
                    act.activation(gates[:, 2 * i:2 * i + 2, :], two(bank), ACT.Tanh, scale=0.5).then_inc(free, 1)
                    if i < 11:
                        split(L, f"g{i + 1}", LAST)

                def exps(h):
                    act.wait_ge(sem("nb_ready"), H * L + h + 1)
                    for a in range(TT):
                        w = slice(0, P) if a == 0 else slice(P, 3 * P)
                        ins = act.activation(Pr[:, h % 3, w], Pr[:, h % 3, w], ACT.Exp, bias=nbs[:, h % 2, a:a + 1],
                                             scale=rqs[:, a * H + h:a * H + h + 1], accum_out=sums[:, h % 2, a:a + 1])
                    ins.then_inc(sem("exp_done"), 1)

                def turned(h):
                    bank, free = full(L, f"pt{h}")
                    if h == 0:
                        act.wait_ge(sem("dec_ready"), L + 1)
                    if h >= 2:
                        _, f, _, n = use(L, f"o{(h - 2) // 2}")
                        act.wait_ge(f, n + 1)
                    act.activation(PT[:, h % 2, :], bank[:, 0:3 * P], ACT.Copy).then_inc(free, 1)

                def values(i):
                    bank, free = full(L, f"o{i}")
                    act.activation(ys[:, i, :], bank[:, 0:T], ACT.Copy).then_inc(free, 1)

                def decay(a, d):
                    act.wait_ge(sem("e_diff"), 4 * L + 2 * a + d + 1)
                    e = scr[:, d * 2048:(d + 1) * 2048]
                    act.activation(e, e, ACT.Exp).then_inc(sem("e_exp"), 1)

                def pool_out(i):
                    bank, free = full(L, f"pl{i}")
                    for j in range(2):
                        ins = act.activation(ys[:, 2 * KB + 2 * i + j, :], bank[:, j * T:(j + 1) * T], ACT.Copy,
                                             scale=pcol("pool_scale", L * NG + 2 * i + j))
                    ins.then_inc(free, 1)

                gate(0), exps(0), exps(1), gate(1), turned(0), turned(1), exps(2), exps(3)
                gate(2), values(0), turned(2), turned(3), exps(4), exps(5), decay(0, 0)
                gate(3), values(1), turned(4), turned(5), exps(6), exps(7), decay(0, 1)
                gate(4), values(2), turned(6), turned(7), decay(1, 0)
                gate(5), pool_out(0), pool_out(1), decay(1, 1)
                gate(6), values(3), gate(7), gate(8), gate(9)
                act.wait_ge(sem("go_full"), L + 1)
                for i in range(2):
                    act.activation(gsq[:, i, :, :], two(PS[:, 6 + i, :]), ACT.Square).then_inc(sem("gsq_ready"), 1)
                gate(10)
                for i in range(2):
                    inverse_rms(L, 2 + i, f"ssg{i}", 2, 1.0 / GDV)
                gate(11)
                _, f, _, n = use(L, "w0")
                act.wait_ge(f, n + 1)
                act.wait_ge(sem("merged"), 4 * (L + 1))
                for j in range(NSPLIT):
                    round_hi(act, NDENSE * L, j, L, 0)
                for i in (0, 2):
                    freed(L, f"w{i + 1}")
                    freed(L, f"w{i}")
                    act.activation(sq[:, 2 * i:2 * i + 2, :], xT[:, 2 * i:2 * i + 2, :], ACT.Square)\
                       .then_inc(sem("sq_act"), 1)
                inverse_rms(L, 4, "ssf", 1, 1.0 / D)

            def dense(u, first=False):
                def gate_up(g):
                    g0, gn = GROUPS[g]
                    for t in range(gn):
                        if t < gn - 1:
                            act.wait_ge(sem("tile_full"), (FT - len(GROUPS)) * u + sum(x[1] - 1 for x in GROUPS[:g]) + t + 1)
                        else:
                            wait_used(act, u, HALF_OF[f"U{g}"] + 1)
                        if g > 0 or not first:
                            act.wait_ge(sem("hidf_ready"), FT * u + g0 + (t if t < GROUPS[g - 1][1] else t - 3)
                                        - GROUPS[g - 1][1] + 1)
                        act.activation(sil[:, t, :], PS[:, (g0 + t) % DB, 0:T], ACT.Silu).then_inc(sem("sil_ready"), 1)
                    act.wait_ge(sem("hidf_ready"), FT * u + g0 + gn)
                    act.activation(hid_hi[:, g0:g0 + gn, :], hidf[:, 0:gn, :], ACT.Copy).then_inc(sem("hid_hi_ready"), 1)

                for j in range(HALVES):
                    for _, g in DENSE_AFTER.get(j - NSPLIT, ()):
                        gate_up(g)
                    if not (first and j < NSPLIT):
                        round_hi(act, u, j, 0, u)

            mixer(0)
            split_h(1)
            dense(0, first=True)
            with act.Fori(1, NDENSE) as i:
                dense(i)
            mixer(1)

            act.wait_ge(sem("logit_gap"), 1)
            act.activation(rsm[:, 2:4], rsm[:, 0:2], ACT.Exp).then_inc(sem("top_exp"), 1)

            def tokens(r, e, n):
                for c in range(2):
                    b, uses = gather_use(r, e - 1, c)
                    wait_aux_full(act, b, uses)
                    act.activation(hTe_hi[:, 4 * c:4 * c + 4, :], PS[:, 4 + b, 0:4 * CAP].rearrange("p (k c) -> p k c", k=4),
                                   ACT.Copy).then_inc(sem("hTe_hi_ready"), 1)

            def rows_out(n):
                wait_used(act, NDENSE + n, HALVES - 1)
                act.activation(ye[:, 0:512], PS[0:CAP, 6, :], ACT.Copy).then_inc(sem("ye_act"), 1)

            def expert(r, e, n, first=False, last=False):
                u = NDENSE + n
                for j in range(HALVES):
                    if j == 2 and not first:
                        rows_out(n - 1)
                    for what, g in EXPERT_AFTER.get(j - NSPLIT, ()):
                        if what == "gu":
                            g0, gn = GROUPS[g]
                            wait_used(act, u, HALF_OF[f"U{g}"] + 1)
                            if g >= 2 or not (isinstance(n, int) and n == 0):
                                act.wait_ge(sem("hide_ready"), len(GROUPS) * n + g - 1)
                            act.activation(sile[:, g % 2, 0:gn * P], PS[0:CAP, 2 * (g % 2), 0:gn * P], ACT.Silu)\
                               .then_inc(sem("sile_ready"), 1)
                        elif what == "tr":
                            b, uses = turn_use(r, e, g, last)
                            g0, gn = GROUPS[g]
                            wait_aux_full(act, b, uses)
                            act.activation(hdT_hi[:, g0:g0 + gn, :], PS[:, 4 + b, 0:gn * CAP].rearrange("p (k c) -> p k c", k=gn),
                                           ACT.Copy).then_inc(sem("hdT_hi_ready"), 1)
                        elif what == "gather" and not last:
                            tokens(r, e + 1, n + 1)
                    if not (j < NSPLIT and isinstance(n, int) and n == 0):
                        round_hi(act, u, j, 1, n)

            def one_pass(r):
                n = r * NE
                for c in range(4):
                    wait_aux_full(act, c % 2, PASS_USES * r + c // 2)
                    act.activation(selT[:, 2 * c:2 * c + 2, :], two(PS[0:CAP, 4 + c % 2, :]), ACT.Copy)\
                       .then_inc(sem(f"aux_free{c % 2}"), 1)
                tokens(r, 0, n)
                expert(r, 0, n, first=True)
                with act.Fori(1, NE - 1) as e:
                    expert(r, e, n + e)
                expert(r, NE - 1, n + NE - 1, last=True)
                rows_out(n + NE - 1)

            one_pass(0)
            act.wait_ge(sem("passes_known"), 1)
            npass = act.value_load(npi[0:1, 0:1], min_val=1, max_val=PASSES)
            with act.If(npass > 1):
                with act.Fori(1, npass) as r:
                    one_pass(r)
            for i in range(4):
                act.wait_ge(sem("yo_full"), i + 1)
                act.activation(yout[:, i // 2, (i % 2) * 512:(i % 2 + 1) * 512], PS[:, 2 + i, :], ACT.Copy)\
                   .then_inc(sem("y_out"), 1)

        @block.vector
        def _(dve):
            step = Chain(dve, sem("dve_step"))

            def full(L, name):
                bank, f, free, n = use(L, name)
                dve.wait_ge(f, n + 1)
                return bank, free

            def freed(L, name):
                _, _, free, n = use(L, name)
                dve.wait_ge(free, n + 1)

            def pcol(name, i=0, rows=P):
                return par[0:rows, PCOL[name] + i:PCOL[name] + i + 1]

            def two(ap):
                return ap.rearrange("p (a t) -> p a t", a=2)

            for i in range(4):
                bank, free = full(-1, f"x{i}")
                dve.tensor_copy(xT[:, 2 * i:2 * i + 2, :], two(bank)).then_inc(free, 1)

            def tables():
                TWO_PI = 2 * np.pi
                c1 = 6.28125
                c2 = float(np.float32(np.floor((TWO_PI - c1) * 2 ** 21) / 2 ** 21))
                c3 = float(np.float32(TWO_PI - c1 - c2))
                magic = 1.5 * 2 ** 23
                pi = float(np.nextafter(np.float32(np.pi), np.float32(0)))
                r = slice(NOPE, QK)
                dve.wait_ge(sem("pos_in"), 16)
                step(dve.tensor_copy(ang[r, 0, :], posi[r, :]))
                freed(-1, "inv")
                step(dve.tensor_scalar(ang[r, 0, :], ang[r, 0, :], invc[r, 0:1], None, MUL))
                for j, shift in ((1, 0.25), (2, 0.0)):
                    step(dve.tensor_scalar(angk[r, :], ang[r, 0, :], 1 / TWO_PI, shift, MUL, ADD))
                    step(dve.tensor_scalar(angk[r, :], angk[r, :], magic, magic, ADD, SUB))
                    step(dve.scalar_tensor_tensor(ang[r, j, :], angk[r, :], -c1, ang[r, 0, :], MUL, ADD))
                    step(dve.scalar_tensor_tensor(ang[r, j, :], angk[r, :], -c2, ang[r, j, :], MUL, ADD))
                    step(dve.scalar_tensor_tensor(ang[r, j, :], angk[r, :], -c3, ang[r, j, :], MUL, ADD))
                    if shift:
                        step(dve.tensor_scalar(ang[r, j, :], ang[r, j, :], np.pi / 2, None, ADD))
                    ins = dve.tensor_scalar(ang[r, j, :], ang[r, j, :], pi, -pi, MIN, MAX)
                    if j == 1:
                        step(ins)
                ins.then_inc(sem("angles"), 1)
                dve.wait_ge(sem("iotas"), 2)
                for g, w in enumerate(WINDOWS):
                    step(dve.tensor_scalar(winf[:, g, :], cnt[:, :], float(w), 1.0 / w, MIN, MUL))
                dve.reciprocal(winf[:, :, :], winf[:, :, :]).then_inc(sem("windows"), 1)
                step(dve.tensor_copy(slots[:, :], sloti[:, :]))
                step(dve.tensor_copy(iot8[:, :], sloti[:, 0:NE]))

            def rms(L, i):
                x = 5 * L + i
                dve.wait_ge(sem("rms_ready"), x + 1)
                return (rt, rr)[x % 2]

            def norm_x(L, which, gain):
                for i in (1, 3):
                    if which == "ssm" and L == 1:
                        dve.wait_ge(sem("x_dense"), i + 1)
                    elif which == "ssf":
                        freed(L, f"w{i}")
                    else:
                        freed(-1, f"x{i}")
                    dve.tensor_tensor(sq[:, 2 * i:2 * i + 2, :], xT[:, 2 * i:2 * i + 2, :], xT[:, 2 * i:2 * i + 2, :], MUL)\
                       .then_inc(sem("sq_dve"), 1)
                if which == "ssm":
                    split(L, "cq")
                r = rms(L, 0 if which == "ssm" else 4)
                low = 0 if (L, which) == (DEPTH - 1, "ssf") else 4
                for i in range(KD):
                    if low and i in (4, 6):
                        split_h(2 * L + (which == "ssf"), i // 2 - 2)
                    dve.scalar_tensor_tensor(hT[:, i, :], xT[:, i, :], pcol(gain, L * KD + i), r[:, 0, :], MUL, MUL)\
                       .then_inc(sem("h_ready"), 1)
                if low:
                    for i in (2, 3):
                        split_h(2 * L + (which == "ssf"), i)

            def split(L, name, pieces=range(PIECES)):
                for p in pieces:
                    dve.wait_ge(sem("m_hi_ready"), piece_no(L, name, p) + 1)
                    raw, hi, lo = piece_of(L, name, p)
                    dve.tensor_tensor(lo, raw, hi.bitcast(F32), SUB).then_inc(sem("m_lo_ready"), 1)

            FIRST, LAST = range(PIECES - 1), [PIECES - 1]

            def split_h(which, i):
                x = slice(2 * i, 2 * i + 2)
                dve.wait_ge(sem("h_hi_ready"), 4 * which + i + 1)
                dve.tensor_tensor(h_lo[:, x, :], hT[:, x, :], h_hi[:, x, :].bitcast(F32), SUB).then_inc(sem("h_lo_ready"), 1)

            def mixer(L):
                norm_x(L, "ssm", "g_mix")
                split(L, "ckv"), split(L, "gq")
                split(L, "gk", FIRST)
                bank, free = full(L, "gq")
                dve.tensor_copy(gq[:, :, :], two(bank)).then_inc(free, 1)
                split(L, "gk", LAST)
                r = rms(L, 1)
                for i in range(4):
                    g = pcol("g_cq" if i < 2 else "g_ckv", L * KR + i % 2)
                    dve.scalar_tensor_tensor(latn[:, i, :], lat[:, i, :], g, r[:, i // 2, :], MUL, MUL)\
                       .then_inc(sem("latn_ready"), 1)
                split(L, "va", FIRST)
                bank, free = full(L, "gk")
                dve.tensor_copy(gk[:, :, :], two(bank)).then_inc(free, 1)
                split(L, "va", LAST)

                def v_half(name, c):
                    bank, free = full(L, name)
                    dve.tensor_copy(gvt[:, :, c * 256:(c + 1) * 256], two(bank)).then_inc(free, 1)
                split(L, "vb", FIRST)
                v_half("va", 0)
                split(L, "vb", LAST)
                if L == 0:
                    tables()
                for a in range(TT):
                    bank, free = full(L, f"vm{a}")
                    dve.tensor_copy(vt[:, a, :], bank).then_inc(free, 1)
                split(L, "oga", FIRST)
                v_half("vb", 1)
                split(L, "oga", LAST)

                def out_gate(i):
                    bank, free = full(L, f"og{'ab'[i]}")
                    dve.wait_ge(sem("og_tanh"), 2 * L + i + 1)
                    y = ys[:, KB + 2 * i:KB + 2 * i + 2, :]
                    dve.scalar_tensor_tensor(y, th[:, :, :], 1.0, two(bank), ADD, MUL).then_inc(free, 1)
                    freed(L, f"og{'ab'[i]}")
                    dve.engine_nop().then_inc(sem("og_done"), 1)
                split(L, "ogb", FIRST)
                out_gate(0)
                split(L, "ogb", LAST)
                freed(L, "ssq")
                step(dve.reciprocal(rqs[:, :], rq16[:, :]))
                dve.reciprocal(rk16[:, :], rk16[:, :]).then_inc(sem("rk_ready"), 1)
                bank, free = full(L, "z")
                for d in range(2):
                    ins = dve.tensor_scalar(ztmp[:, d, :], bank[:, d * T:(d + 1) * T], pcol("b_gla_gate", 2 * L + d), None, ADD)
                ins.then_inc(free, 1)
                freed(L, "z")
                dve.scalar_tensor_tensor(ztmp[:, 2:4, :], ztmp[:, 0:2, :], -1.0, ztmp[:, 0:2, :], MUL, MAX).then_inc(sem("z_abs"), 1)
                dve.wait_ge(sem("z_step"), 2 * L + 2)
                step(dve.scalar_tensor_tensor(ztmp[:, 0:2, :], ztmp[:, 0:2, :], 0.0, ztmp[:, 2:4, :], MIN, SUB))
                step(dve.tensor_scalar(ztmp[:, 0:2, :], ztmp[:, 0:2, :], 1.0 / TAU, None, MUL))
                for d in range(2):
                    ins = dve.tensor_tensor_scan(bc[:, d, :], keep[:, :], ztmp[:, d, :], 0.0, MUL, ADD)
                    if d == 0:
                        step(ins)
                ins.then_inc(sem("bc_ready"), 1)
                dve.wait_ge(sem("bc_ready"), L + 1)
                b4 = bc[:, :, :].rearrange("p d (n c) -> p d n c", c=GC)
                for d in range(2):
                    ins = dve.tensor_tensor(ek[:, d, :].rearrange("p (n c) -> p n c", c=GC),
                                            b4[:, d, :, GC - 1:GC].broadcast_to([P, NCH, GC]), b4[:, d], SUB)
                    if d == 0:
                        step(ins)
                ins.then_inc(sem("db_ready"), 1)
                split(L, "ua", FIRST)
                out_gate(1)
                split(L, "ua", LAST)
                for i in range(4):
                    bank, free = full(L, f"ssk{i}")
                    x = k[:, 2 * i:2 * i + 2, :]
                    dve.tensor_tensor(x, x, two(bank[0:QK, :]), MUL).then_inc(free, 1)

                r = slice(NOPE, QK)
                for c, t in (("q", q), ("k", k)):
                    split(L, "ub" if c == "q" else "g0")
                    for i in range(4):
                        bank, free = full(L, f"r{c}{i}")
                        if L == 0 and c == "q" and i == 0:
                            dve.wait_ge(sem("rope_tables"), 1)
                        x = t[r, 2 * i:2 * i + 2, :]
                        sin = cs[r, 1, :].unsqueeze(1).broadcast_to([ROPE, 2, T])
                        dve.tensor_tensor(rtmp[r, :, :], two(bank[r, :]), sin, MUL).then_inc(free, 1)
                        freed(L, f"r{c}{i}")
                        dve.wait_ge(sem("cos_done"), H * L + 4 * (c == "k") + i + 1)
                        dve.tensor_tensor(x, x, rtmp[r, :, :], ADD).then_inc(sem(f"{c}_ready"), 1)
                        dve.wait_ge(sem(f"{c}_ready"), 4 * L + i + 1)
                        if c == "k" and i == 2:
                            split(L, "g1", FIRST)

                def masked(h):
                    bank, free = full(L, f"s{h}")
                    if h >= 3:
                        _, f, _, n = use(L, f"pt{h - 3}")
                        dve.wait_ge(f, n + 1)
                    dve.tensor_tensor(Pr[:, h % 3, :], bank[:, 0:3 * P], maskc[:, :], ADD).then_inc(free, 1)
                    freed(L, f"s{h}")
                    for a, w in ((0, slice(0, P)), (1, slice(P, 3 * P))):
                        step(dve.tensor_reduce(mx[:, h % 2, a:a + 1], Pr[:, h % 3, w], AX.X, MAX))
                    for a in range(TT):
                        ins = dve.tensor_scalar(nbs[:, h % 2, a:a + 1], mx[:, h % 2, a:a + 1],
                                                rqs[:, a * H + h:a * H + h + 1], -1.0, MUL, MUL)
                        if a == 0:
                            step(ins)
                    ins.then_inc(sem("nb_ready"), 1)

                def scaled(h):
                    dve.wait_ge(sem("exp_done"), H * L + h + 1)
                    step(dve.reciprocal(mx[:, h % 2, :], sums[:, h % 2, :]))
                    for a, w in ((0, slice(0, P)), (1, slice(P, 3 * P))):
                        ins = dve.tensor_scalar(Pr[:, h % 3, w], Pr[:, h % 3, w], mx[:, h % 2, a:a + 1], None, MUL)
                        if a == 0:
                            step(ins)
                    ins.then_inc(sem("p_ready"), 1)
                    dve.wait_ge(sem("p_ready"), H * L + h + 1)

                split(L, "g1", LAST)
                masked(0), masked(1)
                scaled(0), scaled(1)
                split(L, "g2")
                masked(2), masked(3)
                def bcn(d, a):
                    return bc[:, d, a * P:(a + 1) * P].rearrange("p (n c) -> p n c", c=GC)

                def diff(a, d):
                    b = bcn(d, a)
                    if a > 0:
                        _, f, _, n = use(L, "A0")
                        dve.wait_ge(f, n + 1)
                    step(dve.tensor_tensor(E[:, d], b.rearrange("p n c -> p c n").unsqueeze(3).broadcast_to([P, GC, NCT, GC]),
                                           b.unsqueeze(1).broadcast_to([P, GC, NCT, GC]), SUB))
                    e = scr[:, d * 2048:(d + 1) * 2048]
                    dve.tensor_scalar(e, e, 0.0, None, MIN).then_inc(sem("e_diff"), 1)

                def times_q(a, d):
                    dve.wait_ge(sem("e_k"), 4 * L + 2 * a + d + 1)
                    g = gq[:, d, a * P:(a + 1) * P].rearrange("p (n c) -> p n c", c=GC)
                    dve.tensor_tensor(E[:, d], E[:, d],
                                      g.rearrange("p n c -> p c n").unsqueeze(3).broadcast_to([P, GC, NCT, GC]), MUL)\
                       .then_inc(sem("e_ready"), 1)


                def scores_in_chunk(a):
                    bank, free = full(L, f"A{a}")
                    if 2 * L + a:
                        dve.wait_ge(sem("attn_used"), 2 * L + a)
                    A4 = bank[:, 0:GC * GH].rearrange("p (c h) -> p h c", h=GH)
                    for h in range(GH):
                        ins = dve.tensor_tensor(attn[:, h, :].rearrange("p (n c) -> p n c", c=GC),
                                                A4[:, h].unsqueeze(1).broadcast_to([P, NCT, GC]),
                                                maskg[:, :].rearrange("p (n c) -> p n c", c=GC), MUL)
                    ins.then_inc(free, 1)
                    freed(L, f"A{a}")
                    dve.engine_nop().then_inc(sem("attn_ready"), 1)

                def keys_by_chunk(a):
                    bank, free = full(L, f"kd{a}")
                    if a > 0:
                        _, f, _, n = use(L, "U3")
                        dve.wait_ge(f, n + 1)
                    dve.tensor_tensor(kdm[:, :, :], bank[:, 0:T].unsqueeze(1).broadcast_to([P, NCT, T]),
                                      chm[:, :].unsqueeze(2).broadcast_to([P, NCT, T]), MUL).then_inc(free, 1)
                    freed(L, f"kd{a}")
                    dve.engine_nop().then_inc(sem("kdm_ready"), 1)

                def states(a):
                    for i in range(4):
                        bank, free = full(L, f"U{4 * a + i}")
                        for j in range(2):
                            n = NCT * a + 2 * i + j
                            if n == NCH - 1:
                                continue
                            if n >= NCT:
                                dve.wait_ge(sem("state_used"), (NCH - 2) * L + n - NCT + 1)
                            for d in range(2):
                                up = bank[:, j * T + d * P:j * T + (d + 1) * P]
                                dst = S[:, n % NCT, d, :]
                                if n == 0:
                                    ins = dve.tensor_copy(dst, up)
                                else:
                                    ins = dve.scalar_tensor_tensor(dst, S[:, (n - 1) % NCT, d, :], al[:, d, n:n + 1], up, MUL, ADD)
                                if d == 0:
                                    step(ins)
                            if n % 2 == 1 or n == NCH - 2:
                                ins.then_inc(free, 1)
                                freed(L, f"U{n // 2}")
                            else:
                                ins.then_inc(sem("state_ready"), 1)
                                dve.wait_ge(sem("state_ready"), (NCH // 2 - 1) * L + n // 2 + 1)

                scaled(2), scaled(3)
                split(L, "g3")
                masked(4), masked(5)
                dve.wait_ge(sem("pooled"), NG * (L + 1))
                diff(0, 0)
                scaled(4), scaled(5)
                split(L, "g4")
                masked(6), masked(7)
                diff(0, 1)
                times_q(0, 0)
                scaled(6), scaled(7)
                times_q(0, 1)
                split(L, "g5")
                dve.wait_ge(sem("al_ready"), L + 1)
                dve.wait_ge(sem("qdm_ready"), L + 1)
                scores_in_chunk(0)
                diff(1, 0)
                split(L, "g6")
                diff(1, 1)
                keys_by_chunk(0)
                times_q(1, 0)
                states(0)
                split(L, "g7")
                times_q(1, 1)
                scores_in_chunk(1)
                split(L, "g8")
                keys_by_chunk(1)
                split(L, "g9")
                states(1)
                split(L, "g10"), split(L, "g11")
                for i in range(2):
                    r = rms(L, 2 + i)
                    go = PS[:, 6 + i, :]
                    step(dve.scalar_tensor_tensor(gtmp[:, :, :], two(go), pcol("g_gla_out", L), r[:, :, :], MUL, MUL))
                    y = ys[:, KB + 2 * i:KB + 2 * i + 2, :]
                    dve.scalar_tensor_tensor(y, gtmp[:, :, :], 0.5, y, MUL, MUL).then_inc(sem("yb_ready"), 1)
                    dve.wait_ge(sem("yb_ready"), 2 * L + i + 1)
                for n in (0, 2, 1):
                    for m in range(4):
                        bank, free = full(L, f"b{n}{m}")
                        g = gates[:, n * KD + 2 * m:n * KD + 2 * m + 2, :]
                        dst = merged[:, 2 * m:2 * m + 2, :]
                        if n == 0:
                            dve.scalar_tensor_tensor(dst, g, 1.0, two(bank), ADD, MUL).then_inc(free, 1)
                        else:
                            dve.scalar_tensor_tensor(g, g, 1.0, two(bank), ADD, MUL).then_inc(free, 1)
                            freed(L, f"b{n}{m}")
                            ins = dve.tensor_tensor(dst, dst, g, ADD)
                            if n == 2:
                                step(ins)
                            else:
                                ins.then_inc(sem("merged"), 1)
                for m in range(4):
                    bank, free = full(L, f"w{m}")
                    x = xT[:, 2 * m:2 * m + 2, :]
                    dve.scalar_tensor_tensor(x, two(bank), 0.5, x, MUL, ADD).then_inc(free, 1)
                    if m < NSPLIT:
                        rest_lo(dve, NDENSE * L, m)
                norm_x(L, "ssf", "g_ffn")

            def dense(u, first=False):
                def gate_up(g):
                    g0, gn = GROUPS[g]
                    if g > 0 or not first:
                        dve.wait_ge(sem("hid_hi_ready"), len(GROUPS) * u + g)
                    for t in range(gn):
                        dve.wait_ge(sem("sil_ready"), FT * u + g0 + t + 1)
                        dve.tensor_tensor(hidf[:, t, :], sil[:, t, :], PS[:, (g0 + t) % DB, T:2 * T], MUL)\
                           .then_inc(sem("hidf_ready"), 1)
                    dve.wait_ge(sem("hid_hi_ready"), len(GROUPS) * u + g + 1)
                    dve.tensor_tensor(hid_lo[:, g0:g0 + gn, :], hidf[:, 0:gn, :], hid_hi[:, g0:g0 + gn, :].bitcast(F32), SUB)\
                       .then_inc(sem("hid_lo_ready"), 1)

                for j in range(HALVES):
                    for _, g in DENSE_AFTER.get(j - NSPLIT, ()):
                        gate_up(g)
                    if not (first and j < NSPLIT):
                        rest_lo(dve, u, j)

            mixer(0)
            dense(0, first=True)
            with dve.Fori(1, NDENSE) as i:
                dense(i)
            wait_used(dve, NDENSE - 1, HALVES - 1)
            for c in range(4):
                x = xT[:, 2 * c:2 * c + 2, :]
                dve.tensor_tensor(x, x, two(PS[:, 4 + c, :]), ADD).then_inc(sem("x_dense"), 1)
            mixer(1)

            dve.wait_ge(sem("logits_full"), 1)
            step(dve.tensor_copy(lg[:, :, :], PS[:, 0, 0:TT * NE].rearrange("p (a e) -> p a e", a=TT)))
            for a in range(TT):
                step(dve.max(rt8[:, a, :], lg[:, a, :]))
                step(dve.max_index(ri8[:, a, :], rt8[:, a, :], lg[:, a, :]))
            step(dve.tensor_copy(rf8[:, :, :], ri8[:, :, :]))
            dve.tensor_tensor(rsm[:, 0:2], rt8[:, :, 1], rt8[:, :, 0], SUB).then_inc(sem("logit_gap"), 1)
            for a in range(TT):
                for j in range(2):
                    step(dve.tensor_scalar(m12[:, a, j, :], iot8[:, :], rf8[:, a, j:j + 1], None, ALU.is_equal))
            dve.tensor_tensor(msel[:, :, :], m12[:, :, 0, :], m12[:, :, 1, :], ADD).then_inc(sem("msel_ready"), 1)
            dve.wait_ge(sem("msel_ready"), 1)
            dve.wait_ge(sem("top_exp"), 1)
            step(dve.tensor_scalar(rsm[:, 4:6], rsm[:, 2:4], 1.0, None, ADD))
            step(dve.reciprocal(rsm[:, 4:6], rsm[:, 4:6]))
            step(dve.tensor_tensor(rsm[:, 6:8], rsm[:, 2:4], rsm[:, 4:6], MUL))
            for a in range(TT):
                step(dve.tensor_scalar(wt[:, a, :], m12[:, a, 1, :], rsm[:, 6 + a:7 + a], None, MUL))
                step(dve.scalar_tensor_tensor(wt[:, a, :], m12[:, a, 0, :], rsm[:, 4 + a:5 + a], wt[:, a, :], MUL, ADD))
            for c in range(4):
                dve.wait_ge(sem("htok_full"), c + 1)
                dve.tensor_copy(htok[:, c // 2, (c % 2) * 512:(c % 2 + 1) * 512], PS[:, 2 + c, :]).then_inc(sem("htok_ready"), 1)
            dve.wait_ge(sem("rank_full"), 1)
            rank = PS[:, 1, 0:TT * NE].rearrange("p (a e) -> p a e", a=TT)
            step(dve.scalar_tensor_tensor(pos[:, :, :], rank, BIG, msel[:, :, :], ADD, MUL))
            step(dve.tensor_scalar(pos[:, :, :], pos[:, :, :], BIG, None, SUB))
            step(dve.tensor_reduce(rsm[:, 8:9], PS[:, 1, TT * NE:(TT + 1) * NE], AX.X, MAX))
            step(dve.tensor_scalar(rsm[:, 9:10], rsm[:, 8:9], float(CAP), 1.0, ALU.is_gt, ADD))
            for r in range(2, PASSES):
                step(dve.scalar_tensor_tensor(rsm[:, 9:10], rsm[:, 8:9], float(r * CAP), rsm[:, 9:10], ALU.is_gt, ADD))
            dve.tensor_copy(npi[:, :], rsm[:, 9:10]).then_inc(sem("passes_known"), 1)

            def tokens(r, e, n):
                for c in range(2):
                    b, uses = gather_use(r, e - 1, c)
                    dve.wait_ge(sem("hTe_hi_ready"), 2 * n + c + 1)
                    k = slice(4 * c, 4 * c + 4)
                    dve.tensor_tensor(hTe_lo[:, k, :], PS[:, 4 + b, 0:4 * CAP].rearrange("p (k c) -> p k c", k=4),
                                      hTe_hi[:, k, :].bitcast(F32), SUB).then_inc(sem(f"aux_free{b}"), 1)

            def rows_out(n):
                wait_used(dve, NDENSE + n, HALVES - 1)
                dve.tensor_copy(ye[:, 512:1024], PS[0:CAP, 7, :]).then_inc(sem("ye_dve"), 1)

            def added(uses):
                for c in range(4):
                    wait_aux_full(dve, c % 2, uses + c // 2)
                    x = xT[:, 2 * c:2 * c + 2, :]
                    dve.tensor_tensor(x, x, two(PS[:, 4 + c % 2, :]), ADD).then_inc(sem(f"aux_free{c % 2}"), 1)

            def expert(r, e, n, first=False, last=False):
                u = NDENSE + n
                for j in range(HALVES):
                    if j == 2 and not first:
                        rows_out(n - 1)
                    for what, g in EXPERT_AFTER.get(j - NSPLIT, ()):
                        g0, gn = GROUPS[g]
                        if what == "gu":
                            dve.wait_ge(sem("sile_ready"), len(GROUPS) * n + g + 1)
                            dve.tensor_tensor(hide[:, g % 2, 0:gn * P], sile[:, g % 2, 0:gn * P],
                                              PS[0:CAP, 2 * (g % 2) + 1, 0:gn * P], MUL).then_inc(sem("hide_ready"), 1)
                        elif what == "tr":
                            b, _ = turn_use(r, e, g, last)
                            dve.wait_ge(sem("hdT_hi_ready"), len(GROUPS) * n + g + 1)
                            dve.tensor_tensor(hdT_lo[:, g0:g0 + gn, :],
                                              PS[:, 4 + b, 0:gn * CAP].rearrange("p (k c) -> p k c", k=gn),
                                              hdT_hi[:, g0:g0 + gn, :].bitcast(F32), SUB).then_inc(sem(f"aux_free{b}"), 1)
                        elif what == "scatter" and not first:
                            added(scatter_use(r, e))
                        elif what == "gather" and not last:
                            tokens(r, e + 1, n + 1)
                    if not (j < NSPLIT and isinstance(n, int) and n == 0):
                        rest_lo(dve, u, j)

            def one_pass(r):
                n = r * NE
                for a in range(TT):
                    step.plain(dve.tensor_tensor(psel[:, a], slots[:, :].unsqueeze(1).broadcast_to([P, NE, CAP]),
                                                 pos[:, a, :].unsqueeze(2).broadcast_to([P, NE, CAP]), ALU.is_equal),
                               sem("psel_step"), 2 * r + a + 1)
                    dve.tensor_tensor(wsel[:, a], psel[:, a], wt[:, a, :].unsqueeze(2).broadcast_to([P, NE, CAP]), MUL)\
                       .then_inc(sem("sel_ready"), 1)
                dve.tensor_scalar(pos[:, :, :], pos[:, :, :], float(CAP), None, SUB).then_inc(sem("pos_step"), 1)
                dve.wait_ge(sem("pos_step"), r + 1)
                tokens(r, 0, n)
                expert(r, 0, n, first=True)
                with dve.Fori(1, NE - 1) as e:
                    expert(r, e, n + e)
                expert(r, NE - 1, n + NE - 1, last=True)
                rows_out(n + NE - 1)
                added(scatter_use(r, NE))

            one_pass(0)
            dve.wait_ge(sem("passes_known"), 1)
            npass = dve.value_load(npi[0:1, 0:1], min_val=1, max_val=PASSES)
            with dve.If(npass > 1):
                with dve.Fori(1, npass) as r:
                    one_pass(r)


class Chain:

    def __init__(self, eng, sem):
        self.eng, self.sem, self.n = eng, sem, 0

    def __call__(self, ins):
        ins.then_inc(self.sem, 1)
        self.n += 1
        self.wait()

    def wait(self):
        self.eng.wait_ge(self.sem, self.n)

    def plain(self, ins, sem, value):
        ins.then_inc(sem, 1)
        self.eng.wait_ge(sem, value)


_INS = ["x", "positions", "g_mix", "w_in", "g_cq", "w_uq", "g_ckv", "w_ukv", "g_qk_q", "g_qk_k", "w_gla_gate_up",
        "b_gla_gate", "g_gla_out", "w_pool", "pool_scale", "w_branch", "w_out", "g_ffn", "w_ffn_gate", "w_ffn_up",
        "w_ffn_down", "w_router", "w_exp_gate", "w_exp_up", "w_exp_down"]


def kernel(**inputs):
    import numpy as _np
    import concourse.bacc as _bacc
    from concourse import mybir as _mybir
    from concourse.bass_utils import run_bass_kernel_spmd as _run

    nc = _bacc.Bacc("TRN2", target_bir_lowering=False, num_devices=1)
    arrays, aps = {}, {}
    for name in _INS:
        a = _np.ascontiguousarray(inputs[name])
        arrays[f"in_{name}_dram"] = a
        aps[name] = nc.dram_tensor(f"in_{name}_dram", a.shape, _mybir.dt.from_np(a.dtype), kind="ExternalInput").ap()
    out = nc.dram_tensor("out_dram", (1, T, D), _mybir.dt.float32, kind="ExternalOutput").ap()
    hybrid_trunk(nc, aps, out)
    r = _run(nc, [arrays], core_ids=[0])
    return r.results[0]["out_dram"]
```

```python
import concourse.bass as bass
from concourse import mybir
from contextlib import ExitStack
import numpy as np

D, T, DEPTH, P = 1024, 256, 2, 128
KD = D // P
TT = T // P
H, NOPE, ROPE, DV = 8, 64, 32, 64
QK = NOPE + ROPE
HALF = ROPE // 2
RANK = D // 4
KR = RANK // P
GH, GDK, GDV, GRANK, GC = 4, 64, 128, 16, 16
TAU = 16.0
NCH = T // GC
NCT = P // GC
WINDOWS = (2, 4, 8, 16)
NG = len(WINDOWS)
NBR, BW = 3, 512
KB = BW // P
DFF, NE, DE = 2816, 8, 1408
EPS = 1e-6
ROPE_BASE = 10000.0
BIG = 1024.0
NEG = -1e30

C_Q, C_KV, C_KR = 0, RANK, 2 * RANK
C_GQ = C_KR + ROPE
C_GK = C_GQ + GH * GDK
C_GV = C_GK + GH * GDK
C_LR = C_GV + GH * GDV
C_OG = C_LR + GRANK
C_U = C_OG + GH * GDV
C_G = C_U + NG * P

UF = DE
FT = UF // P
GROUPS = [(0, 3), (3, 3), (6, 3), (9, 2)]
UNIT_LOADS = ["G0", "U0", "G1", "U1", "D0", "G2", "U2", "D1", "G3", "U3", "D2", "D3"]
NDENSE = DFF // UF
CAP = 96
PASSES = -(-T // CAP)

HALVES = 2 * len(UNIT_LOADS)
NSPLIT = 3
PERH = HALVES // NSPLIT
HALF_OF = {f"{c}{g}": 2 * UNIT_LOADS.index(f"{c}{g}") for c in "GUD" for g in range(len(GROUPS))}
DENSE_AFTER = {HALF_OF[f"U{g}"] + 1: [("gu", g)] for g in range(4)}
EXPERT_AFTER = {3: [("gu", 0), ("scatter", 0)], 5: [("scatter", 1), ("tr", 0)], 7: [("gu", 1)], 11: [("tr", 1)], 13: [("gu", 2)],
                17: [("tr", 2)], 19: [("gu", 3), ("gather", 0)], 20: [("tr", 3)]}
DB = 4
PASS_USES = 42


def scatter_use(r, e):
    return PASS_USES * r + (5 * e + 1 if not (isinstance(e, int) and e == NE) else PASS_USES - 2)


def turn_use(r, e, g, last=False):
    base = PASS_USES * r + 5 * e + 3
    return (g % 2, base + (g // 2 if g < 3 else (1 if last else 2)))


def gather_use(r, e, c):
    if isinstance(e, int) and e < 0:
        return (1 - c, PASS_USES * r)
    return (1 - c, PASS_USES * r + 5 * e + 3 + 1 + c)


SLOT, NSLOT = 3072, 4
GB = P * max(n for _, n in GROUPS)
MB = 256
PIECES = 4

PARAMS = [("g_mix", DEPTH * KD), ("g_ffn", DEPTH * KD), ("g_cq", DEPTH * KR), ("g_ckv", DEPTH * KR),
          ("b_gla_gate", DEPTH * 2), ("g_gla_out", DEPTH), ("pool_scale", DEPTH * NG),
          ("g_qk_q", DEPTH), ("g_qk_k", DEPTH)]
PCOL, NPAR = {}, 0
for _n, _k in PARAMS:
    PCOL[_n] = NPAR
    NPAR += _k

LOADS = (["cq", "ckv", "gq", "gk", "uq", "va", "ukv", "vb", "oga", "ogb", "ua", "ub"]
         + [f"g{i}" for i in range(5)] + ["pool"] + [f"g{i}" for i in range(5, 12)]
         + ["br00", "br01", "br20", "br21", "br10", "br11"] + ["out0", "out1", "out2", "out3"])
NL = len(LOADS)
LAST_USE = {"uq": "q3", "ukv": "vm1", "pool": "pl1"}
W_IN = {"cq": (C_Q, 256), "ckv": (C_KV, 288), "gq": (C_GQ, 256), "gk": (C_GK, 256),
        "va": (C_GV, 256), "vb": (C_GV + 256, 272), "oga": (C_OG, 256), "ogb": (C_OG + 256, 256),
        "ua": (C_U, 256), "ub": (C_U + 256, 256), **{f"g{b}": (C_G + b * MB, MB) for b in range(12)}}
BRANCH_LOADS = [f"br{n}{hf}" for n in (0, 2, 1) for hf in range(2)]
SPLIT = list(W_IN) + BRANCH_LOADS + [f"out{m}" for m in range(4)]
SPLIT_NO = {name: i for i, name in enumerate(SPLIT)}
READER = {**{x: x for x in W_IN}, "ckv": "kr", "vb": "lr", **{x: f"b{x[2]}{2 * int(x[3]) + 1}" for x in BRANCH_LOADS},
          **{f"out{m}": f"w{m}" for m in range(4)}}
PIECE_WORDS = {x: KD // PIECES * W_IN[x][1] if x in W_IN else 512 for x in SPLIT}
assert len(UNIT_LOADS) % NSLOT == 0


def filled(segment, s):
    mixer, per = len(range(s, NL, NSLOT)), len(UNIT_LOADS) // NSLOT
    return [0, mixer, mixer + NDENSE * per, 2 * mixer + NDENSE * per][segment]


NB = 6
PRE_USES = ["x0", "x1", "x2", "x3"]
MIX_USES = (["ssm", "cq", "ckv", "kr", "gq", "sslat", "gk"] + [f"q{i}" for i in range(4)] + ["va"]
            + [f"k{i}" for i in range(4)] + ["vm0", "vm1", "vb", "lr", "oga", "ssq"]
            + ["z", "rk", "ogb"] + [f"ssk{i}" for i in range(4)]
            + ["ua"] + [f"rq{i}" for i in range(4)] + ["ub"]
            + ["g0", "s0", "s1", "g1", "pt0", "pt1", "s2", "s3", "g2", "o0", "pt2", "pt3", "s4", "s5",
               "g3", "o1", "pt4", "pt5", "s6", "s7", "g4", "o2", "pt6", "pt7", "kd0", "pl0", "pl1", "g5", "A0", "g6"]
            + [f"U{i}" for i in range(4)] + ["o3", "g7", "A1", "g8", "kd1", "g9"]
            + [f"U{i}" for i in range(4, 8)] + ["g10", "g11", "ssg0", "ssg1"]
            + [f"b{n}{m}" for n in (0, 2, 1) for m in range(4)] + [f"w{m}" for m in range(4)] + ["ssf"])
USES = [(-1, u) for u in PRE_USES] + [(0, MIX_USES[0]), (-1, "par"), (-1, "inv")]
USES += [(0, u) for u in MIX_USES[1:]] + [(1, u) for u in MIX_USES]
USE = {u: i for i, u in enumerate(USES)}
MIX_END = [len(USES) - len(MIX_USES), len(USES)]


def hybrid_trunk(nc, A, out):
    F32, F32R, I32, U32, BF16 = (mybir.dt.float32, mybir.dt.float32r, mybir.dt.int32, mybir.dt.uint32,
                                 mybir.dt.bfloat16)
    ALU, ACT, AX = mybir.AluOpType, mybir.ActivationFunctionType, mybir.AxisListType
    ADD, SUB, MUL, MAX, MIN = ALU.add, ALU.subtract, ALU.mult, ALU.max, ALU.min

    ctx = ExitStack()
    with ctx:
        def sb(name, shape, dt=F32):
            return ctx.enter_context(nc.sbuf_tensor(name, shape, dt))

        def over(*wanted):
            with ExitStack() as tmp:
                return [tmp.enter_context(nc.sbuf_tensor(name, shape, dt)) for name, shape, dt in wanted]

        sems = {}

        def sem(name):
            if name not in sems:
                sems[name] = ctx.enter_context(nc.semaphore(name))
            return sems[name]

        ring = sb("ring", [P, NSLOT, SLOT])
        xT = sb("xT", [P, KD, T])
        h_hi = sb("h_hi", [P, KD, T], F32R)
        h_lo = sb("h_lo", [P, KD, T], F32R)
        m_hi = sb("m_hi", [P, PIECES, 576], F32R)
        m_lo = sb("m_lo", [P, PIECES, 576], F32R)
        rt = sb("rt", [P, 2, T])
        rr = sb("rr", [P, 2, T])
        big = sb("big", [P, 24 * T])
        gates = big[:, :].rearrange("p (n t) -> p n t", t=T)
        lat, latn, sq, sk = gates[:, 0:4], gates[:, 4:8], gates[:, 8:16], gates[:, 16:24]
        hT = gates[:, 0:KD]
        xin = big[:, 0:TT * D].rearrange("p (a d) -> p a d", a=TT)
        w_hi, w_lo = over(("w_hi", [P, NSPLIT, SLOT // 2], F32R), ("w_lo", [P, NSPLIT, SLOT // 2], F32R))
        gq = sb("gq", [P, 2, T])
        gk = sb("gk", [P, 2, T])
        gvt = sb("gvt", [P, TT, GH * GDV])
        th = sb("th", [P, 2, T])
        vt = sb("vt", [P, TT, H * DV])
        ys = sb("ys", [P, NBR * KB, T])
        Pr = sb("Pr", [P, 3, 3 * P])
        PT = sb("PT", [P, 2, 3 * P])
        kdec = sb("kdec", [P, 2, T])
        bc = sb("bc", [P, 2, T])
        attn = sb("attn", [P, GH, P])
        rows3 = sb("rows3", [P, 3, T])
        krope = rows3[:, 2, :]
        glr = rows3[0:GRANK, 2, :]
        PADW = max(WINDOWS)
        u = sb("u", [P, NG, PADW + T])
        hid_hi, = over(("hid_hi", [P, FT, T], F32R))
        hTe_hi, hTe_lo, hdT_hi, hdT_lo = over(*((n, [P, k, CAP], F32R) for n, k in (
            ("hTe_hi", KD), ("hTe_lo", KD), ("hdT_hi", FT), ("hdT_lo", FT))))
        _, yA_hi, yA_lo = over(("scr_low", [P, 2048], F32), ("yA_hi", [P, KB, T], F32R), ("yA_lo", [P, KB, T], F32R))
        scr = sb("scr", [P, 4096])
        E = scr[:, :].rearrange("p (d c n j) -> p d c n j", d=2, n=NCT, c=GC)
        pwa = scr[:, 0:NG * (PADW + T)].rearrange("p (g t) -> p g t", g=NG)
        pwb = scr[:, 2048:2048 + NG * (PADW + T)].rearrange("p (g t) -> p g t", g=NG)
        merged = scr[:, 0:KD * T].rearrange("p (k t) -> p k t", k=KD)
        ztmp = scr[:, 2048:4096].rearrange("p (k t) -> p k t", k=8)
        hid_lo, = over(("hid_lo", [P, FT, T], F32R))
        mg_hi, mg_lo = over(("mg_hi", [P, KD, T], F32R), ("mg_lo", [P, KD, T], F32R))
        _, yB_hi, yB_lo = over(("qk_low", [P, 2048], F32), ("yB_hi", [P, KB, T], F32R), ("yB_lo", [P, KB, T], F32R))
        y_parts = {0: (yA_hi, yA_lo), 2: (yB_hi, yB_lo), 1: (yA_hi, yA_lo)}
        qk = sb("qk", [P, 4096])
        q = qk[0:QK, 0:2048].rearrange("p (h t) -> p h t", h=H)
        k = qk[0:QK, 2048:4096].rearrange("p (h t) -> p h t", h=H)
        gsq = qk[:, 0:4 * T].rearrange("p (a b t) -> p a b t", a=2, b=2)
        kdm = qk[:, 0:2048].rearrange("p (n f) -> p n f", n=NCT)
        S = qk[:, 2048:4096].rearrange("p (n d v) -> p n d v", n=NCT, d=2)
        rqs = sb("rqs", [P, TT * H])
        small = sb("small", [P, 64])
        qdm = sb("qdm", [P, 2, 2, T])
        al = sb("al", [P, 2, NCH])
        ident = sb("ident", [P, P])
        ones = sb("ones", [P, P])
        zb = sb("zb", [P, P], BF16)
        maskc = sb("maskc", [P, 3 * P])
        maskg = sb("maskg", [P, P])
        chm = sb("chm", [P, NCT])
        keep = sb("keep", [P, T])
        winf = sb("winf", [P, NG, PADW])
        selh = sb("selh", [P, 2])
        R = sb("R", [QK, QK])
        cs = rows3[:, 0:2, :]
        par = sb("par", [P, NPAR])
        eps = sb("eps", [P, 2])
        one1 = sb("one1", [1, 1])
        invr = sb("invr", [1, QK])
        invc = sb("invc", [QK, 1])
        ang = scr[0:QK, T:5 * T].rearrange("p (a t) -> p a t", a=4)
        cnt = scr[:, 0:PADW].bitcast(I32)
        sloti = scr[:, PADW:PADW + CAP].bitcast(I32)
        eb = attn[:, :, :].rearrange("p h i -> p (h i)").rearrange("p (d t) -> p d t", d=2)
        ek = PT[:, :, :].rearrange("p a j -> p (a j)")[:, 0:2 * T].rearrange("p (d t) -> p d t", d=2)
        rq16 = small[:, 0:16]
        rk16 = small[:, 32:48]
        warmth = small[:, 60:61]
        mx = small[:, 16:20].rearrange("p (a b) -> p a b", a=2)
        nbs = small[:, 20:24].rearrange("p (a b) -> p a b", a=2)
        sums = small[:, 24:28].rearrange("p (a b) -> p a b", a=2)
        angk = ang[:, 3, :]
        rtmp = th[0:QK, :, :]
        gtmp = th
        sil = big[:, 4096:4096 + 3 * T].rearrange("p (f t) -> p f t", f=3)
        hidf = big[:, 5120:5120 + 3 * T].rearrange("p (f t) -> p f t", f=3)
        htok = qk[:, 0:TT * D].rearrange("p (a d) -> p a d", a=TT)
        selT = qk[0:CAP, 2048:2048 + NE * T].rearrange("p (e t) -> p e t", e=NE)
        psel = big[:, 0:TT * NE * CAP].rearrange("p (a e c) -> p a e c", a=TT, e=NE)
        wsel = big[:, 1536:1536 + TT * NE * CAP].rearrange("p (a e c) -> p a e c", a=TT, e=NE)
        ye = big[0:CAP, 3072:3072 + D]
        sile = big[0:CAP, 4096:4096 + 2 * GB].rearrange("p (f t) -> p f t", f=2)
        hide = big[0:CAP, 5120:5120 + 2 * GB].rearrange("p (f t) -> p f t", f=2)
        slots = sb("slots", [P, CAP])
        us = u[:, :, :].rearrange("p g t -> p (g t)")
        tri = us[:, 0:P]
        lg, rt8, rf8, msel, wt, pos = (us[:, P + i * TT * NE:P + (i + 1) * TT * NE].rearrange("p (a e) -> p a e", a=TT)
                                       for i in range(6))
        ri8 = us[:, 2 * P:2 * P + TT * NE].bitcast(U32).rearrange("p (a e) -> p a e", a=TT)
        m12 = us[:, 2 * P + 32:2 * P + 64].rearrange("p (a j e) -> p a j e", a=TT, j=2)
        iot8 = sb("iot8", [P, NE])
        wgu = rows3[0:GRANK, 0:DEPTH, :]
        posi = scr[0:QK, 5 * T:6 * T].bitcast(I32)
        wr = sb("wr", [P, KD, NE])
        rsm = sb("rsm", [P, 16])
        npi = sb("npi", [P, 1], I32)
        yout = big[:, 0:TT * D].rearrange("p (a d) -> p a d", a=TT)

        PS = ctx.enter_context(nc.psum_tensor("PS", [P, 8, 512], F32))

        def use(L, name):
            i = USE[(L, name)]
            return PS[:, i % NB, :], sem(f"bank_full{i % NB}"), sem(f"bank_free{i % NB}"), i // NB

        def slot_of(L, name):
            i = LOADS.index(name)
            return i % NSLOT, filled(2 * L, i % NSLOT) + i // NSLOT + 1

        def half_buffer(u, j):
            return j % NSPLIT, PERH * u + j // NSPLIT + 1

        def wait_hi(eng, u, j):
            b, n = half_buffer(u, j)
            eng.wait_ge(sem(f"hi_ready{b}"), n)

        def wait_lo(eng, u, j):
            b, n = half_buffer(u, j)
            eng.wait_ge(sem(f"lo_ready{b}"), n)

        def wait_used(eng, u, j):
            b, n = half_buffer(u, j)
            eng.wait_ge(sem(f"split_used{b}"), n)

        def half_words(j):
            gn = GROUPS[int(UNIT_LOADS[j // 2][1])][1]
            n = gn * D // 2
            return n, (j % 2) * n

        def round_hi(act, u, j, kind, n):
            b, uses = half_buffer(u, j)
            i = j // 2
            act.wait_ge(sem(f"slot_full{i % NSLOT}"), 16 * (PER * n + filled(2 * kind + 1, i % NSLOT) + i // NSLOT + 1))
            if not isinstance(uses, int) or uses > 1:
                act.wait_ge(sem(f"split_used{b}"), uses - 1)
            words, w0 = half_words(j)
            act.activation(w_hi[:, b, 0:words], ring[:, i % NSLOT, w0:w0 + words], ACT.Copy)\
               .then_inc(sem(f"hi_ready{b}"), 1)

        def rest_lo(dve, u, j):
            b, _ = half_buffer(u, j)
            wait_hi(dve, u, j)
            words, w0 = half_words(j)
            dve.tensor_tensor(w_lo[:, b, 0:words], ring[:, (j // 2) % NSLOT, w0:w0 + words],
                              w_hi[:, b, 0:words].bitcast(F32), SUB).then_inc(sem(f"lo_ready{b}"), 1)

        def wait_aux_full(eng, b, n):
            eng.wait_ge(sem(f"aux_full{b}"), n + 1)

        def wait_aux_free(eng, b, n):
            if not isinstance(n, int) or n > 0:
                eng.wait_ge(sem(f"aux_free{b}"), n)

        PER = len(UNIT_LOADS) // NSLOT

        def piece_done(eng, L, name, p):
            x = len(SPLIT) * L + SPLIT_NO[name] - 1
            if x < 0:
                return
            if p < PIECES - 1:
                eng.wait_ge(sem("piece_used"), (PIECES - 1) * x + p + 1)
            else:
                _, full, _, n = use(x // len(SPLIT), READER[SPLIT[x % len(SPLIT)]])
                eng.wait_ge(full, n + 1)

        def piece_no(L, name, p):
            return PIECES * (len(SPLIT) * L + SPLIT_NO[name]) + p

        def piece_of(L, name, p):
            n = PIECE_WORDS[name]
            s, _ = slot_of(L, name)
            return ring[:, s, p * n:(p + 1) * n], m_hi[:, p, 0:n], m_lo[:, p, 0:n]

        block = ctx.enter_context(nc.Block())

        @block.sync
        def _(sp):
            sp.dma_start(xin, A["x"].rearrange("b (a p) d -> p (b a) d", p=P)).then_inc(sem("x_in"), 16)

            w_in, w_uq, w_ukv = A["w_in"], A["w_uq"], A["w_ukv"]

            def kp(ap):
                return ap.rearrange("(k p) c -> p k c", p=P)

            def mixer_read(L, name):
                if name in SPLIT:
                    sp.wait_ge(sem("m_lo_ready"), piece_no(L, name, PIECES - 1) + 1)
                    return
                _, full, _, n = use(L, LAST_USE[name])
                sp.wait_ge(full, n + 1)

            def unit_read(u, i):
                wait_lo(sp, u, 2 * i + 1)

            def mixer_load(L, name):
                s, _ = slot_of(L, name)
                i = LOADS.index(name)
                if i == NSLOT - 1 and L == 0:
                    sp.wait_ge(use(-1, "par")[1], 1)
                if i >= NSLOT:
                    mixer_read(L, LOADS[i - NSLOT])
                elif L > 0:
                    unit_read(NDENSE - 1, len(UNIT_LOADS) - NSLOT + i)

                def put(src, cols, first=0):
                    kk = src.shape[0] // P
                    dst = ring[:, s, first:first + kk * cols].rearrange("p (k c) -> p k c", k=kk)
                    sp.dma_start(dst, kp(src)).then_inc(sem(f"slot_full{s}"), 16)

                if name in W_IN:
                    c0, cn = W_IN[name]
                    put(w_in[L, :, c0:c0 + cn], cn)
                elif name == "uq":
                    put(w_uq[L], H * QK)
                elif name == "ukv":
                    put(w_ukv[L], H * (NOPE + DV))
                elif name == "pool":
                    dst = ring[:, s, 0:NG * P].rearrange("p (g c) -> p g c", g=NG)
                    sp.dma_start(dst, A["w_pool"][L].rearrange("g p c -> p g c")).then_inc(sem(f"slot_full{s}"), 16)
                elif name[:2] == "br":
                    n, hf = int(name[2]), int(name[3])
                    put(A["w_branch"][L, n, :, hf * 512:(hf + 1) * 512], 512)
                else:
                    m = int(name[3])
                    put(A["w_out"][L, :, m * MB:(m + 1) * MB], MB)

            def unit_loads(kind, wg, wu, wd, x, uo):
                u = kind * NDENSE + uo
                wg, wu, wd = wg[x], wu[x], wd[x]
                for i, name in enumerate(UNIT_LOADS):
                    s = i % NSLOT
                    g0, gn = GROUPS[int(name[1])]
                    if i >= NSLOT:
                        unit_read(u, i - NSLOT)
                    elif isinstance(uo, int) and uo == 0:
                        mixer_read(kind, LOADS[max(x for x in range(NL) if x % NSLOT == i)])
                    else:
                        unit_read(u - 1, len(UNIT_LOADS) - NSLOT + i)
                    if name[0] == "D":
                        src = wd[g0 * P:(g0 + gn) * P, :].rearrange("(k p) c -> p k c", p=P)
                        dst = ring[:, s, 0:gn * D].rearrange("p (k c) -> p k c", k=gn)
                    else:
                        w = wg if name[0] == "G" else wu
                        src = w[:, g0 * P:(g0 + gn) * P].rearrange("(k p) c -> p k c", p=P)
                        dst = ring[:, s, 0:KD * gn * P].rearrange("p (k c) -> p k c", k=KD)
                    sp.dma_start(dst, src).then_inc(sem(f"slot_full{s}"), 16)

            for name in LOADS:
                mixer_load(0, name)
            fg = A["w_ffn_gate"][0].rearrange("k (u c) -> u k c", c=UF)
            fu = A["w_ffn_up"][0].rearrange("k (u c) -> u k c", c=UF)
            fd = A["w_ffn_down"][0].rearrange("(u k) c -> u k c", k=UF)
            unit_loads(0, fg, fu, fd, 0, 0)
            with sp.Fori(1, NDENSE) as i:
                unit_loads(0, fg, fu, fd, i, i)
            for name in LOADS:
                mixer_load(1, name)
            eg, eu, ed = A["w_exp_gate"][0], A["w_exp_up"][0], A["w_exp_down"][0]
            unit_loads(1, eg, eu, ed, 0, 0)
            with sp.Fori(1, NE) as e:
                unit_loads(1, eg, eu, ed, e, e)
            sp.wait_ge(sem("passes_known"), 1)
            npass = sp.value_load(npi[0:1, 0:1], min_val=1, max_val=PASSES)
            with sp.If(npass > 1):
                with sp.Fori(1, npass) as r:
                    with sp.Fori(0, NE) as e:
                        unit_loads(1, eg, eu, ed, e, r * NE + e)
            y = out.rearrange("b (a p) d -> p (b a) d", p=P)
            for i in range(4):
                sp.wait_ge(sem("y_out"), i + 1)
                c = slice((i % 2) * 512, (i % 2 + 1) * 512)
                sp.dma_start(y[:, i // 2, c], yout[:, i // 2, c]).then_inc(sem("stored"), 16)
            sp.wait_ge(sem("stored"), 64)

        @block.tensor
        def _(pe):
            def begin(L, name):
                bank, full, free, n = use(L, name)
                if n >= 1:
                    pe.wait_ge(free, n)
                return bank, full

            def weights(L, name):
                s, r = slot_of(L, name)
                pe.wait_ge(sem(f"slot_full{s}"), 16 * r)
                return s

            def wslot(s, kk, cols):
                return ring[:, s, 0:kk * cols].rearrange("p (k c) -> p k c", k=kk)

            def evacuated(L, name):
                _, _, free, n = use(L, name)
                pe.wait_ge(free, n + 1)

            def project(dst, w, c0, m, rhs, kk=KD):
                for i in range(kk):
                    mm = pe.matmul(dst, w[:, i, c0:c0 + m], rhs(i), start=(i == 0), stop=(i == kk - 1))
                return mm

            def sumsq(L, name, layer):
                bank, full = begin(L, name)
                for i in range(4):
                    pe.wait_ge(sem("sq_act" if i % 2 == 0 else "sq_dve"), 2 * (2 * layer + (name == "ssf")) + i // 2 + 1)
                    for j in range(2):
                        kt = 2 * i + j
                        mm = pe.matmul(bank[:, 0:T], ones[:, :], sq[:, kt, :], start=(kt == 0), stop=(kt == KD - 1))
                mm.then_inc(full, 1)

            def by_pieces(L, name, groups, x_hi=h_hi, x_lo=h_lo, ready=None):
                cols = 512 if name in BRANCH_LOADS else W_IN[name][1] if name in W_IN else MB
                per = PIECE_WORDS[name] // cols
                for p in range(PIECES):
                    if ready:
                        pe.wait_ge(ready[0], ready[1] + p)
                    pe.wait_ge(sem("m_lo_ready"), piece_no(L, name, p) + 1)
                    pe.wait_ge(sem("m_hi_ready"), piece_no(L, name, p) + 1)
                    _, hi, lo = piece_of(L, name, p)
                    hi, lo = (x.rearrange("p (k c) -> p k c", c=cols) for x in (hi, lo))
                    for full, dsts in groups:
                        for x, (dst, c0, m, a) in enumerate(dsts):
                            for k in range(per):
                                kt = p * per + k
                                if name == "cq":
                                    pe.wait_ge(sem("h_lo_ready"), KD // 2 * 2 * L + kt // 2 + 1)
                                w = slice(c0, c0 + m)
                                t = slice(0, T) if a is None else slice(a * P, (a + 1) * P)
                                whi, wlo, xhi, xlo = hi[:, k, w], lo[:, k, w], x_hi[:, kt, t], x_lo[:, kt, t]
                                for y, (ww, xx) in enumerate(((whi, xhi), (whi, xlo), (wlo, xhi))):
                                    l, r = (ww, xx) if a is None else (xx, ww)
                                    mm = pe.matmul(dst, l, r, start=(kt == 0 and x == 0 and y == 0),
                                                   stop=(kt == PIECES * per - 1 and y == 2), skip_group_check=True)
                        if p == PIECES - 1:
                            mm.then_inc(full, 1)
                    if p < PIECES - 1:
                        mm.then_inc(sem("piece_used"), 1)

            def pair(L, name):
                bank, full = begin(L, name)
                by_pieces(L, name, [(full, [(bank[:, j * T:(j + 1) * T], j * P, P, None) for j in range(2)])])

            def by_tokens(L, name):
                bank, full = begin(L, name)
                return (full, [(bank[:, a * 256:(a + 1) * 256], 0, 256, a) for a in range(TT)])

            pe.wait_ge(sem("ident_ready"), 1)
            pe.wait_ge(sem("x_in"), 16)
            for i in range(4):
                bank, full = begin(-1, f"x{i}")
                for j in range(2):
                    for a in range(TT):
                        mm = pe.transpose(bank[:, j * T + a * P:j * T + (a + 1) * P],
                                          xin[:, a, (2 * i + j) * P:(2 * i + j + 1) * P], ident[:, :])
                mm.then_inc(full, 1)

            def parameters():
                pe.wait_ge(sem("consts"), 1)
                pe.wait_ge(sem("params_in"), 16 * len(PARAMS))
                bank, full = begin(-1, "par")
                pe.transpose(bank[:, 0:NPAR], ring[0:NPAR, NSLOT - 1, 0:P], ident[0:NPAR, 0:NPAR]).then_inc(full, 1)
                bank, full = begin(-1, "inv")
                pe.matmul(bank[0:QK, 0:1], invr[:, :], one1[:, :], start=True, stop=True).then_inc(full, 1)

            def mixer(L):
                sumsq(L, "ssm", L)
                if L == 0:
                    parameters()
                pair(L, "cq")
                ckv, full = begin(L, "ckv")
                kr, kr_full = begin(L, "kr")
                by_pieces(L, "ckv", [(full, [(ckv[:, j * T:(j + 1) * T], j * P, P, None) for j in range(2)]),
                                     (kr_full, [(kr[0:QK, 0:T], 256 - NOPE, QK, None)])])
                pair(L, "gq")
                bank, full = begin(L, "sslat")
                evacuated(L, "ckv")
                for g in range(2):
                    for i in range(KR):
                        mm = pe.matmul(bank[:, g * T:(g + 1) * T], ones[:, :], sq[:, g * KR + i, :],
                                       start=(i == 0), stop=(i == KR - 1))
                mm.then_inc(full, 1)
                pair(L, "gk")
                s = weights(L, "uq")
                w = wslot(s, KR, H * QK)
                pe.wait_ge(sem("latn_ready"), 4 * L + KR)
                for i in range(4):
                    bank, full = begin(L, f"q{i}")
                    for j in range(2):
                        mm = project(bank[0:QK, j * T:(j + 1) * T], w, (2 * i + j) * QK, QK,
                                     lambda x: latn[:, x, :], KR)
                    mm.then_inc(full, 1)
                by_pieces(L, "va", [by_tokens(L, "va")])
                s = weights(L, "ukv")
                w = wslot(s, KR, H * (NOPE + DV))
                pe.wait_ge(sem("latn_ready"), 4 * L + 2 * KR)
                for i in range(4):
                    bank, full = begin(L, f"k{i}")
                    for j in range(2):
                        mm = project(bank[0:NOPE, j * T:(j + 1) * T], w, (2 * i + j) * (NOPE + DV), NOPE,
                                     lambda x: latn[:, KR + x, :], KR)
                    mm.then_inc(full, 1)
                wv = w.rearrange("p k (h c) -> p k h c", h=H)
                for a in range(TT):
                    bank, full = begin(L, f"vm{a}")
                    for i in range(KR):
                        mm = pe.matmul(bank[:, :], latn[:, KR + i, a * P:(a + 1) * P], wv[:, i, :, NOPE:NOPE + DV],
                                       start=(i == 0), stop=(i == KR - 1))
                    mm.then_inc(full, 1)
                vb = by_tokens(L, "vb")
                bank, full = begin(L, "lr")
                by_pieces(L, "vb", [vb, (full, [(bank[0:GRANK, 0:T], 256, GRANK, None)])])
                pair(L, "oga")
                bank, full = begin(L, "ssq")
                evacuated(L, "q3")
                evacuated(L, "k3")
                for c, src in enumerate((sq, sk)):
                    for a in range(TT):
                        for h in range(H):
                            x = c * TT * H + a * H + h
                            mm = pe.matmul(bank[:, x:x + 1], src[0:QK, h, a * P:(a + 1) * P], ones[0:QK, 0:1],
                                           start=True, stop=True)
                mm.then_inc(full, 1)
                bank, full = begin(L, "z")
                evacuated(L, "lr")
                pe.wait_ge(sem("gu_in"), 16)
                for d in range(2):
                    mm = pe.matmul(bank[:, d * T:(d + 1) * T], wgu[:, L, d * P:(d + 1) * P], glr[:, :],
                                   start=True, stop=True)
                mm.then_inc(full, 1)
                bank, full = begin(L, "rk")
                pe.wait_ge(sem("kg_ready"), L + 1)
                pe.matmul(bank[0:QK, 0:T], R[NOPE:QK, :], krope[NOPE:QK, :], start=True, stop=True).then_inc(full, 1)
                pair(L, "ogb")
                pe.wait_ge(sem("rk_ready"), L + 1)
                for i in range(4):
                    bank, full = begin(L, f"ssk{i}")
                    for j in range(2):
                        for a in range(TT):
                            x = a * H + 2 * i + j
                            mm = pe.matmul(bank[0:QK, j * T + a * P:j * T + (a + 1) * P], rk16[:, x:x + 1].broadcast_to([P, QK]),
                                           ident[:, :], start=True, stop=True)
                    mm.then_inc(full, 1)
                pair(L, "ua")
                for i in range(4):
                    bank, full = begin(L, f"rq{i}")
                    evacuated(L, f"q{i}")
                    pe.matmul(bank[0:QK, :], R[:, :], q[:, 2 * i:2 * i + 2, :], start=True, stop=True).then_inc(full, 1)
                pair(L, "ub")

                def gate(i):
                    pair(L, f"g{i}")

                def scores(h):
                    bank, full = begin(L, f"s{h}")
                    pe.wait_ge(sem("q_ready"), 4 * L + h // 2 + 1)
                    evacuated(L, f"ssk{h // 2}")
                    pe.matmul(bank[:, 0:P], q[:, h, 0:P], k[:, h, 0:P], start=True, stop=True)
                    pe.matmul(bank[:, P:3 * P], q[:, h, P:T], k[:, h, :], start=True, stop=True).then_inc(full, 1)

                def turn(h):
                    bank, full = begin(L, f"pt{h}")
                    pe.wait_ge(sem("p_ready"), H * L + h + 1)
                    for j in range(3):
                        mm = pe.transpose(bank[:, j * P:(j + 1) * P], Pr[:, h % 3, j * P:(j + 1) * P], ident[:, :])
                    mm.then_inc(full, 1)

                def values(i):
                    bank, full = begin(L, f"o{i}")
                    for j in range(2):
                        h = 2 * i + j
                        evacuated(L, f"pt{h}")
                        o = bank[j * DV:(j + 1) * DV, 0:T]
                        pe.matmul(o, vt[:, 0, h * DV:(h + 1) * DV], PT[:, j, 0:T], start=True, stop=False)
                        mm = pe.matmul(o[:, P:T], vt[:, 1, h * DV:(h + 1) * DV], PT[:, j, T:3 * P], start=False, stop=True)
                    mm.then_inc(full, 1)

                def intra(a):
                    bank, full = begin(L, f"A{a}")
                    for d in range(2):
                        pe.wait_ge(sem("e_ready"), 4 * L + 2 * a + d + 1)
                        for c in range(GC):
                            mm = pe.matmul(bank[:, c * GH + 2 * d:c * GH + 2 * d + 2], E[:, d, c, :, :], selh[:, :],
                                           start=True, stop=True)
                    mm.then_inc(full, 1)

                def turn_k(a):
                    bank, full = begin(L, f"kd{a}")
                    pe.wait_ge(sem("dec_ready"), L + 1)
                    for d in range(2):
                        mm = pe.transpose(bank[:, d * P:(d + 1) * P], kdec[:, d, a * P:(a + 1) * P], ident[:, :])
                    mm.then_inc(full, 1)

                def go(h, lo, hi):
                    return PS[:, 6 + h // 2, (h % 2) * T + lo:(h % 2) * T + hi]

                def within(a):
                    pe.wait_ge(sem("attn_ready"), 2 * L + a + 1)
                    for h in range(GH):
                        mm = pe.matmul(go(h, a * P, (a + 1) * P), gvt[:, a, h * GDV:(h + 1) * GDV], attn[:, h, :],
                                       start=(a == 0 and h % 2 == 0), stop=False, skip_group_check=True)
                    mm.then_inc(sem("attn_used"), 1)

                def updates(a):
                    pe.wait_ge(sem("kdm_ready"), 2 * L + a + 1)
                    for i in range(4):
                        bank, full = begin(L, f"U{4 * a + i}")
                        for j in range(1 if 4 * a + i == 7 else 2):
                            n = 2 * i + j
                            for h in range(GH):
                                mm = pe.matmul(bank[(h % 2) * GDK:(h % 2 + 1) * GDK,
                                                    j * T + (h // 2) * P:j * T + (h // 2 + 1) * P],
                                               kdm[:, n, h * GDK:(h + 1) * GDK], gvt[:, a, h * GDV:(h + 1) * GDV],
                                               start=True, stop=True)
                        mm.then_inc(full, 1)

                def across(a):
                    pe.wait_ge(sem("qdm_ready"), L + 1)
                    for n in range(max(1, a * NCT), (a + 1) * NCT):
                        m = n - 1
                        if m % 2 == 1 or m == NCH - 2:
                            evacuated(L, f"U{m // 2}")
                        else:
                            pe.wait_ge(sem("state_ready"), (NCH // 2 - 1) * L + m // 2 + 1)
                        for d in range(2):
                            mm = pe.matmul(PS[:, 6 + d, :].rearrange("p (h t) -> p h t", h=2)[:, :, n * GC:(n + 1) * GC],
                                           S[:, (n - 1) % NCT, d, :], qdm[:, :, d, n * GC:(n + 1) * GC],
                                           start=False, stop=(n == NCH - 1), skip_group_check=True)
                        if n < NCH - 1:
                            mm.then_inc(sem("state_used"), 1)
                    if a == 1:
                        mm.then_inc(sem("go_full"), 1)

                gate(0)
                scores(0), scores(1)
                gate(1)
                turn(0), turn(1)
                scores(2), scores(3)
                gate(2)
                values(0)
                turn(2), turn(3)
                scores(4), scores(5)
                gate(3)
                values(1)
                turn(4), turn(5)
                scores(6), scores(7)
                gate(4)
                values(2)
                turn(6), turn(7)
                turn_k(0)
                s = weights(L, "pool")
                pe.wait_ge(sem("pooled"), NG * (L + 1))
                for i in range(2):
                    bank, full = begin(L, f"pl{i}")
                    for j in range(2):
                        g = 2 * i + j
                        mm = pe.matmul(bank[:, j * T:(j + 1) * T], ring[:, s, g * P:(g + 1) * P], u[:, g, PADW:PADW + T],
                                       start=True, stop=True)
                    mm.then_inc(full, 1)
                gate(5)
                intra(0)
                gate(6)
                within(0)
                updates(0)
                values(3)
                gate(7)
                intra(1)
                gate(8)
                within(1)
                turn_k(1)
                gate(9)
                across(0)
                updates(1)
                gate(10)
                across(1)
                gate(11)
                for i in range(2):
                    bank, full = begin(L, f"ssg{i}")
                    pe.wait_ge(sem("gsq_ready"), 2 * L + i + 1)
                    pe.matmul(bank[:, :], ones[:, :], gsq[:, i, :, :], start=True, stop=True).then_inc(full, 1)
                for x, n in enumerate((0, 2, 1)):
                    for hf in range(2):
                        groups = []
                        for m in (2 * hf, 2 * hf + 1):
                            bank, full = begin(L, f"b{n}{m}")
                            groups.append((full, [(bank[:, j * T:(j + 1) * T], (m % 2) * 256 + j * P, P, None) for j in range(2)]))
                        pe.wait_ge(sem("y_lo_ready"), NBR * L + x + 1)
                        by_pieces(L, f"br{n}{hf}", groups, *y_parts[n])
                for m in range(4):
                    bank, full = begin(L, f"w{m}")
                    by_pieces(L, f"out{m}", [(full, [(bank[:, j * T:(j + 1) * T], j * P, P, None) for j in range(2)])],
                              mg_hi, mg_lo, (sem("mg_lo_ready"), 4 * L + 1))
                sumsq(L, "ssf", L)
                for b in range(NB):
                    n = len([i for i in range(MIX_END[L]) if i % NB == b])
                    pe.wait_ge(sem(f"bank_free{b}"), n)

            def used(mm, u, j):
                mm.then_inc(sem(f"split_used{j % NSPLIT}"), 1)

            def parts(u, j):
                n, _ = half_words(j)
                wait_hi(pe, u, j)
                wait_lo(pe, u, j)
                hi, lo = w_hi[:, j % NSPLIT, 0:n], w_lo[:, j % NSPLIT, 0:n]
                if UNIT_LOADS[j // 2][0] != "D":
                    hi, lo = (x.rearrange("p (k c) -> p k c", k=KD // 2) for x in (hi, lo))
                return hi, lo

            def dense(u, first=False):
                def three(dst, whi, wlo, xhi, xlo, start, stop):
                    pe.matmul(dst, whi, xhi, start=start, stop=False, skip_group_check=True)
                    pe.matmul(dst, whi, xlo, start=False, stop=False, skip_group_check=True)
                    return pe.matmul(dst, wlo, xhi, start=False, stop=stop, skip_group_check=True)

                for j in range(HALVES):
                    name = UNIT_LOADS[j // 2]
                    g0, gn = GROUPS[int(name[1])]
                    hi, lo = parts(u, j)
                    if name[0] == "D":
                        if j % 2 == 0:
                            pe.wait_ge(sem("hid_lo_ready"), len(GROUPS) * u + int(name[1]) + 1)
                        for x in range(gn * KD // 2):
                            t, m = divmod((j % 2) * gn * KD // 2 + x, KD)
                            c = slice(x * P, (x + 1) * P)
                            mm = three(PS[:, 4 + m // 2, (m % 2) * T:(m % 2 + 1) * T], hi[:, c], lo[:, c],
                                       hid_hi[:, g0 + t, :], hid_lo[:, g0 + t, :], False, False)
                    else:
                        up = name[0] == "U"
                        for t in range(g0, g0 + gn):
                            if j % 2 == 0 and not up and (t >= DB or not first):
                                before = t - DB if t >= DB else max(x for x in range(FT) if x % DB == t % DB) - FT
                                pe.wait_ge(sem("hidf_ready"), FT * u + before + 1)
                            for k in range(KD // 2):
                                kt = (j % 2) * KD // 2 + k
                                if first and j < 2 and t == g0:
                                    pe.wait_ge(sem("h_lo_ready"), KD // 2 + kt // 2 + 1)
                                c = slice((t - g0) * P, (t - g0 + 1) * P)
                                mm = three(PS[:, t % DB, up * T:(up + 1) * T], hi[:, k, c], lo[:, k, c],
                                           h_hi[:, kt, :], h_lo[:, kt, :], kt == 0, kt == KD - 1)
                            if up and j % 2 == 1 and t < g0 + gn - 1:
                                mm.then_inc(sem("tile_full"), 1)
                    used(mm, u, j)

            mixer(0)
            for b in range(4, 8):
                pe.matmul(PS[:, b, :], zb[:, :], zb[:, :].unsqueeze(1).broadcast_to([P, 4, P]), start=True, stop=True,
                          skip_group_check=True)
            dense(0, first=True)
            with pe.Fori(1, NDENSE) as i:
                dense(i)
            mixer(1)

            pe.wait_ge(sem("router_in"), 16)
            for i in range(KD):
                pe.wait_ge(sem("h_ready"), KD * (2 * DEPTH - 1) + i + 1)
                for a in range(TT):
                    mm = pe.matmul(PS[:, 0, a * NE:(a + 1) * NE], hT[:, i, a * P:(a + 1) * P], wr[:, i, :],
                                   start=(i == 0 and a == 0), stop=(i == KD - 1), skip_group_check=True)
            mm.then_inc(sem("logits_full"), 1)
            for a in range(TT):
                for c in range(2):
                    for i in range(4):
                        kt = 4 * c + i
                        mm = pe.transpose(PS[:, 2 + 2 * a + c, i * P:(i + 1) * P], hT[:, kt, a * P:(a + 1) * P], ident[:, :])
                    mm.then_inc(sem("htok_full"), 1)
            pe.wait_ge(sem("msel_ready"), 1)
            pe.wait_ge(sem("tri_ready"), 1)
            pe.matmul(PS[:, 1, 0:NE], tri[:, :], msel[:, 0, :], start=True, stop=True)
            pe.matmul(PS[:, 1, NE:2 * NE], ones[:, :], msel[:, 0, :], start=True, stop=False)
            pe.matmul(PS[:, 1, NE:2 * NE], tri[:, :], msel[:, 1, :], start=False, stop=True)
            pe.matmul(PS[:, 1, 2 * NE:3 * NE], ones[:, :], msel[:, 0, :], start=True, stop=False)
            pe.matmul(PS[:, 1, 2 * NE:3 * NE], ones[:, :], msel[:, 1, :], start=False, stop=True)\
              .then_inc(sem("rank_full"), 1)
            pe.wait_ge(sem("htok_ready"), 4)

            def gather(r, e):
                pe.wait_ge(sem("psel_ready"), 2 * (r + 1))
                for c in range(2):
                    b, n = gather_use(r, e - 1, c)
                    wait_aux_free(pe, b, n)
                    for i in range(4):
                        for a in range(TT):
                            mm = pe.matmul(PS[:, 4 + b, i * CAP:(i + 1) * CAP], htok[:, a, (4 * c + i) * P:(4 * c + i + 1) * P],
                                           psel[:, a, e, :], start=(a == 0), stop=(a == TT - 1))
                    mm.then_inc(sem(f"aux_full{b}"), 1)

            def scatter(e, n, uses, part):
                pe.wait_ge(sem("ye_act"), n + 1)
                pe.wait_ge(sem("ye_dve"), n + 1)
                for c in (2 * part, 2 * part + 1):
                    wait_aux_free(pe, c % 2, uses + c // 2)
                    for j in range(2):
                        kt = 2 * c + j
                        mm = pe.matmul(PS[:, 4 + c % 2, j * T:(j + 1) * T], ye[:, kt * P:(kt + 1) * P], selT[:, e, :],
                                       start=True, stop=True)
                    mm.then_inc(sem(f"aux_full{c % 2}"), 1)

            def turn(r, e, n, g, last):
                b, uses = turn_use(r, e, g, last)
                g0, gn = GROUPS[g]
                pe.wait_ge(sem("hide_ready"), len(GROUPS) * n + g + 1)
                wait_aux_free(pe, b, uses)
                for i in range(gn):
                    mm = pe.transpose(PS[:, 4 + b, i * CAP:(i + 1) * CAP], hide[:, g % 2, i * P:(i + 1) * P],
                                      ident[0:CAP, 0:CAP])
                mm.then_inc(sem(f"aux_full{b}"), 1)

            def prepare(r, part):
                pe.wait_ge(sem("sel_ready"), 2 * (r + 1))
                for c in (2 * part, 2 * part + 1):
                    wait_aux_free(pe, c % 2, PASS_USES * r + 1 + c // 2)
                    for i in range(2):
                        for a in range(TT):
                            mm = pe.transpose(PS[0:CAP, 4 + c % 2, i * T + a * P:i * T + (a + 1) * P],
                                              wsel[:, a, 2 * c + i, :], ident[:, :])
                    mm.then_inc(sem(f"aux_full{c % 2}"), 1)

            def expert(r, e, n, first=False, last=False):
                def three(dst, xhi, xlo, whi, wlo, start, stop):
                    pe.matmul(dst, xhi, whi, start=start, stop=False)
                    pe.matmul(dst, xlo, whi, start=False, stop=False)
                    return pe.matmul(dst, xhi, wlo, start=False, stop=stop)

                for c in range(2):
                    b, uses = gather_use(r, e - 1, c)
                    wait_aux_free(pe, b, uses + 1)
                for j in range(HALVES):
                    name = UNIT_LOADS[j // 2]
                    g = int(name[1])
                    g0, gn = GROUPS[g]
                    hi, lo = parts(NDENSE + n, j)
                    if name[0] == "D":
                        if j % 2 == 0:
                            b, uses = turn_use(r, e, g, last)
                            wait_aux_free(pe, b, uses + 1)
                        if name == "D0" and j % 2 == 0 and not (isinstance(n, int) and n == 0):
                            pe.wait_ge(sem("ye_act"), n)
                            pe.wait_ge(sem("ye_dve"), n)
                        for x in range(gn):
                            t, c = divmod((j % 2) * gn + x, 2)
                            t += g0
                            w = slice(x * 512, (x + 1) * 512)
                            mm = three(PS[0:CAP, 6 + c, :], hdT_hi[:, t, :], hdT_lo[:, t, :], hi[:, w], lo[:, w],
                                       t == 0, t == FT - 1)
                    else:
                        up = name[0] == "U"
                        if j % 2 == 0 and not up and (g >= 2 or not (isinstance(n, int) and n == 0)):
                            pe.wait_ge(sem("hide_ready"), len(GROUPS) * n + g - 1)
                        for k in range(KD // 2):
                            kt = (j % 2) * KD // 2 + k
                            mm = three(PS[0:CAP, 2 * (g % 2) + up, 0:gn * P], hTe_hi[:, kt, :], hTe_lo[:, kt, :],
                                       hi[:, k, :], lo[:, k, :], kt == 0, kt == KD - 1)
                    used(mm, NDENSE + n, j)
                    for what, x in EXPERT_AFTER.get(j, ()):
                        if what == "tr":
                            turn(r, e, n, x, last)
                        elif what == "scatter" and first:
                            prepare(r, x)
                        elif what == "scatter":
                            scatter(e - 1, n - 1, scatter_use(r, e), x)
                        elif what == "gather" and not last:
                            gather(r, e + 1)

            def one_pass(r):
                n = r * NE
                gather(r, 0)
                expert(r, 0, n, first=True)
                with pe.Fori(1, NE - 1) as e:
                    expert(r, e, n + e)
                expert(r, NE - 1, n + NE - 1, last=True)
                for part in range(2):
                    scatter(NE - 1, n + NE - 1, scatter_use(r, NE), part)
                for b in range(2):
                    wait_aux_free(pe, b, PASS_USES * (r + 1))

            one_pass(0)
            pe.wait_ge(sem("passes_known"), 1)
            npass = pe.value_load(npi[0:1, 0:1], min_val=1, max_val=PASSES)
            with pe.If(npass > 1):
                with pe.Fori(1, npass) as r:
                    one_pass(r)
            for i in range(4):
                bank = PS[:, 2 + i, :]
                for j in range(4):
                    a, kt = i // 2, 4 * (i % 2) + j
                    mm = pe.transpose(bank[:, j * P:(j + 1) * P], xT[:, kt, a * P:(a + 1) * P], ident[:, :])
                mm.then_inc(sem("yo_full"), 1)

        @block.gpsimd
        def _(pool):
            step = Chain(pool, sem("pool_step"))
            pool.memset(ring[:, NSLOT - 1, 0:P], 0.0).then_inc(sem("rows_clear"), 1)
            for t, v in ((ident, 0.0), (ones, 1.0), (eps, EPS)):
                pool.memset(t[:], v).then_inc(sem("pool_step"), 1)
                step.n += 1
            step.wait()
            step(pool.memset(eps[:, 1:2], QK * EPS))
            pool.affine_select(out=ident[:, :], in_=ident[:, :], compare_op=ALU.not_equal, fill=1.0, base=0,
                               pattern=[[-1, P]], channel_multiplier=1).then_inc(sem("ident_ready"), 1)
            for t, v in ((zb, 0.0), (maskc, 0.0), (maskg, 1.0), (chm, 1.0), (keep, 1.0),
                         (one1, 1.0), (invr, 0.0), (R, 0.0), (u, 0.0), (qdm, 0.0), (selh, 0.0)):
                pool.memset(t[:], v).then_inc(sem("pool_step"), 1)
                step.n += 1
            step.wait()
            for i in range(ROPE):
                step(pool.memset(invr[0:1, NOPE + i:NOPE + i + 1], float(np.float32(ROPE_BASE ** (-(i % HALF) / HALF)))))
            step(pool.memset(selh[0:GDK, 0:1], GDK ** -0.5))
            step(pool.memset(selh[GDK:P, 1:2], GDK ** -0.5))

            def select(t, pattern, base, cm, fill, op=ALU.is_ge):
                step(pool.affine_select(out=t, in_=t, compare_op=op, fill=fill, base=base, pattern=pattern,
                                        channel_multiplier=cm))
            select(maskc[:, 0:P], [[-1, P]], 0, 1, NEG)
            select(maskc[:, 2 * P:3 * P], [[-1, P]], 0, 1, NEG)
            g3 = maskg[:, :].rearrange("p (n c) -> p n c", n=NCT)
            select(g3, [[-GC, NCT], [0, GC]], 0, 1, 0.0)
            select(g3, [[GC, NCT], [0, GC]], GC - 1, -1, 0.0)
            select(g3, [[GC, NCT], [1, GC]], 0, -1, 0.0)
            select(chm[:, :], [[-GC, NCT]], 0, 1, 0.0)
            select(chm[:, :], [[GC, NCT]], GC - 1, -1, 0.0)
            k3 = keep[:, :].rearrange("p (n c) -> p n c", c=GC)
            select(k3, [[0, NCH], [1, GC]], 0, 0, 0.0, ALU.not_equal)
            rr_ = R[NOPE:QK, NOPE:QK]
            select(rr_, [[-1, ROPE]], -HALF, 1, -1.0, ALU.not_equal)
            select(rr_, [[-1, ROPE]], HALF, 1, 1.0, ALU.not_equal)
            pool.iota(cnt[:, :], pattern=[[1, PADW]], base=1, channel_multiplier=0).then_inc(sem("iotas"), 1)
            pool.iota(sloti[:, :], pattern=[[1, CAP]], base=0, channel_multiplier=0).then_inc(sem("iotas"), 1)
            pool.memset(one1[:, :], 1.0).then_inc(sem("consts"), 1)
            for L in range(DEPTH):
                r = slice(NOPE, QK)
                if L == 0:
                    pool.wait_ge(sem("rope_tables"), 1)
                cos = cs[r, 0, :].unsqueeze(1).broadcast_to([ROPE, 2, T])
                for i in range(4):
                    _, f, _, n = use(L, f"rq{i}")
                    pool.wait_ge(f, n + 1)
                    x = q[r, 2 * i:2 * i + 2, :]
                    pool.tensor_tensor(x, x, cos, MUL).then_inc(sem("cos_done"), 1)
                pool.wait_ge(sem("eb_ready"), L + 1)
                for x in ("gq", "gk"):
                    _, _, free, n = use(L, x)
                    pool.wait_ge(free, n + 1)
                for c in range(2):
                    rows = slice(c * GDK, (c + 1) * GDK)
                    pool.tensor_tensor(qdm[rows, c, :, :], gq[rows, :, :], eb[rows, :, :], MUL).then_inc(sem("qdm_step"), 1)
                pool.wait_ge(sem("qdm_step"), 2 * (L + 1))
                pool.tensor_scalar(qdm[:, :, :, :], qdm[:, :, :, :], GDK ** -0.5, None, MUL).then_inc(sem("qdm_ready"), 1)
                pool.wait_ge(sem("ek_ready"), L + 1)
                pool.tensor_tensor(kdec[:, :, :], gk[:, :, :], ek[:, :, :], MUL).then_inc(sem("dec_ready"), 1)
                for x in ("ua", "ub"):
                    _, _, free, n = use(L, x)
                    pool.wait_ge(free, n + 1)
                if L == 0:
                    pool.wait_ge(sem("windows"), 1)
                W = PADW + T
                step(pool.tensor_tensor(pwa[:, :, 1:W], u[:, :, 1:W], u[:, :, 0:W - 1], ADD))
                step(pool.tensor_tensor(pwb[:, 1:, 3:W], pwa[:, 1:, 3:W], pwa[:, 1:, 1:W - 2], ADD))
                step(pool.tensor_tensor(pwa[:, 2:, 7:W], pwb[:, 2:, 7:W], pwb[:, 2:, 3:W - 4], ADD))
                step(pool.tensor_tensor(pwb[:, 3, 15:W], pwa[:, 3, 15:W], pwa[:, 3, 7:W - 8], ADD))
                for g, w in enumerate(WINDOWS):
                    win = (pwa if g % 2 == 0 else pwb)[:, g, :]
                    step(pool.tensor_tensor(win[:, PADW:2 * PADW], win[:, PADW:2 * PADW], winf[:, g, :], MUL))
                    step(pool.tensor_scalar(win[:, PADW:W], win[:, PADW:W], 1.0 / w, None, MUL))
                    pool.tensor_tensor(u[:, g, PADW:W], win[:, PADW:W], u[:, g, PADW:W], SUB).then_inc(sem("pooled"), 1)
                for a in range(TT):
                    for d in range(2):
                        pool.wait_ge(sem("e_exp"), 4 * L + 2 * a + d + 1)
                        e = scr[:, d * 2048:(d + 1) * 2048].rearrange("p (c t) -> p c t", c=GC)
                        ins = pool.tensor_tensor(e, e, gk[:, d, a * P:(a + 1) * P].unsqueeze(1).broadcast_to([P, GC, P]), MUL)
                        ins.then_inc(sem("e_k"), 1)
            _, f, _, n = use(DEPTH - 1, "pl1")
            pool.wait_ge(f, n + 1)
            step(pool.memset(tri, 1.0))
            pool.affine_select(out=tri, in_=tri, compare_op=ALU.is_ge, fill=0.0, base=-1, pattern=[[1, P]],
                               channel_multiplier=-1).then_inc(sem("tri_ready"), 1)

        @block.scalar
        def _(act):
            rows = ring[:, NSLOT - 1, 0:P]
            act.wait_ge(sem("rows_clear"), 1)
            for name, n in PARAMS:
                r0 = PCOL[name]
                wide = QK if name in ("g_qk_q", "g_qk_k") else P
                src = A[name] if wide == QK else A[name].rearrange("l (k p) -> (l k) p", p=P)
                act.dma_start(rows[r0:r0 + n, 0:wide], src).then_inc(sem("params_in"), 16)
            act.dma_start(posi[NOPE:QK, :], A["positions"].broadcast_to([ROPE, T])).then_inc(sem("pos_in"), 16)
            act.dma_start(wgu[:, :, :], A["w_gla_gate_up"].rearrange("l r c -> r l c")).then_inc(sem("gu_in"), 16)
            act.dma_start(wr[:, :, :], A["w_router"][0].rearrange("(k p) e -> p k e", p=P)).then_inc(sem("router_in"), 16)

            def full(L, name):
                bank, f, free, n = use(L, name)
                act.wait_ge(f, n + 1)
                return bank, free

            def freed(L, name):
                _, _, free, n = use(L, name)
                act.wait_ge(free, n + 1)

            def pcol(name, i=0, rows=P):
                return par[0:rows, PCOL[name] + i:PCOL[name] + i + 1]

            def two(ap):
                return ap.rearrange("p (a t) -> p a t", a=2)

            def inverse_rms(L, i, name, n, scale, parts=(0, 1)):
                x = 5 * L + i
                r = (rt, rr)[x % 2][:, 0:n, :]
                if 0 in parts:
                    bank, free = full(L, name)
                    last = {2: ("h_ready", KD * (2 * L + 1)), 3: ("latn_ready", 4 * (L + 1)), 4: ("yb_ready", 2 * L + 1),
                            0: ("yb_ready", 2 * L), 1: ("h_ready", 2 * KD * L)}[i]
                    if last[1]:
                        act.wait_ge(sem(last[0]), last[1])
                    act.activation(r, bank[:, 0:n * T].rearrange("p (a t) -> p a t", a=n), ACT.Ln, bias=eps[:, 0:1],
                                   scale=scale).then_inc(free, 1)
                if 1 in parts:
                    freed(L, name)
                    act.activation(r, r, ACT.Exp, scale=-0.5).then_inc(sem("rms_ready"), 1)

            warm = [0]

            def load_ln():
                if warm[0]:
                    act.wait_ge(sem("warmed"), warm[0])
                act.activation(warmth[:, :], eps[:, 0:1], ACT.Ln).then_inc(sem("warmed"), 1)
                warm[0] += 1

            def split(L, name, pieces=range(PIECES)):
                s, r = slot_of(L, name)
                act.wait_ge(sem(f"slot_full{s}"), 16 * r)
                for p in pieces:
                    piece_done(act, L, name, p)
                    raw, hi, _ = piece_of(L, name, p)
                    act.activation(hi, raw, ACT.Copy).then_inc(sem("m_hi_ready"), 1)

            FIRST, LAST = range(PIECES - 1), [PIECES - 1]

            def split_h(which):
                for i in range(4):
                    act.wait_ge(sem("h_ready"), KD * which + 2 * i + 2)
                    act.activation(h_hi[:, 2 * i:2 * i + 2, :], hT[:, 2 * i:2 * i + 2, :], ACT.Copy).then_inc(sem("h_hi_ready"), 1)

            def mixer(L):
                for i in (0, 2):
                    if L == 0:
                        freed(-1, f"x{i}")
                    else:
                        act.wait_ge(sem("x_dense"), i + 2)
                    act.activation(sq[:, 2 * i:2 * i + 2, :], xT[:, 2 * i:2 * i + 2, :], ACT.Square)\
                       .then_inc(sem("sq_act"), 1)
                if L == 0:
                    act.wait_ge(sem("ident_ready"), 1)
                split(L, "cq")
                load_ln()
                inverse_rms(L, 0, "ssm", 1, 1.0 / D)
                if L == 0:
                    bank, free = full(-1, "par")
                    act.activation(par[:, :], bank[:, 0:NPAR], ACT.Copy).then_inc(free, 1)
                    bank, free = full(-1, "inv")
                    act.activation(invc[NOPE:QK, :], bank[NOPE:QK, 0:1], ACT.Copy).then_inc(free, 1)
                split_h(2 * L)
                for i, name in enumerate(("cq", "ckv")):
                    split(L, ("ckv", "gq")[i], FIRST)
                    bank, free = full(L, name)
                    act.activation(sq[:, 2 * i:2 * i + 2, :], two(bank), ACT.Square)
                    act.activation(lat[:, 2 * i:2 * i + 2, :], two(bank), ACT.Copy).then_inc(free, 1)
                    if i == 0:
                        split(L, "ckv", LAST)
                bank, free = full(L, "kr")
                act.activation(krope[NOPE:QK, :], bank[NOPE:QK, 0:T], ACT.Copy).then_inc(free, 1)
                split(L, "gq", LAST)
                split(L, "gk")
                inverse_rms(L, 1, "sslat", 2, 1.0 / RANK)
                split(L, "va")
                for i in range(4):
                    bank, free = full(L, f"q{i}")
                    act.activation(sq[0:QK, 2 * i:2 * i + 2, :], two(bank[0:QK, :]), ACT.Square)
                    act.activation(q[:, 2 * i:2 * i + 2, :], two(bank[0:QK, :]), ACT.Copy,
                                   scale=pcol("g_qk_q", L, QK)).then_inc(free, 1)
                split(L, "vb")
                freed(L, "kr")
                kr8 = krope[NOPE:QK, :].unsqueeze(1).broadcast_to([ROPE, H, T])
                act.activation(sk[NOPE:QK, :, :], kr8, ACT.Square).then_inc(sem("krope_read"), 1)
                act.wait_ge(sem("krope_read"), 2 * L + 1)
                act.activation(krope[NOPE:QK, :], krope[NOPE:QK, :], ACT.Copy,
                               scale=par[NOPE:QK, PCOL["g_qk_k"] + L:PCOL["g_qk_k"] + L + 1]).then_inc(sem("kg_ready"), 1)
                for i in range(4):
                    bank, free = full(L, f"k{i}")
                    act.activation(sk[0:NOPE, 2 * i:2 * i + 2, :], two(bank[0:NOPE, :]), ACT.Square)
                    act.activation(k[0:NOPE, 2 * i:2 * i + 2, :], two(bank[0:NOPE, :]), ACT.Copy,
                                   scale=pcol("g_qk_k", L, NOPE)).then_inc(free, 1)
                split(L, "oga", FIRST)
                bank, free = full(L, "lr")
                act.activation(glr[:, :], bank[0:GRANK, 0:T], ACT.Copy).then_inc(free, 1)
                split(L, "oga", LAST)
                if L == 0:
                    act.wait_ge(sem("angles"), 1)
                    act.activation(cs[NOPE:QK, :, :], ang[NOPE:QK, 1:3, :], ACT.Sin).then_inc(sem("rope_tables"), 1)

                def out_gate(i):
                    bank, _ = full(L, f"og{'ab'[i]}")
                    if 2 * L + i:
                        act.wait_ge(sem("og_done"), 2 * L + i)
                    act.activation(th[:, :, :], two(bank), ACT.Tanh, scale=0.5).then_inc(sem("og_tanh"), 1)
                split(L, "ogb", FIRST)
                out_gate(0)
                split(L, "ogb", LAST)
                bank, free = full(L, "ssq")
                act.activation(rq16[:, :], bank[:, 0:TT * H], ACT.Sqrt, bias=eps[:, 1:2])
                act.activation(rk16[:, :], bank[:, TT * H:2 * TT * H], ACT.Sqrt, bias=eps[:, 0:1], scale=1.0 / QK).then_inc(free, 1)
                act.wait_ge(sem("z_abs"), L + 1)
                act.activation(ztmp[:, 2:4, :], ztmp[:, 2:4, :], ACT.Exp, scale=-1.0).then_inc(sem("z_step"), 1)
                act.wait_ge(sem("z_step"), 2 * L + 1)
                act.activation(ztmp[:, 2:4, :], ztmp[:, 2:4, :], ACT.Ln, bias=1.0).then_inc(sem("z_step"), 1)
                act.wait_ge(sem("krope_turned"), L + 1)
                act.activation(k[NOPE:QK, :, :], kr8, ACT.Copy).then_inc(sem("krope_read"), 1)
                split(L, "ua", FIRST)
                out_gate(1)
                split(L, "ua", LAST)
                for i, name in enumerate(("ua", "ub")):
                    split(L, ("ub", "g0")[i], FIRST)
                    bank, free = full(L, name)
                    act.activation(u[:, 2 * i:2 * i + 2, PADW:PADW + T], two(bank), ACT.Copy).then_inc(free, 1)
                    split(L, ("ub", "g0")[i], LAST)
                act.wait_ge(sem("bc_ready"), L + 1)
                act.activation(eb[:, :, :], bc[:, :, :], ACT.Exp).then_inc(sem("eb_ready"), 1)
                act.activation(al[:, :, :], bc[:, :, :].rearrange("p d (n c) -> p d n c", c=GC)[:, :, :, GC - 1],
                               ACT.Exp).then_inc(sem("al_ready"), 1)
                act.wait_ge(sem("db_ready"), L + 1)
                act.activation(ek[:, :, :], ek[:, :, :], ACT.Exp).then_inc(sem("ek_ready"), 1)

                def gate(i):
                    split(L, f"g{i + 1}" if i < 11 else "br00", FIRST)
                    bank, free = full(L, f"g{i}")
                    if i == 0:
                        act.wait_ge(sem("latn_ready"), 4 * (L + 1))
                        _, f, _, n = use(L, "vm1")
                        act.wait_ge(f, n + 1)
                    if i == 8:
                        freed(L, "ssk3")
                    act.activation(gates[:, 2 * i:2 * i + 2, :], two(bank), ACT.Tanh, scale=0.5).then_inc(free, 1)
                    split(L, f"g{i + 1}" if i < 11 else "br00", LAST)

                def y_high(n):
                    if n == 2:
                        freed(L, "pl1")
                    elif n == 1:
                        _, f, _, c = use(L, "b03")
                        act.wait_ge(f, c + 1)
                        act.wait_ge(sem("yb_ready"), 2 * (L + 1))
                    act.activation(y_parts[n][0][:, :, :], ys[:, n * KB:(n + 1) * KB, :], ACT.Copy)\
                       .then_inc(sem("y_hi_ready"), 1)

                def merged_high(m):
                    act.wait_ge(sem("merged"), 4 * L + m + 1)
                    act.activation(mg_hi[:, 2 * m:2 * m + 2, :], merged[:, 2 * m:2 * m + 2, :], ACT.Copy)\
                       .then_inc(sem("mg_hi_ready"), 1)

                def exps(h):
                    act.wait_ge(sem("nb_ready"), H * L + h + 1)
                    for a in range(TT):
                        w = slice(0, P) if a == 0 else slice(P, 3 * P)
                        ins = act.activation(Pr[:, h % 3, w], Pr[:, h % 3, w], ACT.Exp, bias=nbs[:, h % 2, a:a + 1],
                                             scale=rqs[:, a * H + h:a * H + h + 1], accum_out=sums[:, h % 2, a:a + 1])
                    ins.then_inc(sem("exp_done"), 1)

                def turned(h):
                    bank, free = full(L, f"pt{h}")
                    if h == 0:
                        act.wait_ge(sem("dec_ready"), L + 1)
                    if h >= 2:
                        _, f, _, n = use(L, f"o{(h - 2) // 2}")
                        act.wait_ge(f, n + 1)
                    act.activation(PT[:, h % 2, :], bank[:, 0:3 * P], ACT.Copy).then_inc(free, 1)

                def values(i):
                    bank, free = full(L, f"o{i}")
                    act.activation(ys[:, i, :], bank[:, 0:T], ACT.Copy).then_inc(free, 1)

                def decay(a, d):
                    act.wait_ge(sem("e_diff"), 4 * L + 2 * a + d + 1)
                    e = scr[:, d * 2048:(d + 1) * 2048]
                    act.activation(e, e, ACT.Relu).then_inc(sem("e_relu"), 1)
                    act.wait_ge(sem("e_relu"), 4 * L + 2 * a + d + 1)
                    act.activation(e, e, ACT.Exp, scale=-1.0).then_inc(sem("e_exp"), 1)

                def pool_out(i):
                    bank, free = full(L, f"pl{i}")
                    for j in range(2):
                        ins = act.activation(ys[:, 2 * KB + 2 * i + j, :], bank[:, j * T:(j + 1) * T], ACT.Copy,
                                             scale=pcol("pool_scale", L * NG + 2 * i + j))
                    ins.then_inc(free, 1)

                gate(0), exps(0), exps(1), gate(1), turned(0), turned(1), exps(2), exps(3)
                gate(2), values(0), turned(2), turned(3), exps(4), exps(5)
                gate(3), values(1), turned(4), turned(5), exps(6), exps(7)
                gate(4), decay(0, 0), values(2), turned(6), turned(7), decay(0, 1), pool_out(0), pool_out(1)
                gate(5), gate(6), decay(1, 0), decay(1, 1), values(3)
                gate(7), gate(8), y_high(0), gate(9), gate(10)
                act.wait_ge(sem("go_full"), L + 1)
                for i in range(2):
                    act.activation(gsq[:, i, :, :], two(PS[:, 6 + i, :]), ACT.Square).then_inc(sem("gsq_ready"), 1)
                y_high(2)
                gate(11)
                split(L, "br01")
                for i in range(2):
                    inverse_rms(L, 2 + i, f"ssg{i}", 2, 1.0 / GDV, [0])
                split(L, "br20")
                for i in range(2):
                    inverse_rms(L, 2 + i, f"ssg{i}", 2, 1.0 / GDV, [1])
                split(L, "br21"), split(L, "br10", [0, 1]), y_high(1), split(L, "br10", [2, 3]), split(L, "br11")
                split(L, "out0", [0])
                merged_high(0)
                split(L, "out0", [1])
                merged_high(1)
                split(L, "out0", [2])
                merged_high(2)
                split(L, "out0", [3])
                merged_high(3)
                split(L, "out1"), split(L, "out2")

                def squares(i):
                    freed(L, f"w{i + 1}")
                    freed(L, f"w{i}")
                    act.activation(sq[:, 2 * i:2 * i + 2, :], xT[:, 2 * i:2 * i + 2, :], ACT.Square)\
                       .then_inc(sem("sq_act"), 1)
                squares(0)
                split(L, "out3")
                for j in range(NSPLIT):
                    round_hi(act, NDENSE * L, j, L, 0)
                squares(2)
                load_ln()
                inverse_rms(L, 4, "ssf", 1, 1.0 / D)

            def dense(u, first=False):
                def gate_up(g):
                    g0, gn = GROUPS[g]
                    for t in range(gn):
                        if t < gn - 1:
                            act.wait_ge(sem("tile_full"), (FT - len(GROUPS)) * u + sum(x[1] - 1 for x in GROUPS[:g]) + t + 1)
                        else:
                            wait_used(act, u, HALF_OF[f"U{g}"] + 1)
                        if g > 0 or not first:
                            act.wait_ge(sem("hidf_ready"), FT * u + g0 + (t if t < GROUPS[g - 1][1] else t - 3)
                                        - GROUPS[g - 1][1] + 1)
                        act.activation(sil[:, t, :], PS[:, (g0 + t) % DB, 0:T], ACT.Silu).then_inc(sem("sil_ready"), 1)
                    act.wait_ge(sem("hidf_ready"), FT * u + g0 + gn)
                    act.activation(hid_hi[:, g0:g0 + gn, :], hidf[:, 0:gn, :], ACT.Copy).then_inc(sem("hid_hi_ready"), 1)

                for j in range(HALVES):
                    for _, g in DENSE_AFTER.get(j - NSPLIT, ()):
                        gate_up(g)
                    if not (first and j < NSPLIT):
                        round_hi(act, u, j, 0, u)

            mixer(0)
            split_h(1)
            dense(0, first=True)
            with act.Fori(1, NDENSE) as i:
                dense(i)
            mixer(1)

            act.wait_ge(sem("logit_gap"), 1)
            act.activation(rsm[:, 2:4], rsm[:, 0:2], ACT.Exp).then_inc(sem("top_exp"), 1)
            for c in range(4):
                act.wait_ge(sem("htok_full"), c + 1)
                act.activation(htok[:, c // 2, (c % 2) * 512:(c % 2 + 1) * 512], PS[:, 2 + c, :], ACT.Copy)\
                   .then_inc(sem("htok_ready"), 1)

            def tokens(r, e, n):
                for c in range(2):
                    b, uses = gather_use(r, e - 1, c)
                    wait_aux_full(act, b, uses)
                    act.activation(hTe_hi[:, 4 * c:4 * c + 4, :], PS[:, 4 + b, 0:4 * CAP].rearrange("p (k c) -> p k c", k=4),
                                   ACT.Copy).then_inc(sem("hTe_hi_ready"), 1)

            def rows_out(n):
                wait_used(act, NDENSE + n, HALVES - 1)
                act.activation(ye[:, 0:512], PS[0:CAP, 6, :], ACT.Copy).then_inc(sem("ye_act"), 1)

            def expert(r, e, n, first=False, last=False):
                u = NDENSE + n
                for j in range(HALVES):
                    if j == 2 and not first:
                        rows_out(n - 1)
                    for what, g in EXPERT_AFTER.get(j - NSPLIT, ()):
                        if what == "gu":
                            g0, gn = GROUPS[g]
                            wait_used(act, u, HALF_OF[f"U{g}"] + 1)
                            if g >= 2 or not (isinstance(n, int) and n == 0):
                                act.wait_ge(sem("hide_ready"), len(GROUPS) * n + g - 1)
                            act.activation(sile[:, g % 2, 0:gn * P], PS[0:CAP, 2 * (g % 2), 0:gn * P], ACT.Silu)\
                               .then_inc(sem("sile_ready"), 1)
                        elif what == "tr":
                            b, uses = turn_use(r, e, g, last)
                            g0, gn = GROUPS[g]
                            wait_aux_full(act, b, uses)
                            act.activation(hdT_hi[:, g0:g0 + gn, :], PS[:, 4 + b, 0:gn * CAP].rearrange("p (k c) -> p k c", k=gn),
                                           ACT.Copy).then_inc(sem("hdT_hi_ready"), 1)
                        elif what == "gather" and not last:
                            tokens(r, e + 1, n + 1)
                        elif what == "scatter" and first:
                            for c in (2 * g, 2 * g + 1):
                                wait_aux_full(act, c % 2, PASS_USES * r + 1 + c // 2)
                                act.activation(selT[:, 2 * c:2 * c + 2, :], two(PS[0:CAP, 4 + c % 2, :]), ACT.Copy)\
                                   .then_inc(sem(f"aux_free{c % 2}"), 1)
                    if not (j < NSPLIT and isinstance(n, int) and n == 0):
                        round_hi(act, u, j, 1, n)

            def one_pass(r):
                n = r * NE
                tokens(r, 0, n)
                expert(r, 0, n, first=True)
                with act.Fori(1, NE - 1) as e:
                    expert(r, e, n + e)
                expert(r, NE - 1, n + NE - 1, last=True)
                rows_out(n + NE - 1)

            one_pass(0)
            act.wait_ge(sem("passes_known"), 1)
            npass = act.value_load(npi[0:1, 0:1], min_val=1, max_val=PASSES)
            with act.If(npass > 1):
                with act.Fori(1, npass) as r:
                    one_pass(r)
            for i in range(4):
                act.wait_ge(sem("yo_full"), i + 1)
                act.activation(yout[:, i // 2, (i % 2) * 512:(i % 2 + 1) * 512], PS[:, 2 + i, :], ACT.Copy)\
                   .then_inc(sem("y_out"), 1)

        @block.vector
        def _(dve):
            step = Chain(dve, sem("dve_step"))

            def full(L, name):
                bank, f, free, n = use(L, name)
                dve.wait_ge(f, n + 1)
                return bank, free

            def freed(L, name):
                _, _, free, n = use(L, name)
                dve.wait_ge(free, n + 1)

            def pcol(name, i=0, rows=P):
                return par[0:rows, PCOL[name] + i:PCOL[name] + i + 1]

            def two(ap):
                return ap.rearrange("p (a t) -> p a t", a=2)

            for i in range(4):
                bank, free = full(-1, f"x{i}")
                dve.tensor_copy(xT[:, 2 * i:2 * i + 2, :], two(bank)).then_inc(free, 1)

            def tables():
                TWO_PI = 2 * np.pi
                c1 = 6.28125
                c2 = float(np.float32(np.floor((TWO_PI - c1) * 2 ** 21) / 2 ** 21))
                c3 = float(np.float32(TWO_PI - c1 - c2))
                magic = 1.5 * 2 ** 23
                pi = float(np.nextafter(np.float32(np.pi), np.float32(0)))
                r = slice(NOPE, QK)
                dve.wait_ge(sem("pos_in"), 16)
                step(dve.tensor_copy(ang[r, 0, :], posi[r, :]))
                freed(-1, "inv")
                step(dve.tensor_scalar(ang[r, 0, :], ang[r, 0, :], invc[r, 0:1], None, MUL))
                for j, shift in ((1, 0.25), (2, 0.0)):
                    step(dve.tensor_scalar(angk[r, :], ang[r, 0, :], 1 / TWO_PI, shift, MUL, ADD))
                    step(dve.tensor_scalar(angk[r, :], angk[r, :], magic, magic, ADD, SUB))
                    step(dve.scalar_tensor_tensor(ang[r, j, :], angk[r, :], -c1, ang[r, 0, :], MUL, ADD))
                    step(dve.scalar_tensor_tensor(ang[r, j, :], angk[r, :], -c2, ang[r, j, :], MUL, ADD))
                    step(dve.scalar_tensor_tensor(ang[r, j, :], angk[r, :], -c3, ang[r, j, :], MUL, ADD))
                    if shift:
                        step(dve.tensor_scalar(ang[r, j, :], ang[r, j, :], np.pi / 2, None, ADD))
                    ins = dve.tensor_scalar(ang[r, j, :], ang[r, j, :], pi, -pi, MIN, MAX)
                    if j == 1:
                        step(ins)
                ins.then_inc(sem("angles"), 1)
                dve.wait_ge(sem("iotas"), 2)
                for g, w in enumerate(WINDOWS):
                    step(dve.tensor_scalar(winf[:, g, :], cnt[:, :], float(w), 1.0 / w, MIN, MUL))
                dve.reciprocal(winf[:, :, :], winf[:, :, :]).then_inc(sem("windows"), 1)
                step(dve.tensor_copy(slots[:, :], sloti[:, :]))
                step(dve.tensor_copy(iot8[:, :], sloti[:, 0:NE]))

            def rms(L, i):
                x = 5 * L + i
                dve.wait_ge(sem("rms_ready"), x + 1)
                return (rt, rr)[x % 2]

            def norm_x(L, which, gain):
                for i in (1, 3):
                    if which == "ssm" and L == 1:
                        dve.wait_ge(sem("x_dense"), i + 1)
                    elif which == "ssf":
                        freed(L, f"w{i}")
                    else:
                        freed(-1, f"x{i}")
                    dve.tensor_tensor(sq[:, 2 * i:2 * i + 2, :], xT[:, 2 * i:2 * i + 2, :], xT[:, 2 * i:2 * i + 2, :], MUL)\
                       .then_inc(sem("sq_dve"), 1)
                if which == "ssm":
                    split(L, "cq")
                r = rms(L, 0 if which == "ssm" else 4)
                if (L, which) == (0, "ssm"):
                    freed(-1, "par")
                low = 0 if (L, which) == (DEPTH - 1, "ssf") else 4
                for i in range(KD):
                    if low and i in (4, 6):
                        split_h(2 * L + (which == "ssf"), i // 2 - 2)
                    dve.scalar_tensor_tensor(hT[:, i, :], xT[:, i, :], pcol(gain, L * KD + i), r[:, 0, :], MUL, MUL)\
                       .then_inc(sem("h_ready"), 1)
                if low:
                    for i in (2, 3):
                        split_h(2 * L + (which == "ssf"), i)

            def split(L, name, pieces=range(PIECES)):
                for p in pieces:
                    dve.wait_ge(sem("m_hi_ready"), piece_no(L, name, p) + 1)
                    raw, hi, lo = piece_of(L, name, p)
                    dve.tensor_tensor(lo, raw, hi.bitcast(F32), SUB).then_inc(sem("m_lo_ready"), 1)

            FIRST, LAST = range(PIECES - 1), [PIECES - 1]

            def split_h(which, i):
                x = slice(2 * i, 2 * i + 2)
                dve.wait_ge(sem("h_hi_ready"), 4 * which + i + 1)
                dve.tensor_tensor(h_lo[:, x, :], hT[:, x, :], h_hi[:, x, :].bitcast(F32), SUB).then_inc(sem("h_lo_ready"), 1)

            def mixer(L):
                norm_x(L, "ssm", "g_mix")
                split(L, "ckv"), split(L, "gq")
                split(L, "gk", FIRST)
                bank, free = full(L, "gq")
                dve.tensor_copy(gq[:, :, :], two(bank)).then_inc(free, 1)
                split(L, "gk", LAST)
                r = rms(L, 1)
                for i in range(4):
                    g = pcol("g_cq" if i < 2 else "g_ckv", L * KR + i % 2)
                    dve.scalar_tensor_tensor(latn[:, i, :], lat[:, i, :], g, r[:, i // 2, :], MUL, MUL)\
                       .then_inc(sem("latn_ready"), 1)
                split(L, "va", FIRST)
                bank, free = full(L, "gk")
                dve.tensor_copy(gk[:, :, :], two(bank)).then_inc(free, 1)
                split(L, "va", LAST)

                def v_half(name, c):
                    bank, free = full(L, name)
                    dve.tensor_copy(gvt[:, :, c * 256:(c + 1) * 256], two(bank)).then_inc(free, 1)
                split(L, "vb", FIRST)
                v_half("va", 0)
                split(L, "vb", LAST)
                if L == 0:
                    tables()
                for a in range(TT):
                    bank, free = full(L, f"vm{a}")
                    dve.tensor_copy(vt[:, a, :], bank).then_inc(free, 1)
                split(L, "oga", FIRST)
                v_half("vb", 1)
                split(L, "oga", LAST)

                def out_gate(i):
                    bank, free = full(L, f"og{'ab'[i]}")
                    dve.wait_ge(sem("og_tanh"), 2 * L + i + 1)
                    y = ys[:, KB + 2 * i:KB + 2 * i + 2, :]
                    dve.scalar_tensor_tensor(y, th[:, :, :], 1.0, two(bank), ADD, MUL).then_inc(free, 1)
                    freed(L, f"og{'ab'[i]}")
                    dve.engine_nop().then_inc(sem("og_done"), 1)
                split(L, "ogb", FIRST)
                out_gate(0)
                split(L, "ogb", LAST)
                freed(L, "ssq")
                step(dve.reciprocal(rqs[:, :], rq16[:, :]))
                dve.reciprocal(rk16[:, :], rk16[:, :]).then_inc(sem("rk_ready"), 1)
                r = slice(NOPE, QK)
                bank, free = full(L, "rk")
                if L == 0:
                    dve.wait_ge(sem("rope_tables"), 1)
                turned = k[r, 0, :]
                dve.tensor_tensor(turned, bank[r, 0:T], cs[r, 1, :], MUL).then_inc(free, 1)
                step(dve.tensor_tensor(krope[r, :], krope[r, :], cs[r, 0, :], MUL))
                freed(L, "rk")
                dve.tensor_tensor(krope[r, :], krope[r, :], turned, ADD).then_inc(sem("krope_turned"), 1)
                bank, free = full(L, "z")
                for d in range(2):
                    ins = dve.tensor_scalar(ztmp[:, d, :], bank[:, d * T:(d + 1) * T], pcol("b_gla_gate", 2 * L + d), None, ADD)
                ins.then_inc(free, 1)
                freed(L, "z")
                dve.scalar_tensor_tensor(ztmp[:, 2:4, :], ztmp[:, 0:2, :], -1.0, ztmp[:, 0:2, :], MUL, MAX).then_inc(sem("z_abs"), 1)
                dve.wait_ge(sem("z_step"), 2 * L + 2)
                step(dve.scalar_tensor_tensor(ztmp[:, 0:2, :], ztmp[:, 0:2, :], 0.0, ztmp[:, 2:4, :], MIN, SUB))
                step(dve.tensor_scalar(ztmp[:, 0:2, :], ztmp[:, 0:2, :], 1.0 / TAU, None, MUL))
                for d in range(2):
                    ins = dve.tensor_tensor_scan(bc[:, d, :], keep[:, :], ztmp[:, d, :], 0.0, MUL, ADD)
                    if d == 0:
                        step(ins)
                ins.then_inc(sem("bc_ready"), 1)
                dve.wait_ge(sem("bc_ready"), L + 1)
                b4 = bc[:, :, :].rearrange("p d (n c) -> p d n c", c=GC)
                for d in range(2):
                    ins = dve.tensor_tensor(ek[:, d, :].rearrange("p (n c) -> p n c", c=GC),
                                            b4[:, d, :, GC - 1:GC].broadcast_to([P, NCH, GC]), b4[:, d], SUB)
                    if d == 0:
                        step(ins)
                ins.then_inc(sem("db_ready"), 1)
                split(L, "ua", FIRST)
                out_gate(1)
                split(L, "ua", LAST)
                dve.wait_ge(sem("krope_read"), 2 * L + 2)
                for i in range(4):
                    bank, free = full(L, f"ssk{i}")
                    x = k[:, 2 * i:2 * i + 2, :]
                    dve.tensor_tensor(x, x, two(bank[0:QK, :]), MUL).then_inc(free, 1)

                split(L, "ub")
                for i in range(4):
                    bank, free = full(L, f"rq{i}")
                    x = q[r, 2 * i:2 * i + 2, :]
                    sin = cs[r, 1, :].unsqueeze(1).broadcast_to([ROPE, 2, T])
                    dve.tensor_tensor(rtmp[r, :, :], two(bank[r, :]), sin, MUL).then_inc(free, 1)
                    freed(L, f"rq{i}")
                    dve.wait_ge(sem("cos_done"), 4 * L + i + 1)
                    dve.tensor_tensor(x, x, rtmp[r, :, :], ADD).then_inc(sem("q_ready"), 1)
                    dve.wait_ge(sem("q_ready"), 4 * L + i + 1)
                split(L, "g0")
                split(L, "g1", FIRST)

                def masked(h):
                    bank, free = full(L, f"s{h}")
                    if h >= 3:
                        _, f, _, n = use(L, f"pt{h - 3}")
                        dve.wait_ge(f, n + 1)
                    dve.tensor_tensor(Pr[:, h % 3, :], bank[:, 0:3 * P], maskc[:, :], ADD).then_inc(free, 1)
                    freed(L, f"s{h}")
                    for a, w in ((0, slice(0, P)), (1, slice(P, 3 * P))):
                        step(dve.tensor_reduce(mx[:, h % 2, a:a + 1], Pr[:, h % 3, w], AX.X, MAX))
                    for a in range(TT):
                        ins = dve.tensor_scalar(nbs[:, h % 2, a:a + 1], mx[:, h % 2, a:a + 1],
                                                rqs[:, a * H + h:a * H + h + 1], -1.0, MUL, MUL)
                        if a == 0:
                            step(ins)
                    ins.then_inc(sem("nb_ready"), 1)

                def scaled(h):
                    dve.wait_ge(sem("exp_done"), H * L + h + 1)
                    step(dve.reciprocal(mx[:, h % 2, :], sums[:, h % 2, :]))
                    for a, w in ((0, slice(0, P)), (1, slice(P, 3 * P))):
                        ins = dve.tensor_scalar(Pr[:, h % 3, w], Pr[:, h % 3, w], mx[:, h % 2, a:a + 1], None, MUL)
                        if a == 0:
                            step(ins)
                    ins.then_inc(sem("p_ready"), 1)
                    dve.wait_ge(sem("p_ready"), H * L + h + 1)

                split(L, "g1", LAST)
                masked(0), masked(1)
                scaled(0), scaled(1)
                split(L, "g2")
                masked(2), masked(3)

                def bcn(d, a):
                    return bc[:, d, a * P:(a + 1) * P].rearrange("p (n c) -> p n c", c=GC)

                def diff(a, d):
                    b = bcn(d, a)
                    if a > 0:
                        _, f, _, n = use(L, "A0")
                        dve.wait_ge(f, n + 1)
                    dve.tensor_tensor(E[:, d], b.unsqueeze(1).broadcast_to([P, GC, NCT, GC]),
                                      b.rearrange("p n c -> p c n").unsqueeze(3).broadcast_to([P, GC, NCT, GC]),
                                      SUB).then_inc(sem("e_diff"), 1)

                def times_q(a, d):
                    dve.wait_ge(sem("e_k"), 4 * L + 2 * a + d + 1)
                    g = gq[:, d, a * P:(a + 1) * P].rearrange("p (n c) -> p n c", c=GC)
                    dve.tensor_tensor(E[:, d], E[:, d],
                                      g.rearrange("p n c -> p c n").unsqueeze(3).broadcast_to([P, GC, NCT, GC]), MUL)\
                       .then_inc(sem("e_ready"), 1)

                def scores_in_chunk(a):
                    bank, free = full(L, f"A{a}")
                    if 2 * L + a:
                        dve.wait_ge(sem("attn_used"), 2 * L + a)
                    A4 = bank[:, 0:GC * GH].rearrange("p (c h) -> p h c", h=GH)
                    for h in range(GH):
                        ins = dve.tensor_tensor(attn[:, h, :].rearrange("p (n c) -> p n c", c=GC),
                                                A4[:, h].unsqueeze(1).broadcast_to([P, NCT, GC]),
                                                maskg[:, :].rearrange("p (n c) -> p n c", c=GC), MUL)
                    ins.then_inc(free, 1)
                    freed(L, f"A{a}")
                    dve.engine_nop().then_inc(sem("attn_ready"), 1)

                def keys_by_chunk(a):
                    bank, free = full(L, f"kd{a}")
                    if a > 0:
                        _, f, _, n = use(L, "U3")
                        dve.wait_ge(f, n + 1)
                    dve.tensor_tensor(kdm[:, :, :], bank[:, 0:T].unsqueeze(1).broadcast_to([P, NCT, T]),
                                      chm[:, :].unsqueeze(2).broadcast_to([P, NCT, T]), MUL).then_inc(free, 1)
                    freed(L, f"kd{a}")
                    dve.engine_nop().then_inc(sem("kdm_ready"), 1)

                def y_low(n):
                    dve.wait_ge(sem("y_hi_ready"), NBR * L + (0, 2, 1).index(n) + 1)
                    hi, lo = y_parts[n]
                    dve.tensor_tensor(lo[:, :, :], ys[:, n * KB:(n + 1) * KB, :], hi[:, :, :].bitcast(F32), SUB)\
                       .then_inc(sem("y_lo_ready"), 1)

                def states(a):
                    for i in range(4):
                        bank, free = full(L, f"U{4 * a + i}")
                        for j in range(2):
                            n = NCT * a + 2 * i + j
                            if n == NCH - 1:
                                continue
                            if n >= NCT:
                                dve.wait_ge(sem("state_used"), (NCH - 2) * L + n - NCT + 1)
                            for d in range(2):
                                up = bank[:, j * T + d * P:j * T + (d + 1) * P]
                                dst = S[:, n % NCT, d, :]
                                if n == 0:
                                    ins = dve.tensor_copy(dst, up)
                                else:
                                    ins = dve.scalar_tensor_tensor(dst, S[:, (n - 1) % NCT, d, :], al[:, d, n:n + 1], up, MUL, ADD)
                                if d == 0:
                                    step(ins)
                            if n % 2 == 1 or n == NCH - 2:
                                ins.then_inc(free, 1)
                                freed(L, f"U{n // 2}")
                            else:
                                ins.then_inc(sem("state_ready"), 1)
                                dve.wait_ge(sem("state_ready"), (NCH // 2 - 1) * L + n // 2 + 1)

                scaled(2), scaled(3)
                split(L, "g3")
                masked(4), masked(5)
                scaled(4), scaled(5)
                split(L, "g4")
                dve.wait_ge(sem("pooled"), NG * (L + 1))
                masked(6), masked(7)
                diff(0, 0)
                scaled(6), scaled(7)
                diff(0, 1)
                split(L, "g5")
                keys_by_chunk(0)
                times_q(0, 0)
                split(L, "g6")
                times_q(0, 1)
                dve.wait_ge(sem("al_ready"), L + 1)
                dve.wait_ge(sem("qdm_ready"), L + 1)
                scores_in_chunk(0)
                diff(1, 0)
                diff(1, 1)
                split(L, "g7")
                states(0)
                times_q(1, 0)
                split(L, "g8")
                times_q(1, 1)
                scores_in_chunk(1)
                split(L, "g9")
                keys_by_chunk(1)
                split(L, "g10")
                y_low(0)
                states(1)
                split(L, "g11")
                y_low(2)
                split(L, "br00")

                def y_b(i):
                    r = rms(L, 2 + i)
                    go = PS[:, 6 + i, :]
                    step(dve.scalar_tensor_tensor(gtmp[:, :, :], two(go), pcol("g_gla_out", L), r[:, :, :], MUL, MUL))
                    y = ys[:, KB + 2 * i:KB + 2 * i + 2, :]
                    dve.scalar_tensor_tensor(y, gtmp[:, :, :], 0.5, y, MUL, MUL).then_inc(sem("yb_ready"), 1)
                    dve.wait_ge(sem("yb_ready"), 2 * L + i + 1)

                def merge(n, m):
                    bank, free = full(L, f"b{n}{m}")
                    g = gates[:, n * KD + 2 * m:n * KD + 2 * m + 2, :]
                    dst = merged[:, 2 * m:2 * m + 2, :]
                    if n == 0:
                        dve.scalar_tensor_tensor(dst, g, 1.0, two(bank), ADD, MUL).then_inc(free, 1)
                        return
                    dve.scalar_tensor_tensor(g, g, 1.0, two(bank), ADD, MUL).then_inc(free, 1)
                    freed(L, f"b{n}{m}")
                    ins = dve.tensor_tensor(dst, dst, g, ADD)
                    if n == 2:
                        step(ins)
                    else:
                        ins.then_inc(sem("merged"), 1)

                def merged_low(m):
                    x = slice(2 * m, 2 * m + 2)
                    dve.wait_ge(sem("mg_hi_ready"), 4 * L + m + 1)
                    dve.tensor_tensor(mg_lo[:, x, :], merged[:, x, :], mg_hi[:, x, :].bitcast(F32), SUB)\
                       .then_inc(sem("mg_lo_ready"), 1)

                split(L, "br01"), merge(0, 0), merge(0, 1)
                split(L, "br20"), merge(0, 2), merge(0, 3)
                split(L, "br21", FIRST), y_b(0), y_b(1), split(L, "br21", LAST)
                split(L, "br10", [0, 1]), y_low(1), split(L, "br10", [2]), merge(2, 0), merge(2, 1)
                split(L, "br10", [3]), merge(2, 2)
                split(L, "br11", [0, 1]), merge(2, 3)
                split(L, "br11", [2, 3]), split(L, "out0", [0])
                merge(1, 0), merge(1, 1), merged_low(0), merged_low(1)
                split(L, "out0", [1, 2])
                merge(1, 2), merge(1, 3), merged_low(2)
                split(L, "out0", [3])
                merged_low(3)
                split(L, "out1")

                def x_plus(m):
                    bank, free = full(L, f"w{m}")
                    x = xT[:, 2 * m:2 * m + 2, :]
                    dve.scalar_tensor_tensor(x, two(bank), 0.5, x, MUL, ADD).then_inc(free, 1)
                x_plus(0)
                split(L, "out2")
                x_plus(1)
                split(L, "out3")
                x_plus(2)
                for j in range(NSPLIT):
                    rest_lo(dve, NDENSE * L, j)
                x_plus(3)
                norm_x(L, "ssf", "g_ffn")

            def dense(u, first=False):
                def gate_up(g):
                    g0, gn = GROUPS[g]
                    if g > 0 or not first:
                        dve.wait_ge(sem("hid_hi_ready"), len(GROUPS) * u + g)
                    for t in range(gn):
                        dve.wait_ge(sem("sil_ready"), FT * u + g0 + t + 1)
                        dve.tensor_tensor(hidf[:, t, :], sil[:, t, :], PS[:, (g0 + t) % DB, T:2 * T], MUL)\
                           .then_inc(sem("hidf_ready"), 1)
                    dve.wait_ge(sem("hid_hi_ready"), len(GROUPS) * u + g + 1)
                    dve.tensor_tensor(hid_lo[:, g0:g0 + gn, :], hidf[:, 0:gn, :], hid_hi[:, g0:g0 + gn, :].bitcast(F32), SUB)\
                       .then_inc(sem("hid_lo_ready"), 1)

                for j in range(HALVES):
                    for _, g in DENSE_AFTER.get(j - NSPLIT, ()):
                        gate_up(g)
                    if not (first and j < NSPLIT):
                        rest_lo(dve, u, j)

            mixer(0)
            dense(0, first=True)
            with dve.Fori(1, NDENSE) as i:
                dense(i)
            wait_used(dve, NDENSE - 1, HALVES - 1)
            for c in range(4):
                x = xT[:, 2 * c:2 * c + 2, :]
                dve.tensor_tensor(x, x, two(PS[:, 4 + c, :]), ADD).then_inc(sem("x_dense"), 1)
            mixer(1)

            dve.wait_ge(sem("logits_full"), 1)
            step(dve.tensor_copy(lg[:, :, :], PS[:, 0, 0:TT * NE].rearrange("p (a e) -> p a e", a=TT)))
            for a in range(TT):
                step(dve.max(rt8[:, a, :], lg[:, a, :]))
                step(dve.max_index(ri8[:, a, :], rt8[:, a, :], lg[:, a, :]))
            step(dve.tensor_copy(rf8[:, :, :], ri8[:, :, :]))
            dve.tensor_tensor(rsm[:, 0:2], rt8[:, :, 1], rt8[:, :, 0], SUB).then_inc(sem("logit_gap"), 1)
            for a in range(TT):
                for j in range(2):
                    step(dve.tensor_scalar(m12[:, a, j, :], iot8[:, :], rf8[:, a, j:j + 1], None, ALU.is_equal))
            dve.tensor_tensor(msel[:, :, :], m12[:, :, 0, :], m12[:, :, 1, :], ADD).then_inc(sem("msel_ready"), 1)
            dve.wait_ge(sem("msel_ready"), 1)
            dve.wait_ge(sem("rank_full"), 1)
            rank = PS[:, 1, 0:TT * NE].rearrange("p (a e) -> p a e", a=TT)
            step(dve.scalar_tensor_tensor(pos[:, :, :], rank, BIG, msel[:, :, :], ADD, MUL))
            step(dve.tensor_scalar(pos[:, :, :], pos[:, :, :], BIG, None, SUB))

            def tokens(r, e, n):
                for c in range(2):
                    b, uses = gather_use(r, e - 1, c)
                    dve.wait_ge(sem("hTe_hi_ready"), 2 * n + c + 1)
                    k = slice(4 * c, 4 * c + 4)
                    dve.tensor_tensor(hTe_lo[:, k, :], PS[:, 4 + b, 0:4 * CAP].rearrange("p (k c) -> p k c", k=4),
                                      hTe_hi[:, k, :].bitcast(F32), SUB).then_inc(sem(f"aux_free{b}"), 1)

            def rows_out(n):
                wait_used(dve, NDENSE + n, HALVES - 1)
                dve.tensor_copy(ye[:, 512:1024], PS[0:CAP, 7, :]).then_inc(sem("ye_dve"), 1)

            def added(uses, part):
                for c in (2 * part, 2 * part + 1):
                    wait_aux_full(dve, c % 2, uses + c // 2)
                    x = xT[:, 2 * c:2 * c + 2, :]
                    dve.tensor_tensor(x, x, two(PS[:, 4 + c % 2, :]), ADD).then_inc(sem(f"aux_free{c % 2}"), 1)

            def expert(r, e, n, first=False, last=False):
                u = NDENSE + n
                for j in range(HALVES):
                    if j == 2 and not first:
                        rows_out(n - 1)
                    for what, g in EXPERT_AFTER.get(j - NSPLIT, ()):
                        g0, gn = GROUPS[g]
                        if what == "gu":
                            dve.wait_ge(sem("sile_ready"), len(GROUPS) * n + g + 1)
                            dve.tensor_tensor(hide[:, g % 2, 0:gn * P], sile[:, g % 2, 0:gn * P],
                                              PS[0:CAP, 2 * (g % 2) + 1, 0:gn * P], MUL).then_inc(sem("hide_ready"), 1)
                        elif what == "tr":
                            b, _ = turn_use(r, e, g, last)
                            dve.wait_ge(sem("hdT_hi_ready"), len(GROUPS) * n + g + 1)
                            dve.tensor_tensor(hdT_lo[:, g0:g0 + gn, :],
                                              PS[:, 4 + b, 0:gn * CAP].rearrange("p (k c) -> p k c", k=gn),
                                              hdT_hi[:, g0:g0 + gn, :].bitcast(F32), SUB).then_inc(sem(f"aux_free{b}"), 1)
                        elif what == "scatter" and not first:
                            added(scatter_use(r, e), g)
                        elif what == "gather" and not last:
                            tokens(r, e + 1, n + 1)
                    if not (j < NSPLIT and isinstance(n, int) and n == 0):
                        rest_lo(dve, u, j)

            def weigh():
                dve.wait_ge(sem("top_exp"), 1)
                step(dve.tensor_scalar(rsm[:, 4:6], rsm[:, 2:4], 1.0, None, ADD))
                step(dve.reciprocal(rsm[:, 4:6], rsm[:, 4:6]))
                step(dve.tensor_tensor(rsm[:, 6:8], rsm[:, 2:4], rsm[:, 4:6], MUL))
                for a in range(TT):
                    step(dve.tensor_scalar(wt[:, a, :], m12[:, a, 1, :], rsm[:, 6 + a:7 + a], None, MUL))
                    step(dve.scalar_tensor_tensor(wt[:, a, :], m12[:, a, 0, :], rsm[:, 4 + a:5 + a], wt[:, a, :], MUL, ADD))
                step(dve.tensor_reduce(rsm[:, 8:9], PS[:, 1, TT * NE:(TT + 1) * NE], AX.X, MAX))
                step(dve.tensor_scalar(rsm[:, 9:10], rsm[:, 8:9], float(CAP), 1.0, ALU.is_gt, ADD))
                for r in range(2, PASSES):
                    step(dve.scalar_tensor_tensor(rsm[:, 9:10], rsm[:, 8:9], float(r * CAP), rsm[:, 9:10], ALU.is_gt, ADD))
                dve.tensor_copy(npi[:, :], rsm[:, 9:10]).then_inc(sem("passes_known"), 1)

            def one_pass(r):
                n = r * NE
                for a in range(TT):
                    dve.tensor_tensor(psel[:, a], slots[:, :].unsqueeze(1).broadcast_to([P, NE, CAP]),
                                      pos[:, a, :].unsqueeze(2).broadcast_to([P, NE, CAP]), ALU.is_equal)\
                       .then_inc(sem("psel_ready"), 1)
                if isinstance(r, int):
                    weigh()
                dve.wait_ge(sem("psel_ready"), 2 * (r + 1))
                for a in range(TT):
                    dve.tensor_tensor(wsel[:, a], psel[:, a], wt[:, a, :].unsqueeze(2).broadcast_to([P, NE, CAP]), MUL)\
                       .then_inc(sem("sel_ready"), 1)
                dve.tensor_scalar(pos[:, :, :], pos[:, :, :], float(CAP), None, SUB).then_inc(sem("pos_step"), 1)
                dve.wait_ge(sem("pos_step"), r + 1)
                tokens(r, 0, n)
                expert(r, 0, n, first=True)
                with dve.Fori(1, NE - 1) as e:
                    expert(r, e, n + e)
                expert(r, NE - 1, n + NE - 1, last=True)
                rows_out(n + NE - 1)
                for part in range(2):
                    added(scatter_use(r, NE), part)

            one_pass(0)
            dve.wait_ge(sem("passes_known"), 1)
            npass = dve.value_load(npi[0:1, 0:1], min_val=1, max_val=PASSES)
            with dve.If(npass > 1):
                with dve.Fori(1, npass) as r:
                    one_pass(r)


class Chain:

    def __init__(self, eng, sem):
        self.eng, self.sem, self.n = eng, sem, 0

    def __call__(self, ins):
        ins.then_inc(self.sem, 1)
        self.n += 1
        self.wait()

    def wait(self):
        self.eng.wait_ge(self.sem, self.n)


_INS = ["x", "positions", "g_mix", "w_in", "g_cq", "w_uq", "g_ckv", "w_ukv", "g_qk_q", "g_qk_k", "w_gla_gate_up",
        "b_gla_gate", "g_gla_out", "w_pool", "pool_scale", "w_branch", "w_out", "g_ffn", "w_ffn_gate", "w_ffn_up",
        "w_ffn_down", "w_router", "w_exp_gate", "w_exp_up", "w_exp_down"]


def kernel(**inputs):
    import numpy as _np
    import concourse.bacc as _bacc
    from concourse import mybir as _mybir
    from concourse.bass_utils import run_bass_kernel_spmd as _run

    nc = _bacc.Bacc("TRN2", target_bir_lowering=False, num_devices=1)
    arrays, aps = {}, {}
    for name in _INS:
        a = _np.ascontiguousarray(inputs[name])
        arrays[f"in_{name}_dram"] = a
        aps[name] = nc.dram_tensor(f"in_{name}_dram", a.shape, _mybir.dt.from_np(a.dtype), kind="ExternalInput").ap()
    out = nc.dram_tensor("out_dram", (1, T, D), _mybir.dt.float32, kind="ExternalOutput").ap()
    hybrid_trunk(nc, aps, out)
    r = _run(nc, [arrays], core_ids=[0])
    return r.results[0]["out_dram"]
```
